# Optimizing a Trainium2 kernel written in Bass

```python
import math
import jax, jax.numpy as jnp
from jax import lax
import numpy as np

D_MODEL = 1024
BATCH = 1
SEQ = 256
DEPTH = 1
DEC_BATCH = 8
DEC_SEQ = 16
PAST_LEN = 128

CHUNK = 64
HEAD_DIM = 64
H_A = 8
H_B = 8
D_A = H_A * 2 * HEAD_DIM
D_B = H_B * HEAD_DIM
BAND_CHUNKS = 8
REL_CLIP = 128
Q_BLOCK = 128
SPLITS = [D_A, 2 * D_A, 3 * D_A, 3 * D_A + D_B, 3 * D_A + 2 * D_B, 3 * D_A + 3 * D_B,
          3 * D_A + 3 * D_B + D_MODEL]
N_IN = 3 * D_A + 3 * D_B + 2 * D_MODEL
N_EXPERTS = 64
TOP_K = 8
N_GROUP = 8
TOPK_GROUP = 4
D_EXPERT = 256
ROUTED_SCALE = 2.5
EXPERT_BLOCK = 256
ALPHA = (2 * DEPTH) ** 0.25
BETA = (8 * DEPTH) ** -0.25
LN_EPS = 1e-5
NEG = -1e30

kernel_name = "streaming_diffattn_chunkband_moe_step"

def layer_norm(x):
    xf = x.astype(jnp.float32)
    mu = jnp.mean(xf, -1, keepdims=True)
    var = jnp.mean(jnp.square(xf - mu), -1, keepdims=True)
    return ((xf - mu) * lax.rsqrt(var + LN_EPS)).astype(x.dtype)

def rms_norm(x, g):
    xf = x.astype(jnp.float32)
    return (xf * lax.rsqrt(jnp.mean(xf * xf, -1, keepdims=True) + LN_EPS)).astype(x.dtype) * g

def modulate(x, shift, scale):
    return layer_norm(x) * (1.0 + scale) + shift

def post_norm(x, y, g, b):
    return layer_norm(ALPHA * x + y) * g + b

def conditioning(c, w_ada, b_ada):
    mod = jax.nn.silu(c) @ w_ada + b_ada
    return [m[:, None, :] for m in jnp.split(mod, 6, axis=-1)]

def alibi_slopes(n):
    return jnp.asarray(2.0 ** (-8.0 * np.arange(1, n + 1) / n), dtype=jnp.float32)

def diff_attention(q, k, v, tq, ts, lam, subln_g, lam_init):
    s = jnp.einsum('bqhjd,bshjd->bhjqs', q, k).astype(jnp.float32) * HEAD_DIM ** -0.5
    dist = jnp.abs(tq[:, None] - ts[None, :]).astype(jnp.float32)
    bias = -alibi_slopes(H_A)[:, None, None] * dist[None]
    mask = (ts[None, :] // CHUNK) <= (tq[:, None] // CHUNK)
    s = jnp.where(mask, s + bias[:, None], NEG)
    p = jax.nn.softmax(s, axis=-1)
    a = p[:, :, 0] - lam * p[:, :, 1]
    o = jnp.einsum('bhqs,bshe->bqhe', a.astype(v.dtype), v)
    o = rms_norm(o, subln_g) * (1.0 - lam_init)
    return o.reshape(o.shape[0], o.shape[1], D_A)

def diff_attention_prompt(q, k, v, lam, subln_g, lam_init):
    B, S = q.shape[:2]
    nqb = S // Q_BLOCK
    qb = q.reshape(B, nqb, Q_BLOCK, H_A, 2, HEAD_DIM).transpose(1, 0, 2, 3, 4, 5)
    ts = jnp.arange(S)

    def one_block(args):
        qi, b = args
        tq = b * Q_BLOCK + jnp.arange(Q_BLOCK)
        return diff_attention(qi, k, v, tq, ts, lam, subln_g, lam_init)

    o = lax.map(one_block, (qb, jnp.arange(nqb)))
    return o.transpose(1, 0, 2, 3).reshape(B, S, D_A)

def rel_bias_lookup(table, rel):
    return jnp.take(table, jnp.clip(rel, -REL_CLIP, REL_CLIP) + REL_CLIP, axis=1)

def band_attention_prompt(q, k, v, rel_table):
    B, S = q.shape[:2]
    nc = S // CHUNK
    nb = BAND_CHUNKS + 1
    pad = ((0, 0), (BAND_CHUNKS, 0), (0, 0), (0, 0), (0, 0))
    qc = q.reshape(B, nc, CHUNK, H_B, HEAD_DIM)
    kc = jnp.pad(k.reshape(B, nc, CHUNK, H_B, HEAD_DIM), pad)
    vc = jnp.pad(v.reshape(B, nc, CHUNK, H_B, HEAD_DIM), pad)
    s = jnp.concatenate([jnp.einsum('bncha,bnmha->bnhcm', qc, kc[:, j:j + nc]) for j in range(nb)],
                        axis=-1).astype(jnp.float32) * HEAD_DIM ** -0.5
    c = np.arange(CHUNK)
    rel = ((BAND_CHUNKS - np.arange(nb))[:, None, None] * CHUNK + c[None, :, None] - c[None, None, :])
    rel = rel.transpose(1, 0, 2).reshape(CHUNK, nb * CHUNK)
    bias = rel_bias_lookup(rel_table, jnp.asarray(rel, dtype=jnp.int32)).astype(jnp.float32)
    valid = (jnp.arange(nc)[:, None] - BAND_CHUNKS + jnp.arange(nb)[None, :]) >= 0
    valid = jnp.repeat(valid, CHUNK, axis=1)
    s = jnp.where(valid[:, None, None, :], s + bias, NEG)
    p = jax.nn.softmax(s, axis=-1).astype(v.dtype).reshape(B, nc, H_B, CHUNK, nb, CHUNK)
    o = jnp.einsum('bnhcm,bnmha->bncha', p[..., 0, :], vc[:, 0:nc])
    for j in range(1, nb):
        o = o + jnp.einsum('bnhcm,bnmha->bncha', p[..., j, :], vc[:, j:j + nc])
    return o.reshape(B, S, D_B)

def band_attention_sample(q, k, v, tq, ts, rel_table):
    s = jnp.einsum('bqha,bsha->bhqs', q, k).astype(jnp.float32) * HEAD_DIM ** -0.5
    bias = rel_bias_lookup(rel_table, tq[:, None] - ts[None, :]).astype(jnp.float32)
    cq, cs = tq // CHUNK, ts // CHUNK
    mask = (cs[None, :] <= cq[:, None]) & (cs[None, :] >= cq[:, None] - BAND_CHUNKS)
    s = jnp.where(mask, s + bias, NEG)
    p = jax.nn.softmax(s, axis=-1)
    o = jnp.einsum('bhqs,bsha->bqha', p.astype(v.dtype), v)
    return o.reshape(o.shape[0], o.shape[1], D_B)

def token_sublayer(x, shift, scale, gate, w_in, b_in, p_a, p_b, w_out, ln_g, ln_b, attend):
    u = modulate(x, shift, scale)
    B, S, _ = u.shape
    z = u @ w_in + b_in
    qa, ka, va, qb, kb, vb, ga, gb = jnp.split(z, SPLITS, axis=-1)
    qa = qa.reshape(B, S, H_A, 2, HEAD_DIM)
    ka = ka.reshape(B, S, H_A, 2, HEAD_DIM)
    va = va.reshape(B, S, H_A, 2 * HEAD_DIM)
    qb = qb.reshape(B, S, H_B, HEAD_DIM)
    kb = kb.reshape(B, S, H_B, HEAD_DIM)
    vb = vb.reshape(B, S, H_B, HEAD_DIM)
    oa, ob = attend(qa, ka, va, qb, kb, vb)
    m = jax.nn.sigmoid(ga) * (oa @ p_a) + jax.nn.sigmoid(gb) * (ob @ p_b)
    return post_norm(x, gate * (m @ w_out), ln_g, ln_b), (ka, va, kb, vb)

def route(h, w_router, e_bias):
    T = h.shape[0]
    scores = jax.nn.sigmoid((h @ w_router).astype(jnp.float32))
    biased = scores + e_bias.astype(jnp.float32)
    grp = jnp.sum(lax.top_k(biased.reshape(T, N_GROUP, N_EXPERTS // N_GROUP), 2)[0], -1)
    _, gidx = lax.top_k(grp, TOPK_GROUP)
    gmask = jnp.any(gidx[:, :, None] == jnp.arange(N_GROUP)[None, None, :], axis=1)
    emask = jnp.repeat(gmask, N_EXPERTS // N_GROUP, axis=1)
    _, idx = lax.top_k(jnp.where(emask, biased, -jnp.inf), TOP_K)
    w = jnp.take_along_axis(scores, idx, axis=1)
    w = w / jnp.sum(w, -1, keepdims=True) * ROUTED_SCALE
    return idx, w

def routed_experts(h, idx, wts, w1, w3, w2):
    T, D = h.shape
    A = T * TOP_K
    nb = -(-A // EXPERT_BLOCK) + N_EXPERTS
    flat_e = idx.reshape(A)
    flat_w = wts.reshape(A)
    order = jnp.argsort(flat_e)
    e_sorted = flat_e[order]
    counts = jnp.bincount(flat_e, length=N_EXPERTS)
    padded = (counts + EXPERT_BLOCK - 1) // EXPERT_BLOCK * EXPERT_BLOCK
    pad_end = jnp.cumsum(padded)
    pad_start = pad_end - padded
    start = jnp.cumsum(counts) - counts
    dest = pad_start[e_sorted] + jnp.arange(A) - start[e_sorted]
    n_slots = nb * EXPERT_BLOCK
    slot_tok = jnp.full((n_slots,), T, jnp.int32).at[dest].set((order // TOP_K).astype(jnp.int32))
    slot_w = jnp.zeros((n_slots,), h.dtype).at[dest].set(flat_w[order].astype(h.dtype))
    block_e = jnp.minimum(jnp.searchsorted(pad_end, jnp.arange(nb) * EXPERT_BLOCK, side='right'),
                          N_EXPERTS - 1)
    h_pad = jnp.concatenate([h, jnp.zeros((1, D), h.dtype)], axis=0)

    def expert_group(args):
        tok, wt, e = args
        xb = h_pad[tok]
        hid = jax.nn.silu(xb @ w1[e]) * (xb @ w3[e])
        return (hid @ w2[e]) * wt[:, None]

    yb = lax.map(expert_group, (slot_tok.reshape(nb, EXPERT_BLOCK),
                                slot_w.reshape(nb, EXPERT_BLOCK), block_e))
    out = jnp.zeros((T + 1, D), h.dtype).at[slot_tok].add(yb.reshape(n_slots, D))
    return out[:T]

def channel_sublayer(x, shift, scale, gate, w_router, e_bias, w1, w3, w2, ws1, ws3, ws2, ln_g, ln_b):
    u = modulate(x, shift, scale)
    B, S, D = u.shape
    h = u.reshape(B * S, D)
    idx, wts = route(h, w_router, e_bias)
    y = (jax.nn.silu(h @ ws1) * (h @ ws3)) @ ws2 + routed_experts(h, idx, wts, w1, w3, w2)
    return post_norm(x, gate * y.reshape(B, S, D), ln_g, ln_b)

def setup_inputs(seed: int = 0) -> dict:
    key = jax.random.key(seed)
    ks = jax.random.split(key, 40)
    f32 = jnp.float32

    def nrm(k, shape, scale):
        return jax.random.normal(k, shape, f32) * scale

    lb = min(BAND_CHUNKS * CHUNK, PAST_LEN)
    col_scale = jnp.concatenate([jnp.ones((2 * D_A,), f32), jnp.full((D_A,), BETA, f32),
                                 jnp.ones((2 * D_B,), f32), jnp.full((D_B,), BETA, f32),
                                 jnp.ones((2 * D_MODEL,), f32)])
    L, D, E, F = DEPTH, D_MODEL, N_EXPERTS, D_EXPERT
    return {
        "x_prompt": nrm(ks[0], (BATCH, SEQ, D), 1.0),
        "x_sample": nrm(ks[1], (DEC_BATCH, DEC_SEQ, D), 1.0),
        "cache_k_diff": nrm(ks[2], (L, DEC_BATCH, PAST_LEN, H_A, 2, HEAD_DIM), 1.0),
        "cache_v_diff": nrm(ks[3], (L, DEC_BATCH, PAST_LEN, H_A, 2 * HEAD_DIM), BETA),
        "cache_k_band": nrm(ks[4], (L, DEC_BATCH, lb, H_B, HEAD_DIM), 1.0),
        "cache_v_band": nrm(ks[5], (L, DEC_BATCH, lb, H_B, HEAD_DIM), BETA),
        "c_prompt": nrm(ks[6], (BATCH, D), 1.0),
        "c_sample": nrm(ks[7], (DEC_BATCH, D), 1.0),
        "w_ada": nrm(ks[8], (L, D, 6 * D), D ** -0.5),
        "b_ada": nrm(ks[9], (L, 6 * D), 0.02),
        "w_in": nrm(ks[10], (L, D, N_IN), D ** -0.5) * col_scale,
        "b_in": nrm(ks[11], (L, N_IN), 0.02),
        "lambda_q1": nrm(ks[12], (L, HEAD_DIM), 0.1),
        "lambda_k1": nrm(ks[13], (L, HEAD_DIM), 0.1),
        "lambda_q2": nrm(ks[14], (L, HEAD_DIM), 0.1),
        "lambda_k2": nrm(ks[15], (L, HEAD_DIM), 0.1),
        "subln_g": 1.0 + nrm(ks[16], (L, 2 * HEAD_DIM), 0.02),
        "rel_bias": nrm(ks[17], (L, H_B, 2 * REL_CLIP + 1), 0.1),
        "p_a": nrm(ks[18], (L, D_A, D), BETA * D_A ** -0.5),
        "p_b": nrm(ks[19], (L, D_B, D), BETA * D_B ** -0.5),
        "w_out": nrm(ks[20], (L, D, D), BETA * D ** -0.5),
        "ln1_g": 1.0 + nrm(ks[21], (L, D), 0.02),
        "ln1_b": nrm(ks[22], (L, D), 0.02),
        "w_router": nrm(ks[23], (L, D, E), D ** -0.5),
        "e_bias": nrm(ks[24], (L, E), 0.01),
        "w1": nrm(ks[25], (L, E, D, F), BETA * D ** -0.5),
        "w3": nrm(ks[26], (L, E, D, F), BETA * D ** -0.5),
        "w2": nrm(ks[27], (L, E, F, D), BETA * F ** -0.5),
        "ws1": nrm(ks[28], (L, D, F), BETA * D ** -0.5),
        "ws3": nrm(ks[29], (L, D, F), BETA * D ** -0.5),
        "ws2": nrm(ks[30], (L, F, D), BETA * F ** -0.5),
        "ln2_g": 1.0 + nrm(ks[31], (L, D), 0.02),
        "ln2_b": nrm(ks[32], (L, D), 0.02),
    }

def reference(x_prompt, x_sample, cache_k_diff, cache_v_diff, cache_k_band, cache_v_band,
              c_prompt, c_sample, w_ada, b_ada, w_in, b_in, lambda_q1, lambda_k1, lambda_q2,
              lambda_k2, subln_g, rel_bias, p_a, p_b, w_out, ln1_g, ln1_b, w_router, e_bias,
              w1, w3, w2, ws1, ws3, ws2, ln2_g, ln2_b):
    f32 = jnp.float32
    yp, ys = x_prompt, x_sample
    kdp, vdp, kbp, vbp, kds, vds, kbs, vbs = [], [], [], [], [], [], [], []
    for l in range(DEPTH):
        lam_init = 0.8 - 0.6 * math.exp(-0.3 * l)
        lam = (jnp.exp(jnp.sum(lambda_q1[l].astype(f32) * lambda_k1[l].astype(f32)))
               - jnp.exp(jnp.sum(lambda_q2[l].astype(f32) * lambda_k2[l].astype(f32))) + lam_init)

        def attend_prompt(qa, ka, va, qb, kb, vb):
            return (diff_attention_prompt(qa, ka, va, lam, subln_g[l], lam_init),
                    band_attention_prompt(qb, kb, vb, rel_bias[l]))

        sh1, sc1, g1, sh2, sc2, g2 = conditioning(c_prompt, w_ada[l], b_ada[l])
        yp, (ka, va, kb, vb) = token_sublayer(yp, sh1, sc1, g1, w_in[l], b_in[l], p_a[l], p_b[l],
                                              w_out[l], ln1_g[l], ln1_b[l], attend_prompt)
        yp = channel_sublayer(yp, sh2, sc2, g2, w_router[l], e_bias[l], w1[l], w3[l], w2[l],
                              ws1[l], ws3[l], ws2[l], ln2_g[l], ln2_b[l])
        lbp = min(BAND_CHUNKS * CHUNK, ka.shape[1])
        kdp.append(ka)
        vdp.append(va)
        kbp.append(kb[:, -lbp:])
        vbp.append(vb[:, -lbp:])

        def attend_sample(qa, ka, va, qb, kb, vb):
            past = cache_k_diff.shape[2]
            n = qa.shape[1]
            tq = past + jnp.arange(n)
            oa = diff_attention(qa, jnp.concatenate([cache_k_diff[l], ka], axis=1),
                                jnp.concatenate([cache_v_diff[l], va], axis=1),
                                tq, jnp.arange(past + n), lam, subln_g[l], lam_init)
            lb = cache_k_band.shape[2]
            ob = band_attention_sample(qb, jnp.concatenate([cache_k_band[l], kb], axis=1),
                                       jnp.concatenate([cache_v_band[l], vb], axis=1),
                                       tq, jnp.arange(past - lb, past + n), rel_bias[l])
            return oa, ob

        sh1, sc1, g1, sh2, sc2, g2 = conditioning(c_sample, w_ada[l], b_ada[l])
        ys, (ka, va, kb, vb) = token_sublayer(ys, sh1, sc1, g1, w_in[l], b_in[l], p_a[l], p_b[l],
                                              w_out[l], ln1_g[l], ln1_b[l], attend_sample)
        ys = channel_sublayer(ys, sh2, sc2, g2, w_router[l], e_bias[l], w1[l], w3[l], w2[l],
                              ws1[l], ws3[l], ws2[l], ln2_g[l], ln2_b[l])
        kds.append(ka)
        vds.append(va)
        kbs.append(kb)
        vbs.append(vb)

    return (yp, ys, jnp.stack(kdp), jnp.stack(vdp), jnp.stack(kbp), jnp.stack(vbp),
            jnp.stack(kds), jnp.stack(vds), jnp.stack(kbs), jnp.stack(vbs))


_drawn_inputs = setup_inputs


def setup_inputs(seed=0):
    import zlib

    import numpy as np

    out = dict(_drawn_inputs(seed))
    spreads = {}
    factors = {'cache_k_band': 4.294,
     'cache_v_band': 3.77,
     'lambda_q1': 6.746,
     'lambda_k1': 3.306,
     'lambda_q2': 53.626,
     'lambda_k2': 4.952,
     'subln_g': 30.349,
     'rel_bias': 8.0,
     'ln2_g': 8.342,
     'ln2_b': 7.94}
    for name, (base, spread) in spreads.items():
        noise = np.random.default_rng([zlib.crc32(name.encode()), seed]).standard_normal(out[name].shape)
        drawn = base * np.exp(spread * noise) if base else spread * noise
        out[name] = __import__('jax').numpy.asarray(drawn.astype(out[name].dtype))
    for name, factor in factors.items():
        out[name] = (out[name] * factor).astype(out[name].dtype)
    return out
```

```python
from contextlib import ExitStack

import concourse.bass as bass
import concourse.mybir as mybir
import numpy as np

ALU = mybir.AluOpType
ACT = mybir.ActivationFunctionType
AX = mybir.AxisListType
F32 = mybir.dt.float32
F16 = mybir.dt.float16
I32 = mybir.dt.int32
U32 = mybir.dt.uint32

P = 128
D = 1024
KD = D // P
SEQ, NSEQ, NF, PAST = 256, 8, 16, 128
NT = 3
TOK = NT * P
CHUNK = 64
HD = 64
HA = HB = 8
DA, DB = HA * 2 * HD, HB * HD
NU = 12
CLIP = 128
N_IN = 3 * DA + 3 * DB + 2 * D
CW = 512
E, TOPK, NG, TOPG, F = 64, 8, 8, 4, 256
SLOTS = 64
XB = (TOK * TOPK - 1) // SLOTS
NBLK = E + XB
ROUTED_SCALE = 2.5
ALPHA = 2.0 ** 0.25
LAM_INIT = 0.2
EPS = 1e-5
SM = HD ** -0.5
WB = 4
QC = {0: 0, 1: 4, 6: 8}
KC = {2: 0, 3: 512, 7: 1024}
VC = {4: 0, 5: 512, 8: 1024}


def layer_norm(dve, link, ln, out, x):
    stats, mv, rstd = ln.stats, ln.mv, ln.rstd
    for i in range(2):
        link(dve.bn_stats(stats[:, 6 * i:6 * i + 6], x[:, CW * i:CW * i + CW]))
    link(dve.bn_aggr(mv[:, :], stats[:, :]))
    dve.tensor_scalar(mv[:, 1:2], mv[:, 1:2], EPS, None, ALU.add).then_inc(ln.var_done, 1)
    ln.count += 1
    dve.wait_ge(ln.rstd_done, ln.count)
    link(dve.tensor_scalar(out, x, mv[:, 0:1], rstd[:, 0:1], ALU.subtract, ALU.mult))


def layer_norm_state(t, sb, sem, tag):
    ln = Shared()
    ln.stats, ln.mv, ln.rstd = sb("stats" + tag, [P, 12]), sb("mv" + tag, [P, 2]), sb("rstd" + tag, [P, 1])
    ln.power, ln.count = t.power, 0
    ln.var_done, ln.rstd_done = sem("var_done" + tag), sem("rstd_done" + tag)
    return ln


def rsqrts(pool, ln, *norms):
    for n in norms:
        pool.wait_ge(ln.var_done, n + 1)
        pool.tensor_tensor(ln.rstd[:, :], ln.mv[:, 1:2], ln.power[:, 0:1], ALU.pow).then_inc(ln.rstd_done, 1)


def make_link(eng, sem):
    count = [0]

    def link(ins):
        count[0] += 1
        ins.then_inc(sem, 1)
        eng.wait_ge(sem, count[0])
    return link


def conditioning(nc, t):
    PS = t.PS
    with ExitStack() as ctx:
        sb = lambda n, s, d=F32: ctx.enter_context(nc.sbuf_tensor(n, s, d))
        sem = t.phase_semaphore
        NC = 1 + NSEQ
        NA = 6 * D // CW
        c_rows = sb("c_rows", [NC, D])
        c_silu = sb("c_silu", [NC, D])
        cT = sb("cT", [P, KD, 32])
        b_q = sb("b_q", [P, NA, P])
        mod_q = sb("mod_q", [P, NA, P])
        shift = sb("shift", [P, 2, D])
        scale = sb("scale", [P, 2, D])
        u = sb("u", [P, NT, D])
        ln = layer_norm_state(t, sb, sem, "_1")
        c_in, x_in, bada_in = sem("c_in"), sem("x_in"), sem("bada_in")
        ada_in = [sem(f"ada_in{i}") for i in range(2)]
        silu_done, ct_mm, ct_zero, ct_done = sem("silu_done"), sem("ct_mm"), sem("ct_zero"), sem("ct_done")
        ada_mm, ada_ev, mod_out, mod_back = sem("ada_mm"), sem("ada_ev"), sem("mod_out"), sem("mod_back")
        u_done, ut_mm, ut_ev = sem("u_done"), sem("ut_mm"), sem("ut_ev")
        dve_step = sem("cond_dve")
        block = ctx.enter_context(nc.Block())

        @block.sync
        def _(sp):
            sp.dma_start(c_rows[0:1, :], t.c_prompt).then_inc(c_in, 16)
            sp.dma_start(c_rows[1:NC, :], t.c_sample).then_inc(c_in, 16)
            for j in range(4):
                src = t.b_ada.rearrange("l (c j n) -> l j c n", j=4, n=P)[:, j]
                sp.dma_start(b_q[32 * j:32 * j + 32], src.to_broadcast([32, NA, P])).then_inc(bada_in, 16)
            for i in range(NA):
                if i >= 2:
                    sp.wait_ge(ada_mm, i - 1)
                sp.dma_start(t.W[:, i % 2], t.w_ada[0].rearrange("(k p) n -> p k n", p=P)[:, :, CW * i:CW * i + CW]).then_inc(ada_in[i % 2], 16)
                if i == 1:
                    for n in range(2):
                        sp.dma_start(t.X[:, n], t.x_prompt[0, P * n:P * n + P]).then_inc(x_in, 16)
                    sp.dma_start(t.X[:, 2], t.x_sample.rearrange("b s d -> (b s) d")).then_inc(x_in, 16)
            sp.wait_ge(ada_ev, NA)
            for j in range(4):
                dst = t.mod.rearrange("r (c j n) -> r j c n", j=4, n=P)[:, j]
                sp.dma_start(dst, mod_q[32 * j:32 * j + NC]).then_inc(mod_out, 16)
            sp.wait_ge(mod_out, 64)
            t.load_mod(sp, shift, 0, mod_back)
            t.load_mod(sp, scale, 1, mod_back)

        @block.scalar
        def _(act):
            act.wait_ge(c_in, 32)
            act.activation(c_silu[:, :], c_rows[:, :], ACT.Silu).then_inc(silu_done, 1)
            for n in range(6):
                act.wait_ge(ut_mm, n + 1)
                tile, half = n // 2, n % 2
                act.copy(t.uT[:, 4 * half:4 * half + 4, P * tile:P * tile + P],
                         PS[:, 2 + n % 2].rearrange("p (k q) -> p k q", k=4)).then_inc(ut_ev, 1)

        @block.vector
        def _(dve):
            link = make_link(dve, dve_step)
            dve.memset(cT[:, :, :], 0.0).then_inc(ct_zero, 1)
            dve.wait_ge(ct_zero, 1)
            dve.wait_ge(ct_mm, 1)
            dve.tensor_copy(cT[:, :, 0:NC], PS[:, 0, 0:KD * NC].rearrange("p (k r) -> p k r", k=KD)).then_inc(ct_done, 1)
            dve.wait_ge(x_in, 48)
            for n in range(NT):
                layer_norm(dve, link, ln, u[:, n], t.X[:, n])
            dve.wait_ge(bada_in, 64)
            for i in range(NA):
                dve.wait_ge(ada_mm, i + 1)
                dve.tensor_tensor(mod_q[:, i], PS[:, i % 2, 0:P], b_q[:, i], ALU.add).then_inc(ada_ev, 1)
            dve.wait_ge(mod_back, 64)
            for n in range(NT):
                g = n // 2
                link(dve.scalar_tensor_tensor(u[:, n], scale[:, g], 1.0, u[:, n], ALU.add, ALU.mult))
                dve.tensor_tensor(u[:, n], u[:, n], shift[:, g], ALU.add).then_inc(u_done, 1)

        @block.gpsimd
        def _(pool):
            t.build_identity(pool)
            rsqrts(pool, ln, *range(NT))

        @block.tensor
        def _(pe):
            pe.wait_ge(t.ident_done, 2)
            pe.wait_ge(silu_done, 1)
            for k in range(KD):
                mm = pe.transpose(PS[:, 0, NC * k:NC * k + NC], c_silu[:, P * k:P * k + P], t.ident[0:NC, 0:NC])
            mm.then_inc(ct_mm, 1)
            pe.wait_ge(ct_done, 1)
            for i in range(NA):
                pe.wait_ge(ada_in[i % 2], 16 * (i // 2 + 1))
                if i >= 2:
                    pe.wait_ge(ada_ev, i - 1)
                for k in range(KD):
                    for j in range(4):
                        mm = pe.matmul(PS[32 * j:32 * j + 32, i % 2, 0:P], cT[:, k], t.W[:, i % 2, k, P * j:P * j + P],
                                       start=k == 0, stop=k == KD - 1)
                mm.then_inc(ada_mm, 1)
            for n in range(6):
                tile, half = n // 2, n % 2
                pe.wait_ge(u_done, tile + 1)
                if n >= 2:
                    pe.wait_ge(ut_ev, n - 1)
                for k in range(4):
                    mm = pe.transpose(PS[:, 2 + n % 2, P * k:P * k + P], u[:, tile, P * (4 * half + k):P * (4 * half + k) + P], t.ident[:, :])
                mm.then_inc(ut_mm, 1)


def projection_in(nc, t):
    PS = t.PS
    with ExitStack() as ctx:
        sb = lambda n, s, d=F32: ctx.enter_context(nc.sbuf_tensor(n, s, d))
        sem = t.phase_semaphore
        keys = sb("keys", [P, NT, DA + DB])
        b_col = sb("b_col", [P, NU])
        b_row = sb("b_row", [P, 9, CW])
        win_in = [sem(f"win_in{i}") for i in range(2)]
        bin_in, rows_zero = sem("bin_in"), sem("rows_zero")
        z_mm, z_ev_act, z_ev_dve = sem("z_mm"), sem("z_ev_act"), sem("z_ev_dve")
        kt_mm, kt_ev, kv_out = sem("kt_mm"), sem("kt_ev"), sem("kv_out")
        NCH = 9
        jobs = [(c, i) for c in range(NCH) for i in range(4 if c in QC else NT)]
        act_jobs = [n for n, (c, _) in enumerate(jobs) if c in QC]
        dve_jobs = [n for n, (c, _) in enumerate(jobs) if c not in QC]
        block = ctx.enter_context(nc.Block())

        @block.sync
        def _(sp):
            with nc.allow_non_contiguous_dma(reason="128 x 12 bias values, one column each"):
                for u0, c0, n in ((0, 0, 8), (8, 3 * DA, 4)):
                    sp.dma_start(b_col[:, u0:u0 + n], t.b_in[0, c0:c0 + P * n].rearrange("(u p) -> p u", p=P)).then_inc(bin_in, 16)
            sp.dma_start(b_row[:, :, :], t.b_in[:, 0:NCH * CW].rearrange("l (c n) -> l c n", n=CW).to_broadcast([P, NCH, CW])).then_inc(bin_in, 16)
            for c in range(NCH):
                if c >= 2:
                    sp.wait_ge(z_mm, 1 + max(n for n, j in enumerate(jobs) if j[0] == c - 2))
                sp.dma_start(t.W[:, c % 2], t.w_in[0].rearrange("(k p) n -> p k n", p=P)[:, :, CW * c:CW * c + CW]).then_inc(win_in[c % 2], 16)
            sp.wait_ge(t.zeros_done, 1)
            for n in range(E * SLOTS, NBLK * SLOTS, P):
                r = min(P, NBLK * SLOTS - n)
                sp.dma_start(t.y_dram[n:n + r], t.zeros[0:r, :]).then_inc(rows_zero, 16)
            stores = 0
            for width, c0, outs, src in ((DA, 0, (t.kdp, t.kds), keys), (DA, 0, (t.vdp, t.vds), t.V),
                                         (DB, DA, (t.kbp, t.kbs), keys), (DB, DA, (t.vbp, t.vbs), t.V)):
                last = {(0, id(keys)): 3, (0, id(t.V)): 5, (DA, id(keys)): 7, (DA, id(t.V)): 8}[(c0, id(src))]
                sp.wait_ge(z_ev_dve, 1 + max(i for i, n in enumerate(dve_jobs) if jobs[n][0] == last))
                for n in range(2):
                    sp.dma_start(outs[0][P * n:P * n + P], src[:, n, c0:c0 + width]).then_inc(kv_out, 16)
                sp.dma_start(outs[1], src[:, 2, c0:c0 + width]).then_inc(kv_out, 16)
                stores += 3
            sp.wait_ge(kv_out, 16 * stores)
            sp.wait_ge(rows_zero, 16 * -(-(XB * SLOTS) // P))

        @block.tensor
        def _(pe):
            def transpose_keys(c):
                for i in range(NT):
                    n = 3 * [2, 3, 7].index(c) + i
                    pe.wait_ge(z_ev_dve, 1 + dve_jobs.index(jobs.index((c, i))))
                    if n >= 2:
                        pe.wait_ge(kt_ev, n - 1)
                    for m in range(4):
                        mm = pe.transpose(PS[:, 6 + n % 2, P * m:P * m + P], keys[:, i, KC[c] + P * m:KC[c] + P * m + P], t.ident[:, :])
                    mm.then_inc(kt_mm, 1)

            for n, (c, i) in enumerate(jobs):
                if i == 0:
                    pe.wait_ge(win_in[c % 2], 16 * (c // 2 + 1))
                if n >= 6:
                    o = n - 6
                    if o in act_jobs:
                        pe.wait_ge(z_ev_act, act_jobs.index(o) + 1)
                    else:
                        pe.wait_ge(z_ev_dve, dve_jobs.index(o) + 1)
                for k in range(KD):
                    if c in QC:
                        mm = pe.matmul(PS[:, n % 6, 0:TOK], t.W[:, c % 2, k, P * i:P * i + P], t.uT[:, k], start=k == 0, stop=k == KD - 1)
                    else:
                        mm = pe.matmul(PS[:, n % 6], t.uT[:, k, P * i:P * i + P], t.W[:, c % 2, k], start=k == 0, stop=k == KD - 1)
                mm.then_inc(z_mm, 1)
                if i == (3 if c in QC else NT - 1):
                    if c - 1 in KC:
                        transpose_keys(c - 1)

        @block.scalar
        def _(act):
            act.wait_ge(bin_in, 48)
            k_done = [0]

            def turn_keys(c):
                for i in range(NT):
                    k_done[0] += 1
                    act.wait_ge(kt_mm, k_done[0])
                    u0 = KC[c] // P
                    act.copy(t.kT[:, u0:u0 + 4, P * i:P * i + P],
                             PS[:, 6 + (k_done[0] - 1) % 2].rearrange("p (u q) -> p u q", u=4)).then_inc(kt_ev, 1)

            for n, (c, i) in enumerate(jobs):
                if c in QC:
                    act.wait_ge(z_mm, n + 1)
                    u = QC[c] + i
                    act.activation(t.qT[:, u], PS[:, n % 6, 0:TOK], ACT.Identity, bias=b_col[:, u:u + 1]).then_inc(z_ev_act, 1)
                if i == (3 if c in QC else NT - 1) and c - 1 in KC:
                    turn_keys(c - 1)

        @block.vector
        def _(dve):
            dve.wait_ge(bin_in, 48)
            for n, (c, i) in enumerate(jobs):
                if c in QC:
                    continue
                dve.wait_ge(z_mm, n + 1)
                dst = keys[:, i, KC[c]:KC[c] + CW] if c in KC else t.V[:, i, VC[c]:VC[c] + CW]
                dve.tensor_tensor(dst, PS[:, n % 6], b_row[:, c], ALU.add).then_inc(z_ev_dve, 1)


def attention_constants(nc, t):
    with ExitStack() as ctx:
        sb = lambda n, s, d=F32: ctx.enter_context(nc.sbuf_tensor(n, s, d))
        sem = t.phase_semaphore
        NR = 3 * CLIP
        table = sb("table", [HB, 2 * CLIP + 1])
        rev = sb("rev", [HB, NR])
        di = sb("di", [P, 256], I32)
        df = sb("df", [P, 256])
        xi = sb("xi", [P, PAST + NF], I32)
        xf = sb("xf", [P, PAST + NF])
        xn = sb("xn", [P, PAST + NF])
        qi = sb("qi", [P, 1], I32)
        qf = sb("qf", [P, 1])
        slope = sb("slope", [P, 2])
        lamv = sb("lamv", [P, 4, HD])
        lamp = sb("lamp", [P, 2, HD])
        lamd = sb("lamd", [P, 2])
        lame = sb("lame", [P, 2])
        fall_p, fall_s = sb("fall_p", [P, HB, 256]), sb("fall_s", [P, PAST + NF])
        flip, flip16 = sb("flip", [P, P]), sb("flip16", [P, P])
        flip_done, flip_mm = sem("flip_done"), sem("flip_mm")
        PS = t.PS
        table_in, rev_done, rev_out, band_in = sem("table_in"), sem("rev_done"), sem("rev_out"), sem("band_in")
        lam_in, g_in, iota_done, lamd_done, lame_done = sem("lam_in"), sem("g_in"), sem("iota_done"), sem("lamd_done"), sem("lame_done")
        dve_step = sem("const_dve")
        block = ctx.enter_context(nc.Block())

        @block.sync
        def _(sp):
            sp.dma_start(table[:, :], t.rel_bias[0]).then_inc(table_in, 16)
            for i, v in enumerate((t.lq1, t.lk1, t.lq2, t.lk2)):
                sp.dma_start(lamv[:, i], v.to_broadcast([P, HD])).then_inc(lam_in, 16)
            sp.dma_start(t.sub_g[:, :], t.subln_g.to_broadcast([P, 2 * HD])).then_inc(g_in, 16)
            sp.wait_ge(rev_done, 1)
            sp.dma_start(t.rev_dram, rev[:, :]).then_inc(rev_out, 16)
            sp.wait_ge(rev_out, 16)
            h = t.rev_dram.tensor
            sp.dma_start(fall_p[:, :, :], bass.AP(h, 0, [[1, P], [NR, HB], [1, 256]])).then_inc(band_in, 16)
            sp.dma_start(fall_s[:, :], bass.AP(h, P - NF, [[NR, HB], [1, NF], [1, PAST + NF]])).then_inc(band_in, 16)

        @block.gpsimd
        def _(pool):
            pool.iota(di[:, :], pattern=[[-1, 256]], base=PAST, channel_multiplier=1).then_inc(iota_done, 1)
            pool.iota(xi[:, :], pattern=[[-1, PAST + NF]], base=PAST, channel_multiplier=0).then_inc(iota_done, 1)
            pool.iota(qi[:, :], pattern=[[0, 1]], base=0, channel_multiplier=1).then_inc(iota_done, 1)

        @block.tensor
        def _(pe):
            pe.wait_ge(flip_done, 1)
            pe.wait_ge(band_in, 32)
            for n in range(4):
                pe.matmul(PS[:, n], flip[:, :], fall_p[:, 2 * n:2 * n + 2].rearrange("p h x -> p (h x)"), start=True, stop=True)
            pe.matmul(PS[:, 4, 0:PAST + NF], flip16[:, :], fall_s[:, :], start=True, stop=True).then_inc(flip_mm, 1)

        @block.scalar
        def _(act):
            act.wait_ge(lamd_done, 1)
            act.activation(lame[:, :], lamd[:, :], ACT.Exp).then_inc(lame_done, 1)

        @block.vector
        def _(dve):
            link = make_link(dve, dve_step)
            dve.wait_ge(lam_in, 64)
            for i in range(2):
                link(dve.tensor_tensor(lamp[:, i], lamv[:, 2 * i], lamv[:, 2 * i + 1], ALU.mult))
            dve.tensor_reduce(lamd[:, :], lamp[:, :, :], AX.X, ALU.add).then_inc(lamd_done, 1)
            dve.wait_ge(table_in, 16)
            dve.tensor_copy(rev[:, 0:P - 1], table[:, 2 * CLIP:2 * CLIP + 1].to_broadcast([HB, P - 1]))
            dve.tensor_copy(rev[:, P - 1:NR], table[:, ::-1]).then_inc(rev_done, 1)
            dve.tensor_copy(flip[:, :], t.ident[:, ::-1])
            dve.tensor_copy(flip16[:, :].rearrange("p (h q) -> p h q", q=NF),
                            t.ident[:, :].rearrange("p (h q) -> p h q", q=NF)[:, :, ::-1]).then_inc(flip_done, 1)
            dve.wait_ge(iota_done, 3)
            link(dve.tensor_copy(df[:, :], di[:, :]))
            link(dve.scalar_tensor_tensor(df[:, :], df[:, :], -1.0, df[:, :], ALU.mult, ALU.max))
            link(dve.tensor_scalar(df[0:CHUNK, 192:256], df[0:CHUNK, 192:256], 1e9, None, ALU.add))
            for h in range(HA):
                dve.tensor_scalar(t.alibi_p[:, h], df[:, :], -2.0 ** -(h + 1), None, ALU.mult)
            link(dve.tensor_scalar(qi[:, :], qi[:, :], NF - 1, None, ALU.bitwise_and))
            link(dve.tensor_copy(qf[:, :], qi[:, :]))
            link(dve.tensor_copy(xf[:, :], xi[:, :]))
            link(dve.tensor_scalar(xf[:, :], xf[:, :], qf[:, 0:1], None, ALU.add))
            link(dve.scalar_tensor_tensor(xn[:, :], xf[:, :], -1.0, xf[:, :], ALU.mult, ALU.max))
            for g in range(2):
                for i in range(4):
                    link(dve.memset(slope[32 * i:32 * i + 32, g:g + 1], -2.0 ** -(4 * g + i + 1)))
            for g in range(2):
                dve.tensor_scalar(t.sbias[:, g], xn[:, :], slope[:, g:g + 1], None, ALU.mult)
            dve.wait_ge(lame_done, 1)
            link(dve.tensor_tensor(t.neg_lam[:, :], lame[:, 1:2], lame[:, 0:1], ALU.subtract))
            link(dve.tensor_scalar(t.neg_lam[:, :], t.neg_lam[:, :], -LAM_INIT, None, ALU.add))
            idv = t.ident[:, :].rearrange("p (i j q) -> p i j q", i=4, j=2)
            dve.scalar_tensor_tensor(t.join[:, :].rearrange("p (i q) -> p i q", i=4), idv[:, :, 1], t.neg_lam[:, 0:1],
                                     idv[:, :, 0], ALU.mult, ALU.add)
            dve.wait_ge(g_in, 16)
            dve.tensor_scalar(t.sub_g[:, :], t.sub_g[:, :], 1.0 - LAM_INIT, None, ALU.mult)
            dve.wait_ge(flip_mm, 1)
            dve.tensor_copy(t.sbias[:, 2], PS[:, 4, 0:PAST + NF])
            link(dve.tensor_copy(t.band_p[:, :, :].rearrange("p h x -> p (h x)"), PS[:, 0:4].rearrange("p b x -> p (b x)")))
            dve.memset(t.band_p[0:CHUNK, :, 192:256], -1e30)


def attention_prompt(nc, t):
    PS = t.PS
    GR = [(tile, g) for tile in range(2) for g in range(6)]
    with ExitStack() as ctx:
        sb = lambda n, s, d=F32: ctx.enter_context(nc.sbuf_tensor(n, s, d))
        sem = t.phase_semaphore
        L = sb("L", [P, 2, 2, 2, 256])
        mx = sb("mx", [P, 2, 4])
        lsum = sb("lsum", [P, 2, 4])
        A = sb("A", [P, 2, 4, 256])
        AT = sb("AT", [P, 2, 8, P])
        O = sb("O", [P, 2, DA])
        OBt = sb("OBt", [P, 2, DB])
        sq = sb("sq", [P, DA])
        ss = sb("ss", [P, HA])
        sc_mm, lg_done, exp_done, a_done = sem("sc_mm"), sem("lg_done"), sem("exp_done"), sem("a_done")
        at_mm, at_ev, pv_mm, o_done, o_norm, ot_mm, ot_ev = (sem(x) for x in
            ("at_mm", "at_ev", "pv_mm", "o_done", "o_norm", "ot_mm", "ot_ev"))
        dve_step = sem("prompt_dve")
        ms_done, rms_done = sem("ms_done"), sem("rms_done")
        block = ctx.enter_context(nc.Block())

        def heads(g, j, hh):
            return (slice(64 * j, 64 * j + 64), 2 * g + hh)


        @block.gpsimd
        def _(pool):
            for tile in range(2):
                pool.wait_ge(ms_done, tile + 1)
                pool.tensor_tensor(ss[:, :], ss[:, :], t.power[:, 0:HA], ALU.pow).then_inc(rms_done, 1)

        nmat = lambda tile, g: (2 if g < 4 else 4) * (tile + 1)

        @block.tensor
        def _(pe):
            def scores(n):
                tile, g = GR[n]
                S = P * (tile + 1)
                if n >= 1:
                    pe.wait_ge(lg_done, n)
                for hh in range(2):
                    for j in range(2):
                        rows, u = heads(g, j, hh)
                        mm = pe.matmul(PS[:, j, 256 * hh:256 * hh + S], t.qT[rows, u, P * tile:P * tile + P],
                                       t.kT[rows, u, 0:S], start=True, stop=True)
                mm.then_inc(sc_mm, 1)

            def turn(n):
                tile, g = GR[n]
                pe.wait_ge(a_done, n + 1)
                if n >= 1:
                    pe.wait_ge(at_ev, n)
                for m in range(nmat(tile, g)):
                    hd, st = m // (tile + 1), m % (tile + 1)
                    mm = pe.transpose(PS[:, 2 + m // 4, P * (m % 4):P * (m % 4) + P], A[:, n % 2, hd, P * st:P * st + P], t.ident[:, :])
                mm.then_inc(at_mm, 1)

            def values(n):
                tile, g = GR[n]
                pe.wait_ge(at_ev, n + 1)
                if n >= 2:
                    pe.wait_ge(o_done, n - 1)
                for hd in range(2 if g < 4 else 4):
                    for st in range(tile + 1):
                        if g < 4:
                            v = t.V[:, st, P * (2 * g + hd):P * (2 * g + hd) + P]
                            o = PS[:, 4 + n % 2, P * hd:P * hd + P]
                        else:
                            h = 4 * (g - 4) + hd
                            v = t.V[:, st, DA + HD * h:DA + HD * h + HD]
                            o = PS[:, 4 + n % 2, HD * hd:HD * hd + HD]
                        mm = pe.matmul(o, AT[:, n % 2, hd * (tile + 1) + st], v, start=st == 0, stop=st == tile)
                mm.then_inc(pv_mm, 1)

            def turn_out(tile):
                pe.wait_ge(o_norm, tile + 1)
                for b in range(3):
                    n = 3 * tile + b
                    if n >= 2:
                        pe.wait_ge(ot_ev, n - 1)
                    for m in range(4):
                        src = O[:, tile, P * (4 * b + m):P * (4 * b + m) + P] if b < 2 else OBt[:, tile, P * m:P * m + P]
                        mm = pe.transpose(PS[:, 6 + n % 2, P * m:P * m + P], src, t.ident[:, :])
                    mm.then_inc(ot_mm, 1)

            for n in range(len(GR) + 2):
                if n < len(GR):
                    scores(n)
                if 1 <= n <= len(GR):
                    turn(n - 1)
                if n >= 2:
                    values(n - 2)
                if n == 9:
                    turn_out(0)
            turn_out(1)

        @block.vector
        def _(dve):
            link = make_link(dve, dve_step)

            def logits(n):
                tile, g = GR[n]
                S, x0 = P * (tile + 1), P * (1 - tile)
                dve.wait_ge(sc_mm, n + 1)
                if n >= 2:
                    dve.wait_ge(a_done, n - 1)
                for j in range(2):
                    bias = t.alibi_p[:, 2 * g:2 * g + 2, x0:256] if g < 4 else \
                        t.band_p[:, :, x0:256].rearrange("p (u j) x -> p u j x", j=2)[:, 2 * (g - 4):2 * (g - 4) + 2, j]
                    ins = dve.scalar_tensor_tensor(L[:, n % 2, j, :, 0:S], PS[:, j].rearrange("p (h x) -> p h x", h=2)[:, :, 0:S],
                                                   SM, bias, ALU.mult, ALU.add)
                    link(ins)
                link(dve.tensor_reduce(mx[:, n % 2], L[:, n % 2, :, :, 0:S], AX.X, ALU.max))
                dve.tensor_scalar(mx[:, n % 2], mx[:, n % 2], -1.0, None, ALU.mult).then_inc(lg_done, 1)

            def weights(n):
                tile, g = GR[n]
                S = P * (tile + 1)
                dve.wait_ge(exp_done, n + 1)
                link(dve.reciprocal(lsum[:, n % 2], lsum[:, n % 2]))
                if n >= 2:
                    dve.wait_ge(at_mm, n - 1)
                if g < 4:
                    link(dve.tensor_scalar(lsum[:, n % 2, 2:4], lsum[:, n % 2, 2:4], t.neg_lam[:, 0:1], None, ALU.mult))
                    for hh in range(2):
                        link(dve.tensor_scalar(A[:, n % 2, hh, 0:S], L[:, n % 2, 0, hh, 0:S], lsum[:, n % 2, hh:hh + 1], None, ALU.mult))
                        ins = dve.scalar_tensor_tensor(A[:, n % 2, hh, 0:S], L[:, n % 2, 1, hh, 0:S], lsum[:, n % 2, 2 + hh:3 + hh],
                                                       A[:, n % 2, hh, 0:S], ALU.mult, ALU.add)
                        if hh == 0:
                            link(ins)
                else:
                    for m in range(4):
                        ins = dve.tensor_scalar(A[:, n % 2, m, 0:S], L[:, n % 2, m % 2, m // 2, 0:S],
                                                lsum[:, n % 2, 2 * (m % 2) + m // 2:2 * (m % 2) + m // 2 + 1], None, ALU.mult)
                ins.then_inc(a_done, 1)

            def normalise(tile):
                dve.wait_ge(o_done, 6 * tile + 4)
                link(dve.tensor_tensor(sq[:, :], O[:, tile], O[:, tile], ALU.mult))
                link(dve.tensor_reduce(ss[:, :], sq[:, :].rearrange("p (h e) -> p h e", h=HA), AX.X, ALU.add))
                dve.tensor_scalar(ss[:, :], ss[:, :], 1.0 / P, EPS, ALU.mult, ALU.add).then_inc(ms_done, 1)
                dve.wait_ge(rms_done, tile + 1)
                o3 = O[:, tile].rearrange("p (h e) -> p h e", h=HA)
                link(dve.tensor_tensor(o3, o3, ss[:, :].unsqueeze(2).to_broadcast([P, HA, P]), ALU.mult))
                dve.wait_ge(o_done, 6 * tile + 6)
                dve.tensor_tensor(o3, o3, t.sub_g[:, :].unsqueeze(1).to_broadcast([P, HA, P]), ALU.mult).then_inc(o_norm, 1)

            for n in range(len(GR) + 1):
                if n < len(GR):
                    logits(n)
                if n >= 1:
                    weights(n - 1)
                if n == 9:
                    normalise(0)
            normalise(1)

        @block.scalar
        def _(act):
            outs = [0]

            def out_turned(tile):
                for b in range(3):
                    outs[0] += 1
                    act.wait_ge(ot_mm, outs[0])
                    dst = t.oaT[:, 4 * b:4 * b + 4] if b < 2 else t.obT[:, :]
                    act.copy(dst[:, :, P * tile:P * tile + P], PS[:, 6 + (outs[0] - 1) % 2].rearrange("p (k q) -> p k q", k=4)).then_inc(ot_ev, 1)

            for n in range(len(GR) + 2):
                if n < len(GR):
                    tile, g = GR[n]
                    S = P * (tile + 1)
                    act.wait_ge(lg_done, n + 1)
                    for j in range(2):
                        for hh in range(2):
                            r = L[:, n % 2, j, hh, 0:S]
                            ins = act.activation(r, r, ACT.Exp, bias=mx[:, n % 2, 2 * j + hh:2 * j + hh + 1],
                                                 accum_out=lsum[:, n % 2, 2 * j + hh:2 * j + hh + 1])
                    ins.then_inc(exp_done, 1)
                if 1 <= n <= len(GR):
                    tile, g = GR[n - 1]
                    act.wait_ge(at_mm, n)
                    if n >= 3:
                        act.wait_ge(pv_mm, n - 2)
                    m = nmat(tile, g)
                    act.copy(AT[:, (n - 1) % 2, 0:m].rearrange("p m q -> p (m q)"),
                             PS[:, 2:4].rearrange("p b x -> p (b x)")[:, 0:P * m]).then_inc(at_ev, 1)
                if n >= 2:
                    tile, g = GR[n - 2]
                    act.wait_ge(pv_mm, n - 1)
                    dst = O[:, tile, 256 * g:256 * g + 256] if g < 4 else OBt[:, tile, 256 * (g - 4):256 * (g - 4) + 256]
                    act.copy(dst, PS[:, 4 + n % 2, 0:256]).then_inc(o_done, 1)
                if n == 9:
                    out_turned(0)
            out_turned(1)


def attention_sample(nc, t):
    PS = t.PS
    SW = PAST + NF
    with ExitStack() as ctx:
        sb = lambda n, s, d=F32: ctx.enter_context(nc.sbuf_tensor(n, s, d))
        sem = t.phase_semaphore
        kc = sb("kc", [P, 2, NU, P])
        vc = sb("vc", [P, 2, NU, P])
        kcT = sb("kcT", [P, NU, P])
        qbd = sb("qbd", [P, 2, NU, 32])
        Ls = sb("Ls", [P, 2, 3, SW])
        Pn = sb("Pn", [P, 2, 3, P])
        mxs = sb("mxs", [P, 2, 3])
        sums = sb("sums", [P, 2, 3])
        PT = sb("PT", [P, 6, P])
        Os = sb("Os", [P, 3, NSEQ, P])
        On = sb("On", [64, 2 * NSEQ, P])
        sqs = sb("sqs", [64, 2 * NSEQ, P])
        sss = sb("sss", [64, 2 * NSEQ])
        cache_in = [sem(f"cache_in{i}") for i in range(2)]
        q_done, kct_mm, kct_ev, ssc_mm, slg_done, sexp_done, pn_done = (sem(x) for x in
            ("q_done", "kct_mm", "kct_ev", "ssc_mm", "slg_done", "sexp_done", "pn_done"))
        pt_mm, pt_ev, spv_mm, os_done, join_mm, join_ev, on_done, sot_mm, sot_ev = (sem(x) for x in
            ("pt_mm", "pt_ev", "spv_mm", "os_done", "join_mm", "join_ev", "on_done", "sot_mm", "sot_ev"))
        dve_step = sem("sample_dve")
        sms_done, srms_done = sem("sms_done"), sem("srms_done")
        block = ctx.enter_context(nc.Block())


        @block.gpsimd
        def _(pool):
            pool.wait_ge(sms_done, 1)
            pool.tensor_tensor(sss[:, :], sss[:, :], t.power[0:64, :], ALU.pow).then_inc(srms_done, 1)

        @block.sync
        def _(sp):
            for b in range(NSEQ):
                if b >= 2:
                    sp.wait_ge(spv_mm, b - 1)
                s = cache_in[b % 2]
                sp.dma_start(kc[:, b % 2, 0:8], t.ckd[b]).then_inc(s, 16)
                sp.dma_start(kc[:, b % 2, 8:12], t.ckb[b]).then_inc(s, 16)
                sp.dma_start(vc[:, b % 2, 0:8], t.cvd[b]).then_inc(s, 16)
                sp.dma_start(vc[:, b % 2, 8:12], t.cvb[b]).then_inc(s, 16)

        @block.tensor
        def _(pe):
            def turn_cache(b):
                pe.wait_ge(cache_in[b % 2], 64 * (b // 2 + 1))
                for g in range(3):
                    n = 3 * b + g
                    if n >= 2:
                        pe.wait_ge(kct_ev, n - 1)
                    for i in range(4):
                        mm = pe.transpose(PS[:, n % 2, P * i:P * i + P], kc[:, b % 2, 4 * g + i], t.ident[:, :])
                    mm.then_inc(kct_mm, 1)

            def scores(b):
                pe.wait_ge(q_done, b + 1)
                pe.wait_ge(kct_ev, 3 * b + 3)
                if b >= 1:
                    pe.wait_ge(slg_done, b)
                for g in range(3):
                    for i in range(4):
                        u = 4 * g + i
                        rows = slice(32 * i, 32 * i + 32)
                        pe.matmul(PS[rows, 2, SW * g:SW * g + PAST], qbd[:, b % 2, u], kcT[:, u], start=True, stop=True)
                        mm = pe.matmul(PS[rows, 2, SW * g + PAST:SW * g + SW], qbd[:, b % 2, u],
                                       t.kT[:, u, 256 + NF * b:256 + NF * b + NF], start=True, stop=True)
                mm.then_inc(ssc_mm, 1)

            def turn_p(b):
                pe.wait_ge(pn_done, b + 1)
                if b >= 1:
                    pe.wait_ge(pt_ev, b)
                for m in range(6):
                    src = Ls[:, b % 2, m // 2, 0:PAST] if m % 2 == 0 else Pn[:, b % 2, m // 2]
                    mm = pe.transpose(PS[:, 3 + m // 4, P * (m % 4):P * (m % 4) + P], src, t.ident[:, :])
                mm.then_inc(pt_mm, 1)

            def values(b):
                pe.wait_ge(pt_ev, b + 1)
                if b >= 1:
                    pe.wait_ge(os_done, b)
                for g in range(3):
                    for i in range(4):
                        u = 4 * g + i
                        o = PS[32 * i:32 * i + 32, 5, P * g:P * g + P]
                        pe.matmul(o, PT[:, 2 * g, 32 * i:32 * i + 32], vc[:, b % 2, u], start=True, stop=False)
                        mm = pe.matmul(o, PT[:, 2 * g + 1, 32 * i:32 * i + 32], t.V[:, 2, P * u:P * u + P], start=False, stop=True)
                mm.then_inc(spv_mm, 1)

            turn_cache(0)
            for b in range(NSEQ):
                scores(b)
                if b + 1 < NSEQ:
                    pe.wait_ge(ssc_mm, b + 1)
                    turn_cache(b + 1)
                turn_p(b)
                values(b)
            pe.wait_ge(os_done, NSEQ)
            for n in range(2):
                for i in range(4):
                    mm = pe.transpose(PS[:, n, P * i:P * i + P], Os[:, 2, 4 * n + i], t.ident[:, :])
                mm.then_inc(sot_mm, 1)
            for n in range(4):
                g, b0 = n // 2, 4 * (n % 2)
                if n >= 2:
                    pe.wait_ge(join_ev, n - 1)
                pe.matmul(PS[0:64, 2 + n % 2], t.join[:, :], Os[:, g, b0:b0 + 4].rearrange("p b e -> p (b e)"),
                          start=True, stop=True).then_inc(join_mm, 1)
            pe.wait_ge(on_done, 1)
            pe.wait_ge(sot_ev, 2)
            for n in range(2):
                for i in range(NSEQ):
                    mm = pe.transpose(PS[:, n, 64 * i:64 * i + 64], On[:, NSEQ * n + i], t.ident[0:64, 0:64])
                mm.then_inc(sot_mm, 1)

        @block.scalar
        def _(act):
            def keys(b):
                for g in range(3):
                    n = 3 * b + g
                    act.wait_ge(kct_mm, n + 1)
                    if g == 0 and b >= 1:
                        act.wait_ge(ssc_mm, b)
                    act.copy(kcT[:, 4 * g:4 * g + 4].rearrange("p u s -> p (u s)"), PS[:, n % 2]).then_inc(kct_ev, 1)

            keys(0)
            for b in range(NSEQ):
                act.wait_ge(slg_done, b + 1)
                for g in range(3):
                    r = Ls[:, b % 2, g]
                    ins = act.activation(r, r, ACT.Exp, bias=mxs[:, b % 2, g:g + 1], accum_out=sums[:, b % 2, g:g + 1])
                ins.then_inc(sexp_done, 1)
                if b + 1 < NSEQ:
                    keys(b + 1)
                act.wait_ge(pt_mm, b + 1)
                if b >= 1:
                    act.wait_ge(spv_mm, b)
                act.copy(PT[:, :, :].rearrange("p m s -> p (m s)"), PS[:, 3:5].rearrange("p b x -> p (b x)")[:, 0:6 * P]).then_inc(pt_ev, 1)
            for n in range(2):
                act.wait_ge(sot_mm, n + 1)
                ob = t.obT[:, :, 256 + 64 * n:320 + 64 * n].rearrange("p i (b q) -> p b i q", q=NF)
                src = PS[:, n].rearrange("p (b i j q) -> p b i j q", b=4, i=4, j=2)
                for b in range(4):
                    for j in range(2):
                        rows = slice(64 * j, 64 * j + 64)
                        ins = act.copy(ob[rows, b], src[rows, b, :, j])
                ins.then_inc(sot_ev, 1)
            for n in range(4):
                act.wait_ge(join_mm, n + 1)
                act.copy(On[:, NSEQ * (n // 2) + 4 * (n % 2):NSEQ * (n // 2) + 4 * (n % 2) + 4].rearrange("p b e -> p (b e)"),
                         PS[0:64, 2 + n % 2]).then_inc(join_ev, 1)
            for n in range(2):
                act.wait_ge(sot_mm, 3 + n)
                src = PS[:, n].rearrange("p (b i q) -> p i b q", b=NSEQ, i=4)
                for i in range(4):
                    act.copy(t.oaT[:, 4 * n + i, 256:TOK].rearrange("p (b q) -> p b q", q=NF), src[:, i])

        @block.vector
        def _(dve):
            link = make_link(dve, dve_step)
            link(dve.memset(qbd[:, :, :, :], 0.0))
            link(dve.memset(Pn[:, :, :, :], 0.0))

            def queries(b):
                if b >= 2:
                    dve.wait_ge(ssc_mm, b - 1)
                for j in range(2):
                    rows = slice(64 * j, 64 * j + 64)
                    ins = dve.tensor_copy(qbd[rows, b % 2, :, NF * j:NF * j + NF], t.qT[rows, :, 256 + NF * b:256 + NF * b + NF])
                ins.then_inc(q_done, 1)

            queries(0)
            for b in range(NSEQ):
                r = Ls[:, b % 2]
                dve.wait_ge(ssc_mm, b + 1)
                if b >= 2:
                    dve.wait_ge(pt_mm, b - 1)
                    link(dve.memset(Pn[:, b % 2, :, NF * (b - 2):NF * (b - 2) + NF], 0.0))
                link(dve.scalar_tensor_tensor(r.rearrange("p g s -> p (g s)"), PS[:, 2, 0:3 * SW], SM,
                                              t.sbias[:, :, :].rearrange("p g s -> p (g s)"), ALU.mult, ALU.add))
                link(dve.tensor_reduce(mxs[:, b % 2], r, AX.X, ALU.max))
                dve.tensor_scalar(mxs[:, b % 2], mxs[:, b % 2], -1.0, None, ALU.mult).then_inc(slg_done, 1)
                if b + 1 < NSEQ:
                    queries(b + 1)
                dve.wait_ge(sexp_done, b + 1)
                dve.tensor_copy(Pn[:, b % 2, :, NF * b:NF * b + NF], r[:, :, PAST:SW]).then_inc(pn_done, 1)
                link(dve.reciprocal(sums[:, b % 2], sums[:, b % 2]))
                dve.wait_ge(spv_mm, b + 1)
                dve.tensor_tensor(Os[:, :, b], PS[:, 5, 0:3 * P].rearrange("p (g e) -> p g e", g=3),
                                  sums[:, b % 2].unsqueeze(2).to_broadcast([P, 3, P]), ALU.mult).then_inc(os_done, 1)
            dve.wait_ge(join_ev, 4)
            link(dve.tensor_tensor(sqs[:, :, :], On[:, :, :], On[:, :, :], ALU.mult))
            link(dve.tensor_reduce(sss[:, :], sqs[:, :, :], AX.X, ALU.add))
            dve.tensor_scalar(sss[:, :], sss[:, :], 1.0 / P, EPS, ALU.mult, ALU.add).then_inc(sms_done, 1)
            dve.wait_ge(srms_done, 1)
            link(dve.tensor_tensor(On[:, :, :], On[:, :, :], sss[:, :].unsqueeze(2).to_broadcast([64, 2 * NSEQ, P]), ALU.mult))
            dve.tensor_tensor(On[:, :, :], On[:, :, :], t.sub_g[0:64, :].unsqueeze(1).to_broadcast([64, 2 * NSEQ, P]),
                              ALU.mult).then_inc(on_done, 1)


def projection_out(nc, t):
    PS = t.PS
    with ExitStack() as ctx:
        sb = lambda n, s, d=F32: ctx.enter_context(nc.sbuf_tensor(n, s, d))
        sem = t.phase_semaphore
        M = sb("M", [P, NT, D])
        MT = sb("MT", [P, KD, TOK])
        U2 = sb("U2", [P, NT, D])
        W4 = sb("W4", [P, 4, KD, CW])
        bg = sb("bg", [P, 2, 2, CW])
        ga, gb, ma = sb("ga", [P, CW]), sb("gb", [P, CW]), sb("ma", [P, CW])
        vec = sb("vec", [P, 2, D])
        vec2 = sb("vec2", [P, 2, D])
        ln = layer_norm_state(t, sb, sem, "_4")
        w4_in = [sem(f"w4_in{i}") for i in range(4)]
        bg_in, vec_in, vec_in2 = sem("bg_in"), sem("vec_in"), sem("vec_in2")
        g_mm, g_add, g_sig, m_ev, mt_mm, mt_ev, y_mm, y_ev = (sem(x) for x in
            ("g_mm", "g_add", "g_sig", "m_ev", "mt_mm", "mt_ev", "y_mm", "y_ev"))
        x1_done, u2_done, u2_out, u2t_mm, u2t_ev = (sem(x) for x in ("x1_done", "u2_done", "u2_out", "u2t_mm", "u2t_ev"))
        G0 = 3 * DA + 3 * DB
        dve_step = sem("proj_dve")
        block = ctx.enter_context(nc.Block())
        win = t.w_in[0].rearrange("(k p) n -> p k n", p=P)

        @block.sync
        def _(sp):
            for g in range(2):
                for c in range(2):
                    sp.dma_start(bg[:, g, c], t.b_in[:, G0 + D * g + CW * c:G0 + D * g + CW * c + CW].to_broadcast([P, CW])).then_inc(bg_in, 16)
            for c in range(2):
                if c:
                    sp.wait_ge(g_mm, 3)
                cols = slice(CW * c, CW * c + CW)
                sp.dma_start(W4[:, 0], win[:, :, G0 + CW * c:G0 + CW * c + CW]).then_inc(w4_in[0], 16)
                sp.dma_start(W4[:, 1], win[:, :, G0 + D + CW * c:G0 + D + CW * c + CW]).then_inc(w4_in[1], 16)
                sp.dma_start(W4[:, 2], t.p_a[0].rearrange("(k p) n -> p k n", p=P)[:, :, cols]).then_inc(w4_in[2], 16)
                sp.dma_start(W4[:, 3, 0:4], t.p_b[0].rearrange("(k p) n -> p k n", p=P)[:, :, cols]).then_inc(w4_in[3], 16)
                if c == 0:
                    t.load_mod(sp, vec, 2, vec_in)
                    sp.dma_start(vec2[:, 0], t.ln1_g.to_broadcast([P, D])).then_inc(vec_in, 16)
                    sp.dma_start(vec2[:, 1], t.ln1_b.to_broadcast([P, D])).then_inc(vec_in, 16)
            sp.wait_ge(g_mm, 6)
            for c in range(2):
                sp.dma_start(W4[:, c], t.w_out[0].rearrange("(k p) n -> p k n", p=P)[:, :, CW * c:CW * c + CW]).then_inc(w4_in[c], 16)
            sp.wait_ge(x1_done, NT)
            t.load_mod(sp, vec, 3, vec_in2)
            t.load_mod(sp, vec2, 4, vec_in2)
            for n in range(NT):
                sp.wait_ge(u2_done, n + 1)
                sp.dma_start(t.h_dram[P * n:P * n + P], U2[:, n]).then_inc(u2_out, 16)
            sp.wait_ge(u2_out, 16 * NT)

        @block.tensor
        def _(pe):
            for c in range(2):
                for n in range(NT):
                    m = NT * c + n
                    if n == 0:
                        for i in range(4):
                            pe.wait_ge(w4_in[i], 16 * (c + 1))
                    if m:
                        pe.wait_ge(m_ev, m)
                    q = slice(P * n, P * n + P)
                    for i, src, K in ((0, t.uT, 8), (1, t.uT, 8), (2, t.oaT, 8), (3, t.obT, 4)):
                        for k in range(K):
                            mm = pe.matmul(PS[:, i], src[:, k, q], W4[:, i, k], start=k == 0, stop=k == K - 1)
                    mm.then_inc(g_mm, 1)
            for n in range(NT):
                pe.wait_ge(m_ev, 4 + n)
                for half in range(2):
                    j = 2 * n + half
                    if j >= 2:
                        pe.wait_ge(mt_ev, j - 1)
                    for k in range(4):
                        mm = pe.transpose(PS[:, 4 + j % 2, P * k:P * k + P], M[:, n, P * (4 * half + k):P * (4 * half + k) + P], t.ident[:, :])
                    mm.then_inc(mt_mm, 1)
            for n in range(NT):
                pe.wait_ge(mt_ev, 2 * n + 2)
                if n == 0:
                    pe.wait_ge(w4_in[0], 48)
                    pe.wait_ge(w4_in[1], 48)
                if n == 2:
                    pe.wait_ge(y_ev, 1)
                for c in range(2):
                    for k in range(KD):
                        mm = pe.matmul(PS[:, 2 * (n % 2) + c], MT[:, k, P * n:P * n + P], W4[:, c, k], start=k == 0, stop=k == KD - 1)
                mm.then_inc(y_mm, 1)
            for n in range(NT):
                pe.wait_ge(u2_done, n + 1)
                for half in range(2):
                    j = 2 * n + half
                    if j >= 2:
                        pe.wait_ge(u2t_ev, j - 1)
                    for k in range(4):
                        mm = pe.transpose(PS[:, 4 + j % 2, P * k:P * k + P], U2[:, n, P * (4 * half + k):P * (4 * half + k) + P], t.ident[:, :])
                    mm.then_inc(u2t_mm, 1)

        @block.gpsimd
        def _(pool):
            rsqrts(pool, ln, *range(2 * NT))

        @block.scalar
        def _(act):
            for m in range(2 * NT):
                act.wait_ge(g_add, m + 1)
                act.activation(ga[:, :], ga[:, :], ACT.Sigmoid)
                act.activation(gb[:, :], gb[:, :], ACT.Sigmoid).then_inc(g_sig, 1)
            for mm, ev, dst in ((mt_mm, mt_ev, MT), (u2t_mm, u2t_ev, t.hT)):
                for j in range(6):
                    act.wait_ge(mm, j + 1)
                    act.copy(dst[:, 4 * (j % 2):4 * (j % 2) + 4, P * (j // 2):P * (j // 2) + P],
                             PS[:, 4 + j % 2].rearrange("p (k q) -> p k q", k=4)).then_inc(ev, 1)

        @block.vector
        def _(dve):
            link = make_link(dve, dve_step)
            dve.wait_ge(bg_in, 64)
            for m in range(2 * NT):
                c, n = m // NT, m % NT
                dve.wait_ge(g_mm, m + 1)
                dve.tensor_tensor(ga[:, :], PS[:, 0], bg[:, 0, c], ALU.add)
                dve.tensor_tensor(gb[:, :], PS[:, 1], bg[:, 1, c], ALU.add).then_inc(g_add, 1)
                dve.wait_ge(g_sig, m + 1)
                dve.tensor_tensor(ga[:, :], PS[:, 2], ga[:, :], ALU.mult)
                link(dve.tensor_tensor(gb[:, :], PS[:, 3], gb[:, :], ALU.mult))
                link(dve.tensor_tensor(M[:, n, CW * c:CW * c + CW], ga[:, :], gb[:, :], ALU.add))
                dve.sem_inc(m_ev, 1)
            dve.wait_ge(vec_in, 64)
            for n in range(NT):
                dve.wait_ge(y_mm, n + 1)
                dve.wait_ge(mt_mm, 2 * n + 2)
                r = M[:, n]
                y = PS[:, 2 * (n % 2):2 * (n % 2) + 2].rearrange("p b x -> p (b x)")
                link(dve.tensor_tensor(r, y, vec[:, n // 2], ALU.mult))
                dve.sem_inc(y_ev, 1)
                link(dve.scalar_tensor_tensor(r, t.X[:, n], ALPHA, r, ALU.mult, ALU.add))
                layer_norm(dve, link, ln, t.X[:, n], r)
                link(dve.tensor_tensor(t.X[:, n], t.X[:, n], vec2[:, 0], ALU.mult))
                link(dve.tensor_tensor(t.X[:, n], t.X[:, n], vec2[:, 1], ALU.add))
                dve.sem_inc(x1_done, 1)
            dve.wait_ge(vec_in2, 64)
            for n in range(NT):
                layer_norm(dve, link, ln, M[:, n], t.X[:, n])
                link(dve.scalar_tensor_tensor(M[:, n], vec2[:, n // 2], 1.0, M[:, n], ALU.add, ALU.mult))
                dve.tensor_tensor(U2[:, n].rearrange("r (k p) -> r p k", k=KD), M[:, n].rearrange("r (p k) -> r p k", k=KD),
                                  vec[:, n // 2].rearrange("r (p k) -> r p k", k=KD), ALU.add).then_inc(u2_done, 1)


def load_expert(sp, t, e, i):
    s = t.wexp_in[i]
    sp.dma_start(t.W13[:, i, 0], t.w1v[e] if isinstance(e, int) else t.w1v[bass.ds(e, 1)].rearrange("e p k n -> (e p) k n")).then_inc(s, 16)
    sp.dma_start(t.W13[:, i, 1], t.w3v[e] if isinstance(e, int) else t.w3v[bass.ds(e, 1)].rearrange("e p k n -> (e p) k n")).then_inc(s, 16)
    sp.dma_start(t.W2[:, i], t.w2v[e] if isinstance(e, int) else t.w2v[bass.ds(e, 1)].rearrange("e p k n -> (e p) k n")).then_inc(s, 16)


def routing(nc, t):
    PS = t.PS
    with ExitStack() as ctx:
        sb = lambda n, s, d=F32: ctx.enter_context(nc.sbuf_tensor(n, s, d))
        sem = t.phase_semaphore
        wr = sb("wr", [P, KD, E])
        ws13 = sb("ws13", [P, KD, 2, F])
        ws2 = sb("ws2_sb", [P, 2, D])
        ebias = sb("ebias", [P, E])
        sc = sb("sc", [P, NT, E])
        bi = sb("bi", [P, E])
        g8 = sb("g8", [P, NG, 8])
        gs, gm, gn = sb("gs", [P, NG]), sb("gm", [P, NG]), sb("gn", [P, NG])
        cmp, tie, gi = sb("cmp", [P, NG, NG]), sb("tie", [P, NG, NG]), sb("gi", [P, NG, NG], I32)
        t8, i8, i8f = sb("t8", [P, 8]), sb("i8", [P, 8], U32), sb("i8f", [P, 8])
        oh = sb("oh", [P, NT, TOPK, E])
        tmp = sb("tmp", [P, TOPK, E])
        mask = sb("mask", [P, NT, E], F16)
        wsum = sb("wsum", [P, 1])
        tri, ones = sb("tri", [P, P], F16), sb("ones", [P, P], F16)
        tri_f = sb("tri_f", [P, P])
        io_i, io = sb("io_i", [P, P], I32), sb("io", [P, P])
        tk_i, tk = sb("tk_i", [P, NT], I32), sb("tk", [P, NT])
        cnt, ext, inc, base = sb("cnt", [P, E]), sb("ext", [P, E]), sb("inc", [P, E]), sb("base", [P, E])
        one_e = sb("one_e", [P, E])
        code, code2 = sb("code", [P, E]), sb("code2", [P, E])
        ck, si, ci = sb("ck", [P, TOPK]), sb("si", [P, TOPK], I32), sb("ci", [P, TOPK], I32)
        sf, cf = sb("sf", [P, TOPK]), sb("cf", [P, TOPK])
        SL = sb("SL", [P, 2, TOPK, SLOTS], F16)
        CB = sb("CB", [P, 2, TOPK, NBLK], F16)
        CBf = sb("CBf", [P, TOPK, NBLK])
        sh_g, sh_h, sh_T = sb("sh_g", [P, 2, F]), sb("sh_h", [P, NT, F]), sb("sh_T", [P, 2, 2, P])
        wr_in, ws_in, eb_in = sem("wr_in"), sem("ws_in"), sem("eb_in")
        r_mm, sig_done, mask_done, rank_mm, cnt_mm, code_done, list_mm, iota_done = (sem(x) for x in
            ("r_mm", "sig_done", "mask_done", "rank_mm", "cnt_mm", "code_done", "list_mm", "riota_done"))
        s_mm, s_silu, s_hid, st_mm, st_ev, sy_mm, sy_ev, rc_done = (sem(x) for x in
            ("s_mm", "s_silu", "s_hid", "st_mm", "st_ev", "sy_mm", "sy_ev", "rc_done"))
        dve_step = sem("route_dve")
        block = ctx.enter_context(nc.Block())

        @block.sync
        def _(sp):
            sp.dma_start(wr[:, :, :], t.w_router[0].rearrange("(p k) e -> p k e", k=KD)).then_inc(wr_in, 16)
            sp.dma_start(ebias[:, :], t.e_bias.to_broadcast([P, E])).then_inc(eb_in, 16)
            sp.dma_start(ws13[:, :, 0], t.ws1[0].rearrange("(p k) n -> p k n", k=KD)).then_inc(ws_in, 16)
            sp.dma_start(ws13[:, :, 1], t.ws3[0].rearrange("(p k) n -> p k n", k=KD)).then_inc(ws_in, 16)
            sp.dma_start(ws2[:, :, :], t.ws2[0].rearrange("(p k) n -> p k n", k=2)).then_inc(ws_in, 16)
            for i in range(WB):
                load_expert(sp, t, i, i)

        @block.gpsimd
        def _(pool):
            pool.iota(io_i[:, :], pattern=[[1, P]], base=0, channel_multiplier=0).then_inc(iota_done, 1)
            pool.iota(tk_i[:, :], pattern=[[P, NT]], base=0, channel_multiplier=1).then_inc(iota_done, 1)
            pool.iota(gi[:, :, :], pattern=[[1, NG], [-1, NG]], base=0, channel_multiplier=0).then_inc(iota_done, 1)

        @block.tensor
        def _(pe):
            pe.wait_ge(wr_in, 16)
            for n in range(NT):
                for k in range(KD):
                    mm = pe.matmul(PS[:, n, 0:E], t.hT[:, k, P * n:P * n + P], wr[:, k], start=k == 0, stop=k == KD - 1)
                mm.then_inc(r_mm, 1)
            pe.wait_ge(ws_in, 48)
            for n in range(NT):
                if n >= 2:
                    pe.wait_ge(s_hid, n - 1)
                for k in range(KD):
                    mm = pe.matmul(PS[:, 4 + n % 2], t.hT[:, k, P * n:P * n + P], ws13[:, k].rearrange("p j n -> p (j n)"),
                                   start=k == 0, stop=k == KD - 1)
                mm.then_inc(s_mm, 1)
                pe.wait_ge(mask_done, n + 1)
                for m in range(n):
                    pe.matmul(PS[:, n, 64:64 + E], ones[:, :], mask[:, m], start=m == 0, stop=False)
                pe.matmul(PS[:, n, 64:64 + E], tri[:, :], mask[:, n], start=n == 0, stop=True).then_inc(rank_mm, 1)
            for m in range(NT):
                mm = pe.matmul(PS[:, 3, 0:E], ones[:, :], mask[:, m], start=m == 0, stop=m == NT - 1)
            mm.then_inc(cnt_mm, 1)
            for n in range(NT):
                pe.wait_ge(s_hid, NT)
                if n:
                    pe.wait_ge(st_ev, n)
                for j in range(2):
                    mm = pe.transpose(PS[:, 6, P * j:P * j + P], sh_h[:, n, P * j:P * j + P], t.ident[:, :])
                mm.then_inc(st_mm, 1)
                pe.wait_ge(st_ev, n + 1)
                if n:
                    pe.wait_ge(sy_ev, n)
                for c in range(2):
                    for j in range(2):
                        mm = pe.matmul(PS[:, 4 + 3 * c], sh_T[:, n % 2, j], ws2[:, j, CW * c:CW * c + CW], start=j == 0, stop=j == 1)
                mm.then_inc(sy_mm, 1)
            for n in range(NT):
                pe.wait_ge(code_done, n + 1)
                for k in range(TOPK):
                    mm = pe.matmul(PS[0:SLOTS, 5, 0:NBLK], SL[:, n % 2, k], CB[:, n % 2, k], start=n + k == 0, stop=n == NT - 1 and k == TOPK - 1)
                mm.then_inc(list_mm, 1)

        @block.scalar
        def _(act):
            for n in range(NT):
                act.wait_ge(r_mm, n + 1)
                act.activation(sc[:, n], PS[:, n, 0:E], ACT.Sigmoid).then_inc(sig_done, 1)
            for n in range(NT):
                act.wait_ge(s_mm, n + 1)
                if n >= 2:
                    act.wait_ge(s_hid, n - 1)
                act.activation(sh_g[:, n % 2], PS[:, 4 + n % 2, 0:F], ACT.Silu).then_inc(s_silu, 1)
            for n in range(NT):
                act.wait_ge(st_mm, n + 1)
                if n >= 2:
                    act.wait_ge(sy_mm, n - 1)
                act.copy(sh_T[:, n % 2].rearrange("p j q -> p (j q)"), PS[:, 6, 0:2 * P]).then_inc(st_ev, 1)
                act.wait_ge(sy_mm, n + 1)
                for c in range(2):
                    ins = act.copy(t.acc[:, n, CW * c:CW * c + CW], PS[:, 4 + 3 * c])
                ins.then_inc(sy_ev, 1)

        @block.vector
        def _(dve):
            link = make_link(dve, dve_step)
            dve.wait_ge(iota_done, 3)
            link(dve.tensor_copy(io[:, :], io_i[:, :]))
            link(dve.tensor_copy(tk[:, :], tk_i[:, :]))
            link(dve.tensor_scalar(tie[:, :, :], gi[:, :, :], 0.0, None, ALU.is_gt))
            link(dve.tensor_scalar(tri[:, :], io[:, :], tk[:, 0:1], None, ALU.is_gt))
            link(dve.memset(ones[:, :], 1.0))
            link(dve.memset(one_e[:, :], 1.0))
            dve.wait_ge(eb_in, 16)

            def hidden(n):
                dve.wait_ge(s_silu, n + 1)
                dve.tensor_tensor(sh_h[:, n].rearrange("r (j p) -> r p j", j=2), sh_g[:, n % 2].rearrange("r (p j) -> r p j", j=2),
                                  PS[:, 4 + n % 2, F:2 * F].rearrange("r (p j) -> r p j", j=2), ALU.mult).then_inc(s_hid, 1)

            for n in range(NT):
                dve.wait_ge(sig_done, n + 1)
                link(dve.tensor_tensor(bi[:, :], sc[:, n], ebias[:, :], ALU.add))
                for g in range(NG):
                    ins = dve.max(g8[:, g], bi[:, 8 * g:8 * g + 8])
                link(ins)
                link(dve.tensor_tensor(gs[:, :], g8[:, :, 0], g8[:, :, 1], ALU.add))
                mine = gs[:, :].unsqueeze(2).to_broadcast([P, NG, NG])
                other = gs[:, :].unsqueeze(1).to_broadcast([P, NG, NG])
                link(dve.tensor_tensor(cmp[:, :, :], other, mine, ALU.is_equal))
                link(dve.tensor_tensor(cmp[:, :, :], cmp[:, :, :], tie[:, :, :], ALU.mult))
                link(dve.tensor_reduce(gm[:, :], cmp[:, :, :], AX.X, ALU.add))
                link(dve.tensor_tensor(cmp[:, :, :], other, mine, ALU.is_gt))
                link(dve.tensor_reduce(gn[:, :], cmp[:, :, :], AX.X, ALU.add))
                link(dve.tensor_tensor(gm[:, :], gm[:, :], gn[:, :], ALU.add))
                link(dve.tensor_scalar(gm[:, :], gm[:, :], float(TOPG), None, ALU.is_lt))
                link(dve.tensor_scalar(gn[:, :], gm[:, :], -1.0, 1e30, ALU.add, ALU.mult))
                b3 = bi[:, :].rearrange("p (g e) -> p g e", g=NG)
                link(dve.tensor_tensor(b3, b3, gm[:, :].unsqueeze(2).to_broadcast([P, NG, 8]), ALU.mult))
                link(dve.tensor_tensor(b3, b3, gn[:, :].unsqueeze(2).to_broadcast([P, NG, 8]), ALU.add))
                link(dve.max(t8[:, :], bi[:, :]))
                link(dve.max_index(i8[:, :], t8[:, :], bi[:, :]))
                link(dve.tensor_copy(i8f[:, :], i8[:, :]))
                link(dve.tensor_tensor(oh[:, n], io[:, 0:E].unsqueeze(1).to_broadcast([P, TOPK, E]),
                                       i8f[:, :].unsqueeze(2).to_broadcast([P, TOPK, E]), ALU.is_equal))
                with nc.allow_low_precision("a count of at most one"):
                    dve.tensor_reduce(mask[:, n], oh[:, n].rearrange("p k e -> p e k"), AX.X, ALU.add).then_inc(mask_done, 1)
                link(dve.tensor_tensor(tmp[:, :, :], oh[:, n], sc[:, n].unsqueeze(1).to_broadcast([P, TOPK, E]), ALU.mult))
                link(dve.tensor_reduce(t.wts[:, n], tmp[:, :, :], AX.X, ALU.add))
                link(dve.tensor_reduce(wsum[:, :], t.wts[:, n], AX.X, ALU.add))
                link(dve.reciprocal(wsum[:, :], wsum[:, :]))
                link(dve.tensor_scalar(t.wts[:, n], t.wts[:, n], wsum[:, 0:1], ROUTED_SCALE, ALU.mult, ALU.mult))
                hidden(n)
            dve.wait_ge(cnt_mm, 1)
            link(dve.tensor_copy(cnt[:, :], PS[:, 3, 0:E]))
            link(dve.tensor_scalar(ext[:, :], cnt[:, :], float(SLOTS), None, ALU.is_gt))
            for m in range(2, TOK // SLOTS):
                link(dve.scalar_tensor_tensor(ext[:, :], cnt[:, :], float(SLOTS * m), ext[:, :], ALU.is_gt, ALU.add))
            link(dve.tensor_tensor_scan(inc[:, :], one_e[:, :], ext[:, :], 0.0, ALU.mult, ALU.add))
            link(dve.memset(t.ov[:, 0:1], 0))
            link(dve.tensor_copy(t.ov[:, 1:E + 1], inc[0:1, :]))
            link(dve.tensor_tensor(base[:, :], inc[:, :], ext[:, :], ALU.subtract))
            link(dve.tensor_tensor(base[:, :], base[:, :], io[:, 0:E], ALU.subtract))
            link(dve.tensor_scalar(base[:, :], base[:, :], float(E - 1), None, ALU.add))
            for n in range(NT):
                dve.wait_ge(rank_mm, n + 1)
                link(dve.tensor_copy(code2[:, :], PS[:, n, 64:64 + E]))
                link(dve.scalar_tensor_tensor(code[:, :], code2[:, :], float(SLOTS), base[:, :], ALU.is_ge, ALU.mult))
                link(dve.tensor_tensor(code[:, :], code[:, :], io[:, 0:E], ALU.add))
                link(dve.scalar_tensor_tensor(code[:, :], code[:, :], float(SLOTS), code2[:, :], ALU.mult, ALU.add))
                link(dve.tensor_tensor(tmp[:, :, :], oh[:, n], code[:, :].unsqueeze(1).to_broadcast([P, TOPK, E]), ALU.mult))
                link(dve.tensor_reduce(ck[:, :], tmp[:, :, :], AX.X, ALU.add))
                link(dve.tensor_copy(t.rows[:, n], ck[:, :]))
                link(dve.tensor_scalar(si[:, :], t.rows[:, n], SLOTS - 1, None, ALU.bitwise_and))
                link(dve.tensor_scalar(ci[:, :], t.rows[:, n], 6, None, ALU.logical_shift_right))
                link(dve.tensor_copy(sf[:, :], si[:, :]))
                link(dve.tensor_copy(cf[:, :], ci[:, :]))
                if n >= 2:
                    dve.wait_ge(list_mm, n - 1)
                link(dve.tensor_tensor(SL[:, n % 2], io[:, 0:SLOTS].unsqueeze(1).to_broadcast([P, TOPK, SLOTS]),
                                       sf[:, :].unsqueeze(2).to_broadcast([P, TOPK, SLOTS]), ALU.is_equal))
                link(dve.tensor_tensor(CBf[:, :, :], io[:, 0:NBLK].unsqueeze(1).to_broadcast([P, TOPK, NBLK]),
                                       cf[:, :].unsqueeze(2).to_broadcast([P, TOPK, NBLK]), ALU.is_equal))
                dve.tensor_scalar(CB[:, n % 2], CBf[:, :, :], tk[:, n:n + 1], None, ALU.mult).then_inc(code_done, 1)
            dve.wait_ge(list_mm, NT)
            dve.tensor_copy(t.tokens[:, :], PS[0:SLOTS, 5, 0:NBLK])


def experts(nc, t):
    PS = t.PS
    with ExitStack() as ctx:
        sb = lambda n, s, d=F32: ctx.enter_context(nc.sbuf_tensor(n, s, d))
        sem = t.phase_semaphore
        XG = sb("XG", [SLOTS, WB, D])
        XT = sb("XT", [P, 2, KD, SLOTS])
        sg, hid, hidT = sb("sg", [SLOTS, 2, F]), sb("hid", [SLOTS, 2, F]), sb("hidT", [P, 2, 2, SLOTS])
        Y = sb("Y", [P, 2, CW])
        ix = sb("ix", [SLOTS, WB], I32)
        XGo, XTo = sb("XGo", [SLOTS, D]), sb("XTo", [P, KD, SLOTS])
        sgo, hido, hidTo = sb("sgo", [SLOTS, F]), sb("hido", [SLOTS, F]), sb("hidTo", [P, 2, SLOTS])
        Yo = sb("Yo", [P, CW])
        ixo = sb("ixo", [SLOTS, 1], I32)
        g_in = [sem(f"g_in{i}") for i in range(WB)]
        y_out = [sem(f"y_out{i}") for i in range(2)]
        ix_done, xt_mm, xt_ev, h_mm, silu_done, hid_done, ht_mm, ht_ev, yy_mm, yy_ev = (sem(x) for x in
            ("ix_done", "xt_mm", "xt_ev", "h_mm", "esilu_done", "hid_done", "ht_mm", "ht_ev", "yy_mm", "yy_ev"))
        o_ix, o_in, o_xt, o_xe, o_h, o_silu, o_hid, o_ht, o_he, o_y, o_ye, o_out = (sem(x) for x in
            ("o_ix", "o_in", "o_xt", "o_xe", "o_h", "o_silu", "o_hid", "o_ht", "o_he", "o_y", "o_ye", "o_out"))
        waited = sem("waited")
        block = ctx.enter_context(nc.Block())

        def at(it, i, off=0):
            return it * WB + (i + off)

        def extra(eng, e, step):
            lo = eng.value_load(t.ov[0:1, bass.ds(e, 1)], min_val=0, max_val=XB)
            hi = eng.value_load(t.ov[0:1, bass.ds(e + 1, 1)], min_val=0, max_val=XB)
            with eng.If(lo < hi):
                with eng.Fori(lo, hi) as g:
                    step(g)

        def once_above(eng, semaphore, count):
            if not isinstance(count, int) or count > 0:
                eng.wait_ge(semaphore, count)

        def stand_alone(eng):
            eng.sem_inc(waited, 1)

        def loops(eng, body):
            for i in range(WB):
                body(0, i, False)
            with eng.Fori(1, E // WB - 1) as it:
                for i in range(WB):
                    body(it, i, False)
            for i in range(WB):
                body(E // WB - 1, i, True)

        @block.sync
        def _(sp):
            def store_extra(g):
                sp.wait_ge(o_ye, g + 1)
                for h in range(2):
                    sp.dma_start(t.y_dram[bass.ds((g + E) * SLOTS, SLOTS), CW * h:CW * h + CW], Yo[64 * h:64 * h + 64, :]).then_inc(o_out, 16)

            def body(it, i, last):
                sp.wait_ge(yy_ev, at(it, i, 1))
                for h in range(2):
                    sp.dma_start(t.y_dram[bass.ds(at(it, i) * SLOTS, SLOTS), CW * h:CW * h + CW], Y[64 * h:64 * h + 64, i % 2]).then_inc(y_out[i % 2], 16)
                extra(sp, at(it, i), store_extra)
                if not last:
                    load_expert(sp, t, at(it, i, WB), i)
            loops(sp, body)
            for i in range(2):
                sp.wait_ge(y_out[i], 32 * E // 2)
            total = sp.value_load(t.ov[0:1, E:E + 1], min_val=0, max_val=XB)
            with sp.If(total > 0):
                sp.wait_ge(o_out, total * 32)
                stand_alone(sp)

        @block.gpsimd
        def _(pool):
            def gather(e, i, n):
                pool.tensor_copy(ix[:, i:i + 1], t.tokens[:, bass.ds(e, 1)]).then_inc(ix_done, 1)
                pool.wait_ge(ix_done, n)
                stand_alone(pool)
                pool.indirect_dma_start(XG[:, i], None, t.h_dram, bass.IndirectOffsetOnAxis(ap=ix[:, i:i + 1], axis=0)).then_inc(g_in[i], 16)

            def gather_extra(g):
                with pool.If(g > 0):
                    pool.wait_ge(o_xt, g)
                pool.tensor_copy(ixo[:, 0:1], t.tokens[:, bass.ds(g + E, 1)]).then_inc(o_ix, 1)
                pool.wait_ge(o_ix, g + 1)
                stand_alone(pool)
                pool.indirect_dma_start(XGo[:, :], None, t.h_dram, bass.IndirectOffsetOnAxis(ap=ixo[:, 0:1], axis=0)).then_inc(o_in, 16)

            for i in range(WB):
                gather(i, i, i + 1)

            def body(it, i, last):
                extra(pool, at(it, i), gather_extra)
                if not last:
                    pool.wait_ge(xt_mm, at(it, i, 1))
                    gather(at(it, i, WB), i, at(it, i, WB + 1))
            loops(pool, body)

        @block.tensor
        def _(pe):
            def turn(n, i, it):
                pe.wait_ge(g_in[i], (it + 1) * 16)
                once_above(pe, xt_ev, n - 1)
                stand_alone(pe)
                for k in range(KD):
                    mm = pe.transpose(PS[:, i % 2, SLOTS * k:SLOTS * k + SLOTS], XG[:, i, P * k:P * k + P], t.ident[0:SLOTS, 0:SLOTS])
                mm.then_inc(xt_mm, 1)

            def up(n, i, it):
                pe.wait_ge(t.wexp_in[i], (it + 1) * 48)
                pe.wait_ge(xt_ev, n + 1)
                once_above(pe, hid_done, n - 1)
                for k in range(KD):
                    for h in range(2):
                        mm = pe.matmul(PS[64 * h:64 * h + 64, 2 + i % 2, 0:F], XT[:, i % 2, k], t.W13[:, i, h, k], start=k == 0, stop=k == KD - 1)
                mm.then_inc(h_mm, 1)

            def extra_block(i):
                def step(g):
                    pe.wait_ge(o_in, (g + 1) * 16)
                    with pe.If(g > 0):
                        pe.wait_ge(o_ye, g)
                    stand_alone(pe)
                    for k in range(KD):
                        mm = pe.transpose(PS[:, 7, SLOTS * k:SLOTS * k + SLOTS], XGo[:, P * k:P * k + P], t.ident[0:SLOTS, 0:SLOTS])
                    mm.then_inc(o_xt, 1)
                    pe.wait_ge(o_xe, g + 1)
                    for k in range(KD):
                        for h in range(2):
                            mm = pe.matmul(PS[64 * h:64 * h + 64, 7, 0:F], XTo[:, k], t.W13[:, i, h, k], start=k == 0, stop=k == KD - 1)
                    mm.then_inc(o_h, 1)
                    pe.wait_ge(o_hid, g + 1)
                    stand_alone(pe)
                    for j in range(2):
                        mm = pe.transpose(PS[:, 7, SLOTS * j:SLOTS * j + SLOTS], hido[:, P * j:P * j + P], t.ident[0:SLOTS, 0:SLOTS])
                    mm.then_inc(o_ht, 1)
                    pe.wait_ge(o_he, g + 1)
                    for j in range(2):
                        for h in range(2):
                            mm = pe.matmul(PS[64 * h:64 * h + 64, 7], hidTo[:, j], t.W2[:, i, j, CW * h:CW * h + CW], start=j == 0, stop=j == 1)
                    mm.then_inc(o_y, 1)
                return step

            def body(it, i, last):
                n = at(it, i)
                nxt = (it + (i + 1) // WB, (i + 1) % WB)
                nx2 = (it + (i + 2) // WB, (i + 2) % WB)
                if not last or i + 1 < WB:
                    up(at(it, i, 1), nxt[1], nxt[0])
                pe.wait_ge(hid_done, n + 1)
                once_above(pe, ht_ev, n)
                stand_alone(pe)
                for j in range(2):
                    mm = pe.transpose(PS[:, 4, SLOTS * j:SLOTS * j + SLOTS], hid[:, i % 2, P * j:P * j + P], t.ident[0:SLOTS, 0:SLOTS])
                mm.then_inc(ht_mm, 1)
                if not last or i + 2 < WB:
                    turn(at(it, i, 2), nx2[1], nx2[0])
                pe.wait_ge(ht_ev, n + 1)
                once_above(pe, yy_ev, at(it, i, -1))
                for j in range(2):
                    for h in range(2):
                        mm = pe.matmul(PS[64 * h:64 * h + 64, 5 + i % 2], hidT[:, i % 2, j], t.W2[:, i, j, CW * h:CW * h + CW], start=j == 0, stop=j == 1)
                mm.then_inc(yy_mm, 1)
                extra(pe, n, extra_block(i))

            turn(0, 0, 0)
            turn(1, 1, 0)
            up(0, 0, 0)
            loops(pe, body)

        @block.scalar
        def _(act):
            def evict(n, i):
                act.wait_ge(xt_mm, n + 1)
                once_above(act, h_mm, n - 1)
                act.copy(XT[:, i % 2].rearrange("p k s -> p (k s)"), PS[:, i % 2]).then_inc(xt_ev, 1)

            def silu(n, i):
                act.wait_ge(h_mm, n + 1)
                once_above(act, hid_done, n - 1)
                act.activation(sg[:, i % 2], PS[0:SLOTS, 2 + i % 2, 0:F], ACT.Silu).then_inc(silu_done, 1)

            def step(g):
                act.wait_ge(o_xt, g + 1)
                act.copy(XTo[:, :, :].rearrange("p k s -> p (k s)"), PS[:, 7]).then_inc(o_xe, 1)
                act.wait_ge(o_h, g + 1)
                act.activation(sgo[:, :], PS[0:SLOTS, 7, 0:F], ACT.Silu).then_inc(o_silu, 1)

            def body(it, i, last):
                if not last or i + 1 < WB:
                    silu(at(it, i, 1), i + 1)
                if not last or i + 2 < WB:
                    evict(at(it, i, 2), i)
                extra(act, at(it, i), step)

            evict(0, 0)
            evict(1, 1)
            silu(0, 0)
            loops(act, body)

        @block.vector
        def _(dve):
            def hidden(n, i):
                dve.wait_ge(silu_done, n + 1)
                once_above(dve, ht_mm, n - 1)
                dve.tensor_tensor(hid[:, i % 2].rearrange("r (j p) -> r p j", j=2), sg[:, i % 2].rearrange("r (p j) -> r p j", j=2),
                                  PS[SLOTS:P, 2 + i % 2, 0:F].rearrange("r (p j) -> r p j", j=2), ALU.mult).then_inc(hid_done, 1)

            def step(g):
                dve.wait_ge(o_silu, g + 1)
                dve.tensor_tensor(hido[:, :].rearrange("r (j p) -> r p j", j=2), sgo[:, :].rearrange("r (p j) -> r p j", j=2),
                                  PS[SLOTS:P, 7, 0:F].rearrange("r (p j) -> r p j", j=2), ALU.mult).then_inc(o_hid, 1)
                dve.wait_ge(o_ht, g + 1)
                dve.tensor_copy(hidTo[:, :, :].rearrange("p j s -> p (j s)"), PS[:, 7, 0:P]).then_inc(o_he, 1)
                with dve.If(g > 0):
                    dve.wait_ge(o_out, g * 32)
                    stand_alone(dve)
                dve.wait_ge(o_y, g + 1)
                dve.tensor_copy(Yo[:, :], PS[:, 7]).then_inc(o_ye, 1)

            def body(it, i, last):
                n = at(it, i)
                dve.wait_ge(ht_mm, n + 1)
                once_above(dve, yy_mm, at(it, i, -1))
                dve.tensor_copy(hidT[:, i % 2].rearrange("p j s -> p (j s)"), PS[:, 4, 0:P]).then_inc(ht_ev, 1)
                if not last or i + 1 < WB:
                    hidden(at(it, i, 1), i + 1)
                dve.wait_ge(yy_mm, n + 1)
                once_above(dve, y_out[i % 2], (it * (WB // 2) + i // 2) * 32)
                dve.tensor_copy(Y[:, i % 2], PS[:, 5 + i % 2]).then_inc(yy_ev, 1)
                extra(dve, n, step)

            hidden(0, 0)
            loops(dve, body)


def combine(nc, t):
    NB = 8
    with ExitStack() as ctx:
        sb = lambda n, s, d=F32: ctx.enter_context(nc.sbuf_tensor(n, s, d))
        sem = t.phase_semaphore
        G = sb("G", [P, NB, D])
        vec = sb("vec7", [P, 4, D])
        ln = layer_norm_state(t, sb, sem, "_7")
        row_in = [sem(f"row_in{i}") for i in range(NB)]
        vec_in, row_used, y_done, fin_out = sem("vec7_in"), sem("row_used"), sem("y_done"), sem("fin_out")
        dve_step = sem("comb_dve")
        block = ctx.enter_context(nc.Block())

        @block.gpsimd
        def _(pool):
            for n in range(NT):
                for k in range(TOPK):
                    j = TOPK * n + k
                    if j >= NB:
                        pool.wait_ge(row_used, j - NB + 1)
                    pool.indirect_dma_start(G[:, j % NB], None, t.y_dram, bass.IndirectOffsetOnAxis(ap=t.rows[:, n, k:k + 1], axis=0)).then_inc(row_in[j % NB], 16)
                if n:
                    rsqrts(pool, ln, n - 1)
            rsqrts(pool, ln, NT - 1)

        @block.sync
        def _(sp):
            t.load_mod(sp, vec, 5, vec_in)
            sp.dma_start(vec[:, 2], t.ln2_g.to_broadcast([P, D])).then_inc(vec_in, 16)
            sp.dma_start(vec[:, 3], t.ln2_b.to_broadcast([P, D])).then_inc(vec_in, 16)
            for n in range(NT):
                sp.wait_ge(y_done, n + 1)
                dst = t.yp[P * n:P * n + P] if n < 2 else t.ys
                sp.dma_start(dst, t.acc[:, n]).then_inc(fin_out, 16)
            sp.wait_ge(fin_out, 16 * NT)

        @block.vector
        def _(dve):
            link = make_link(dve, dve_step)
            for n in range(NT):
                a = t.acc[:, n]
                for k in range(TOPK):
                    j = TOPK * n + k
                    dve.wait_ge(row_in[j % NB], 16 * (j // NB + 1))
                    link(dve.scalar_tensor_tensor(a, G[:, j % NB], t.wts[:, n, k:k + 1], a, ALU.mult, ALU.add))
                    dve.sem_inc(row_used, 1)
                if n == 0:
                    dve.wait_ge(vec_in, 64)
                link(dve.tensor_tensor(a, a, vec[:, n // 2], ALU.mult))
                link(dve.scalar_tensor_tensor(a, t.X[:, n], ALPHA, a, ALU.mult, ALU.add))
                layer_norm(dve, link, ln, a, a)
                link(dve.tensor_tensor(a, a, vec[:, 2], ALU.mult))
                dve.tensor_tensor(a, a, vec[:, 3], ALU.add).then_inc(y_done, 1)


INS = ["x_prompt", "x_sample", "cache_k_diff", "cache_v_diff", "cache_k_band", "cache_v_band", "c_prompt",
       "c_sample", "w_ada", "b_ada", "w_in", "b_in", "lambda_q1", "lambda_k1", "lambda_q2", "lambda_k2",
       "subln_g", "rel_bias", "p_a", "p_b", "w_out", "ln1_g", "ln1_b", "w_router", "e_bias", "w1", "w3", "w2",
       "ws1", "ws3", "ws2", "ln2_g", "ln2_b"]
OUTS = [("y_prompt", (1, SEQ, D)), ("y_sample", (NSEQ, NF, D)),
        ("k_diff_prompt", (1, 1, SEQ, HA, 2, HD)), ("v_diff_prompt", (1, 1, SEQ, HA, 2 * HD)),
        ("k_band_prompt", (1, 1, SEQ, HB, HD)), ("v_band_prompt", (1, 1, SEQ, HB, HD)),
        ("k_diff_sample", (1, NSEQ, NF, HA, 2, HD)), ("v_diff_sample", (1, NSEQ, NF, HA, 2 * HD)),
        ("k_band_sample", (1, NSEQ, NF, HB, HD)), ("v_band_sample", (1, NSEQ, NF, HB, HD))]


class Shared:
    pass


def streaming_layer(nc, a, o):
    t = Shared()
    t.x_prompt, t.x_sample, t.c_prompt, t.c_sample = a["x_prompt"], a["x_sample"], a["c_prompt"], a["c_sample"]
    t.w_ada, t.b_ada, t.w_in, t.b_in = a["w_ada"], a["b_ada"], a["w_in"], a["b_in"]
    t.subln_g, t.rel_bias, t.p_a, t.p_b = a["subln_g"], a["rel_bias"], a["p_a"], a["p_b"]
    t.w_out, t.ln1_g, t.ln1_b, t.w_router = a["w_out"], a["ln1_g"], a["ln1_b"], a["w_router"]
    t.e_bias, t.ws1, t.ws3, t.ws2 = a["e_bias"], a["ws1"], a["ws3"], a["ws2"]
    t.ln2_g, t.ln2_b = a["ln2_g"], a["ln2_b"]
    t.lq1, t.lk1, t.lq2, t.lk2 = (a[n] for n in ("lambda_q1", "lambda_k1", "lambda_q2", "lambda_k2"))
    t.ckd = a["cache_k_diff"].rearrange("l b s h j d -> (l b) s h (j d)")
    t.cvd = a["cache_v_diff"].rearrange("l b s h d -> (l b) s h d")
    t.ckb = a["cache_k_band"].rearrange("l b s (u j) d -> (l b) s u (j d)", j=2)
    t.cvb = a["cache_v_band"].rearrange("l b s (u j) d -> (l b) s u (j d)", j=2)
    t.w1v = a["w1"].rearrange("l e (p k) n -> (l e) p k n", k=KD)
    t.w3v = a["w3"].rearrange("l e (p k) n -> (l e) p k n", k=KD)
    t.w2v = a["w2"].rearrange("l e (p k) n -> (l e) p k n", k=2)
    t.yp = o["y_prompt"].rearrange("b s d -> (b s) d")
    t.ys = o["y_sample"].rearrange("b s d -> (b s) d")
    t.kdp = o["k_diff_prompt"].rearrange("l b s h j d -> (l b s) (h j d)")
    t.kds = o["k_diff_sample"].rearrange("l b s h j d -> (l b s) (h j d)")
    t.vdp = o["v_diff_prompt"].rearrange("l b s h d -> (l b s) (h d)")
    t.vds = o["v_diff_sample"].rearrange("l b s h d -> (l b s) (h d)")
    t.kbp = o["k_band_prompt"].rearrange("l b s h d -> (l b s) (h d)")
    t.kbs = o["k_band_sample"].rearrange("l b s h d -> (l b s) (h d)")
    t.vbp = o["v_band_prompt"].rearrange("l b s h d -> (l b s) (h d)")
    t.vbs = o["v_band_sample"].rearrange("l b s h d -> (l b s) (h d)")
    t.mod = nc.dram_tensor("mod", (1 + NSEQ, 6 * D), F32, kind="Internal").ap()
    t.rev_dram = nc.dram_tensor("rev_table", (HB, 3 * CLIP), F32, kind="Internal").ap()
    t.h_dram = nc.dram_tensor("h_rows", (TOK, D), F32, kind="Internal").ap()
    t.y_dram = nc.dram_tensor("expert_rows", (NBLK * SLOTS, D), F32, kind="Internal").ap()

    with ExitStack() as ctx:
        t.PS = ctx.enter_context(nc.psum_tensor("PS", [P, 8, CW], F32))

        used = []

        def scoped(scope, name, shape, dtype=F32):
            used.append(name)
            return scope.enter_context(nc.sbuf_tensor(f"{name}_{len(used)}", shape, dtype))

        t.zeros = scoped(ctx, "zeros", [P, D])
        t.power = scoped(ctx, "power", [P, 2 * NSEQ])
        t.ident = scoped(ctx, "ident", [P, P])
        t.X = scoped(ctx, "X", [P, NT, D])
        t.hT = scoped(ctx, "hT", [P, KD, TOK])
        t.zeros_done = ctx.enter_context(nc.semaphore("zeros_done"))
        t.ident_done = ctx.enter_context(nc.semaphore("ident_done"))
        t.wexp_in = [ctx.enter_context(nc.semaphore(f"wexp_in{i}")) for i in range(WB)]

        t.phase_sems = []

        def phase_semaphore(name):
            t.phase_sems.append(nc.alloc_semaphore(name=name))
            return t.phase_sems[-1]

        def recycle():
            nc.clear_and_free_semaphores(t.phase_sems)
            nc.all_engine_barrier()
            t.phase_sems = []
        t.phase_semaphore = phase_semaphore

        def build_identity(pool):
            pool.memset(t.power[:, :], -0.5)
            pool.memset(t.zeros[:, :], 0.0).then_inc(t.zeros_done, 1)
            pool.memset(t.ident[:, :], 0.0).then_inc(t.ident_done, 1)
            pool.wait_ge(t.ident_done, 1)
            pool.affine_select(out=t.ident[:, :], in_=t.ident[:, :], compare_op=ALU.not_equal, fill=1.0, base=0,
                               pattern=[[-1, P]], channel_multiplier=1).then_inc(t.ident_done, 1)
        t.build_identity = build_identity

        def load_mod(sp, dst, part, s):
            cols = slice(D * part, D * part + D)
            sp.dma_start(dst[:, 0], t.mod[0:1, cols].to_broadcast([P, D])).then_inc(s, 16)
            sp.dma_start(dst[:, 1], bass.AP(t.mod.tensor, 6 * D + D * part, [[6 * D, NSEQ], [0, NF], [1, D]])).then_inc(s, 16)
        t.load_mod = load_mod

        with ExitStack() as mixer:
            t.uT = scoped(mixer, "uT", [P, KD, TOK])
            t.oaT = scoped(mixer, "oaT", [P, HA, TOK])
            t.obT = scoped(mixer, "obT", [P, 4, TOK])
            with ExitStack() as scope:
                t.W = scoped(scope, "W", [P, 2, KD, CW])
                conditioning(nc, t)
            with ExitStack() as attention:
                t.qT = scoped(attention, "qT", [P, NU, TOK])
                t.kT = scoped(attention, "kT", [P, NU, TOK])
                t.V = scoped(attention, "V", [P, NT, DA + DB])
                with ExitStack() as scope:
                    t.W = scoped(scope, "W", [P, 2, KD, CW])
                    projection_in(nc, t)
                t.alibi_p = scoped(attention, "alibi_p", [P, HA, 256])
                t.band_p = scoped(attention, "band_p", [P, HB, 256])
                t.sbias = scoped(attention, "sbias", [P, 3, PAST + NF])
                t.sub_g = scoped(attention, "sub_g", [P, 2 * HD])
                t.neg_lam = scoped(attention, "neg_lam", [P, 1])
                t.join = scoped(attention, "join", [P, 64])
                attention_constants(nc, t)
                attention_prompt(nc, t)
                attention_sample(nc, t)
            recycle()
            projection_out(nc, t)
        t.acc = scoped(ctx, "acc", [P, NT, D])
        t.wts = scoped(ctx, "wts", [P, NT, TOPK])
        t.rows = scoped(ctx, "rows", [P, NT, TOPK], I32)
        t.tokens = scoped(ctx, "tokens", [SLOTS, NBLK], I32)
        t.ov = scoped(ctx, "ov", [1, E + 1], I32)
        with ExitStack() as scope:
            t.W13 = scoped(scope, "W13", [P, WB, 2, KD, F])
            t.W2 = scoped(scope, "W2", [P, WB, 2, D])
            routing(nc, t)
            experts(nc, t)
        combine(nc, t)


def kernel(**inputs):
    import concourse.bacc as bacc
    from concourse.bass_utils import run_bass_kernel_spmd

    nc = bacc.Bacc("TRN2", target_bir_lowering=False, num_devices=1)
    arrays, a, o = {}, {}, {}
    for name in INS:
        x = np.ascontiguousarray(inputs[name])
        arrays[name] = x
        a[name] = nc.dram_tensor(name, x.shape, mybir.dt.from_np(x.dtype), kind="ExternalInput").ap()
    for name, shape in OUTS:
        o[name] = nc.dram_tensor(name, shape, F32, kind="ExternalOutput").ap()
    streaming_layer(nc, a, o)
    r = run_bass_kernel_spmd(nc, [arrays], core_ids=[0])
    return tuple(r.results[0][name] for name, _ in OUTS)
```

```python
from contextlib import ExitStack

import concourse.bass as bass
import concourse.mybir as mybir
import numpy as np

ALU = mybir.AluOpType
ACT = mybir.ActivationFunctionType
AX = mybir.AxisListType
F32 = mybir.dt.float32
F16 = mybir.dt.float16
I32 = mybir.dt.int32
U32 = mybir.dt.uint32

P = 128
D = 1024
KD = D // P
SEQ, NSEQ, NF, PAST = 256, 8, 16, 128
NC = 1 + NSEQ
NT = 3
TOK = NT * P
CHUNK = 64
HD = 64
HA = HB = 8
DA, DB = HA * 2 * HD, HB * HD
NU = 12
CLIP = 128
N_IN = 3 * DA + 3 * DB + 2 * D
CW = 512
E, TOPK, NG, TOPG, F = 64, 8, 8, 4, 256
SLOTS = 64
XB = (TOK * TOPK - 1) // SLOTS
NBLK = E + XB
ROUTED_SCALE = 2.5
ALPHA = 2.0 ** 0.25
LAM_INIT = 0.2
EPS = 1e-5
SM = HD ** -0.5
WB = 4
QC = {0: 0, 1: 4, 6: 8}
KC = {2: 0, 3: 512, 7: 1024}
VC = {4: 0, 5: 512, 8: 1024}
GC = (9, 10, 11, 12)


def layer_norm(dve, link, ln, out, x):
    stats, mv, rstd = ln.stats, ln.mv, ln.rstd
    for i in range(2):
        link(dve.bn_stats(stats[:, 6 * i:6 * i + 6], x[:, CW * i:CW * i + CW]))
    link(dve.bn_aggr(mv[:, :], stats[:, :]))
    dve.tensor_scalar(mv[:, 1:2], mv[:, 1:2], EPS, None, ALU.add).then_inc(ln.var_done, 1)
    ln.count += 1
    dve.wait_ge(ln.rstd_done, ln.count)
    link(dve.tensor_scalar(out, x, mv[:, 0:1], rstd[:, 0:1], ALU.subtract, ALU.mult))


def layer_norm_state(t, sb, sem, tag):
    ln = Shared()
    ln.stats, ln.mv, ln.rstd = sb("stats" + tag, [P, 12]), sb("mv" + tag, [P, 2]), sb("rstd" + tag, [P, 1])
    ln.power, ln.count = t.power, 0
    ln.var_done, ln.rstd_done = sem("var_done" + tag), sem("rstd_done" + tag)
    return ln


def rsqrts(pool, ln, *norms):
    for n in norms:
        pool.wait_ge(ln.var_done, n + 1)
        pool.tensor_tensor(ln.rstd[:, :], ln.mv[:, 1:2], ln.power[:, 0:1], ALU.pow).then_inc(ln.rstd_done, 1)


def make_link(eng, sem):
    count = [0]

    def link(ins):
        count[0] += 1
        ins.then_inc(sem, 1)
        eng.wait_ge(sem, count[0])
    return link


def conditioning(nc, t):
    PS = t.PS
    with ExitStack() as ctx:
        sb = lambda n, s, d=F32: ctx.enter_context(nc.sbuf_tensor(n, s, d))
        sem = t.phase_semaphore
        NA = 2 * D // CW
        c_rows = sb("c_rows", [NC, D])
        cT = t.cT
        b_q = sb("b_q", [P, NA, P])
        mod_q = sb("mod_q", [P, NA, P])
        shift = sb("shift", [P, 2, D])
        scale = sb("scale", [P, 2, D])
        u = sb("u", [P, NT, D])
        ln = layer_norm_state(t, sb, sem, "_1")
        c_in, x_in, bada_in = sem("c_in"), sem("x_in"), sem("bada_in")
        ada_in = [sem(f"ada_in{i}") for i in range(2)]
        silu_done, ct_mm, ct_zero, ct_done = sem("silu_done"), sem("ct_mm"), sem("ct_zero"), sem("ct_done")
        ada_mm, ada_ev, mod_out, mod_back = sem("ada_mm"), sem("ada_ev"), sem("mod_out"), sem("mod_back")
        u_done, ut_mm, ut_ev = sem("u_done"), sem("ut_mm"), sem("ut_ev")
        dve_step = sem("cond_dve")
        block = ctx.enter_context(nc.Block())

        @block.sync
        def _(sp):
            sp.dma_start(c_rows[0:1, :], t.c_prompt).then_inc(c_in, 16)
            sp.dma_start(c_rows[1:NC, :], t.c_sample).then_inc(c_in, 16)
            for j in range(4):
                src = t.b_ada.rearrange("l (c j n) -> l j c n", j=4, n=P)[:, j, 0:NA]
                sp.dma_start(b_q[32 * j:32 * j + 32], src.to_broadcast([32, NA, P])).then_inc(bada_in, 16)
            for i in range(NA):
                if i >= 2:
                    sp.wait_ge(ada_mm, i - 1)
                sp.dma_start(t.W[:, i % 2], t.w_ada[0].rearrange("(k p) n -> p k n", p=P)[:, :, CW * i:CW * i + CW]).then_inc(ada_in[i % 2], 16)
                if i == 1:
                    for n in range(2):
                        sp.dma_start(t.X[:, n], t.x_prompt[0, P * n:P * n + P]).then_inc(x_in, 16)
                    sp.dma_start(t.X[:, 2], t.x_sample.rearrange("b s d -> (b s) d")).then_inc(x_in, 16)
            sp.wait_ge(ada_ev, NA)
            for j in range(4):
                dst = t.mod.rearrange("r (c j n) -> r j c n", j=4, n=P)[:, j, 0:NA]
                sp.dma_start(dst, mod_q[32 * j:32 * j + NC]).then_inc(mod_out, 16)
            sp.wait_ge(mod_out, 64)
            t.load_mod(sp, shift, 0, mod_back)
            t.load_mod(sp, scale, 1, mod_back)
            for c in range(2):
                sp.dma_start(t.W[:, c], t.w_in[0].rearrange("(k p) n -> p k n", p=P)[:, :, CW * c:CW * c + CW]).then_inc(t.win_in[c], 16)

        @block.scalar
        def _(act):
            act.wait_ge(c_in, 32)
            act.activation(c_rows[:, :], c_rows[:, :], ACT.Silu).then_inc(silu_done, 1)
            for n in range(6):
                act.wait_ge(ut_mm, n + 1)
                tile, half = n // 2, n % 2
                act.copy(t.uT[:, 4 * half:4 * half + 4, P * tile:P * tile + P],
                         PS[:, 2 + n % 2].rearrange("p (k q) -> p k q", k=4)).then_inc(ut_ev, 1)

        @block.vector
        def _(dve):
            link = make_link(dve, dve_step)
            dve.memset(cT[:, :, :], 0.0).then_inc(ct_zero, 1)
            dve.wait_ge(ct_zero, 1)
            dve.wait_ge(ct_mm, 1)
            dve.tensor_copy(cT[:, :, 0:NC], PS[:, 0, 0:KD * NC].rearrange("p (k r) -> p k r", k=KD)).then_inc(ct_done, 1)
            dve.wait_ge(x_in, 48)
            for n in range(NT):
                layer_norm(dve, link, ln, u[:, n], t.X[:, n])
            dve.wait_ge(bada_in, 64)
            for i in range(NA):
                dve.wait_ge(ada_mm, i + 1)
                dve.tensor_tensor(mod_q[:, i], PS[:, i % 2, 0:P], b_q[:, i], ALU.add).then_inc(ada_ev, 1)
            dve.wait_ge(mod_back, 64)
            for n in range(NT):
                g = n // 2
                link(dve.scalar_tensor_tensor(u[:, n], scale[:, g], 1.0, u[:, n], ALU.add, ALU.mult))
                dve.tensor_tensor(u[:, n], u[:, n], shift[:, g], ALU.add).then_inc(u_done, 1)

        @block.gpsimd
        def _(pool):
            t.build_identity(pool)
            rsqrts(pool, ln, *range(NT))

        @block.tensor
        def _(pe):
            pe.wait_ge(t.ident_done, 2)
            pe.wait_ge(silu_done, 1)
            for k in range(KD):
                mm = pe.transpose(PS[:, 0, NC * k:NC * k + NC], c_rows[:, P * k:P * k + P], t.ident[0:NC, 0:NC])
            mm.then_inc(ct_mm, 1)
            pe.wait_ge(ct_done, 1)
            for i in range(NA):
                pe.wait_ge(ada_in[i % 2], 16 * (i // 2 + 1))
                if i >= 2:
                    pe.wait_ge(ada_ev, i - 1)
                for k in range(KD):
                    for j in range(4):
                        mm = pe.matmul(PS[32 * j:32 * j + 32, i % 2, 0:P], cT[:, k], t.W[:, i % 2, k, P * j:P * j + P],
                                       start=k == 0, stop=k == KD - 1)
                mm.then_inc(ada_mm, 1)
            for n in range(6):
                tile, half = n // 2, n % 2
                pe.wait_ge(u_done, tile + 1)
                if n >= 2:
                    pe.wait_ge(ut_ev, n - 1)
                for k in range(4):
                    mm = pe.transpose(PS[:, 2 + n % 2, P * k:P * k + P], u[:, tile, P * (4 * half + k):P * (4 * half + k) + P], t.ident[:, :])
                mm.then_inc(ut_mm, 1)


def projection_in(nc, t):
    PS = t.PS
    with ExitStack() as ctx:
        sb = lambda n, s, d=F32: ctx.enter_context(nc.sbuf_tensor(n, s, d))
        sem = t.phase_semaphore
        keys = sb("keys", [P, NT, DA + DB])
        b_col = sb("b_col", [P, NU])
        b_row = sb("b_row", [P, 2, CW])
        gate = sb("gate", [P, 2, CW])
        win_in = t.win_in
        wada = (t.oaT[:, :, :].rearrange("p k q -> p (k q)").rearrange("p (k n) -> p k n", n=CW),
                t.obT[:, :, :].rearrange("p k q -> p (k q)")[:, 0:2 * CW].rearrange("p (k n) -> p k n", n=CW))
        b_q = sb("b_q2", [P, 2, P])
        mod_q = sb("mod_q2", [P, 2, P])
        A0, NA = 2 * D // CW, 4 * D // CW
        ada_in, ada_mm, ada_ev = sem("ada2_in"), sem("ada2_mm"), sem("ada2_ev")
        mod_out = [sem(f"mod2_out{i}") for i in range(2)]
        brow_in = [sem(f"brow_in{i}") for i in range(2)]
        bin_in, rows_zero = sem("bin_in"), sem("rows_zero")
        g_add, g_sig = sem("g_add"), sem("g_sig")
        g_out = [sem(f"g_out{i}") for i in range(2)]
        z_mm, z_ev_act, z_ev_dve = sem("z_mm"), sem("z_ev_act"), sem("z_ev_dve")
        kt_mm, kt_ev, kv_out = sem("kt_mm"), sem("kt_ev"), sem("kv_out")
        NCH = N_IN // CW
        RC = [c for c in range(NCH) if c not in QC]
        constants = attention_constants(nc, t, sb, keys)
        jobs = [(c, i) for c in range(NCH) for i in range(4 if c in QC else NT)]
        act_jobs = [n for n, (c, _) in enumerate(jobs) if c in QC]
        dve_jobs = [n for n, (c, _) in enumerate(jobs) if c not in QC]
        block = ctx.enter_context(nc.Block())

        @block.sync
        def _(sp):
            with nc.allow_non_contiguous_dma(reason="128 x 12 bias values, one column each"):
                for u0, c0, n in ((0, 0, 8), (8, 3 * DA, 4)):
                    sp.dma_start(b_col[:, u0:u0 + n], t.b_in[0, c0:c0 + P * n].rearrange("(u p) -> p u", p=P)).then_inc(bin_in, 16)
            for c in range(NCH):
                if c >= 2:
                    sp.wait_ge(z_mm, 1 + max(n for n, j in enumerate(jobs) if j[0] == c - 2))
                    sp.dma_start(t.W[:, c % 2], t.w_in[0].rearrange("(k p) n -> p k n", p=P)[:, :, CW * c:CW * c + CW]).then_inc(win_in[c % 2], 16)
                if c not in QC:
                    b = RC.index(c)
                    if b >= 2:
                        sp.wait_ge(z_ev_dve, NT * (b - 1))
                    sp.dma_start(b_row[:, b % 2], t.b_in[:, CW * c:CW * c + CW].to_broadcast([P, CW])).then_inc(brow_in[b % 2], 16)
                if c < NA:
                    if c:
                        sp.wait_ge(ada_mm, c)
                    src = t.w_ada[0].rearrange("(k p) n -> p k n", p=P)[:, :, CW * (A0 + c):CW * (A0 + c) + CW]
                    sp.dma_start(wada[0], src[:, 0:6]).then_inc(ada_in, 16)
                    sp.dma_start(wada[1], src[:, 6:8]).then_inc(ada_in, 16)
                    for j in range(4):
                        sp.dma_start(b_q[32 * j:32 * j + 32, c % 2], t.b_ada[:, CW * (A0 + c) + P * j:CW * (A0 + c) + P * j + P].to_broadcast([32, P])).then_inc(ada_in, 16)
                if c == 0:
                    constants.sync(sp)

        @block.gpsimd
        def _(pool):
            constants.gpsimd(pool)
            pool.wait_ge(t.zeros_done, 1)
            for n in range(E * SLOTS, NBLK * SLOTS, P):
                r = min(P, NBLK * SLOTS - n)
                pool.dma_start(t.y_dram[n:n + r], t.zeros[0:r, :]).then_inc(rows_zero, 16)
            stores = 0
            groups = {3: (DA, 0, (t.kdp, t.kds), keys), 5: (DA, 0, (t.vdp, t.vds), t.V),
                      7: (DB, DA, (t.kbp, t.kbs), keys), 8: (DB, DA, (t.vbp, t.vbs), t.V)}
            for c in range(NCH):
                if c in groups:
                    width, c0, outs, src = groups[c]
                    pool.wait_ge(z_ev_dve, 1 + max(i for i, n in enumerate(dve_jobs) if jobs[n][0] == c))
                    for n in range(2):
                        pool.dma_start(outs[0][P * n:P * n + P], src[:, n, c0:c0 + width]).then_inc(kv_out, 16)
                    pool.dma_start(outs[1], src[:, 2, c0:c0 + width]).then_inc(kv_out, 16)
                    stores += 3
                if c < NA:
                    pool.wait_ge(ada_ev, c + 1)
                    for j in range(4):
                        n0 = CW * (A0 + c) + P * j
                        pool.dma_start(t.mod[:, n0:n0 + P], mod_q[32 * j:32 * j + NC, c % 2]).then_inc(mod_out[c % 2], 16)
            for i in range(2):
                pool.wait_ge(mod_out[i], 64 * (NA // 2))
            pool.wait_ge(kv_out, 16 * stores)
            pool.wait_ge(rows_zero, 16 * -(-(XB * SLOTS) // P))

        @block.tensor
        def _(pe):
            def transpose_keys(c):
                for i in range(NT):
                    n = 3 * [2, 3, 7].index(c) + i
                    pe.wait_ge(z_ev_dve, 1 + dve_jobs.index(jobs.index((c, i))))
                    if n >= 2:
                        pe.wait_ge(kt_ev, n - 1)
                    for m in range(4):
                        mm = pe.transpose(PS[:, 6 + n % 2, P * m:P * m + P], keys[:, i, KC[c] + P * m:KC[c] + P * m + P], t.ident[:, :])
                    mm.then_inc(kt_mm, 1)

            for n, (c, i) in enumerate(jobs):
                if i == 0:
                    pe.wait_ge(win_in[c % 2], 16 * (c // 2 + 1))
                if n >= 5:
                    o = n - 5
                    if o in act_jobs:
                        pe.wait_ge(z_ev_act, act_jobs.index(o) + 1)
                    else:
                        pe.wait_ge(z_ev_dve, dve_jobs.index(o) + 1)
                for k in range(KD):
                    if c in QC:
                        mm = pe.matmul(PS[:, n % 5, 0:TOK], t.W[:, c % 2, k, P * i:P * i + P], t.uT[:, k], start=k == 0, stop=k == KD - 1)
                    else:
                        mm = pe.matmul(PS[:, n % 5], t.uT[:, k, P * i:P * i + P], t.W[:, c % 2, k], start=k == 0, stop=k == KD - 1)
                mm.then_inc(z_mm, 1)
                if (c, i) == (1, 3):
                    constants.tensor(pe)
                if i == (3 if c in QC else NT - 1):
                    if c - 1 in KC:
                        transpose_keys(c - 1)
                    if c < NA:
                        pe.wait_ge(ada_in, 96 * (c + 1))
                        if c:
                            pe.wait_ge(ada_ev, c)
                        for k in range(KD):
                            w = wada[0][:, k] if k < 6 else wada[1][:, k - 6]
                            for m in range(4):
                                mm = pe.matmul(PS[32 * m:32 * m + 32, 5, 0:P], t.cT[:, k], w[:, P * m:P * m + P], start=k == 0, stop=k == KD - 1)
                        mm.then_inc(ada_mm, 1)

        @block.scalar
        def _(act):
            constants.scalar(act)
            act.wait_ge(bin_in, 32)
            k_done = [0]

            def turn_keys(c):
                for i in range(NT):
                    k_done[0] += 1
                    act.wait_ge(kt_mm, k_done[0])
                    u0 = KC[c] // P
                    act.copy(t.kT[:, u0:u0 + 4, P * i:P * i + P],
                             PS[:, 6 + (k_done[0] - 1) % 2].rearrange("p (u q) -> p u q", u=4)).then_inc(kt_ev, 1)

            for n, (c, i) in enumerate(jobs):
                if c in QC:
                    act.wait_ge(z_mm, n + 1)
                    u = QC[c] + i
                    act.activation(t.qT[:, u], PS[:, n % 5, 0:TOK], ACT.Identity, bias=b_col[:, u:u + 1]).then_inc(z_ev_act, 1)
                if c in GC:
                    m = NT * (c - GC[0]) + i
                    act.wait_ge(g_add, m + 1)
                    act.activation(gate[:, m % 2], gate[:, m % 2], ACT.Sigmoid).then_inc(g_sig, 1)
                    act.wait_ge(g_sig, m + 1)
                    act.dma_start(t.gates[c - GC[0], P * i:P * i + P], gate[:, m % 2]).then_inc(g_out[m % 2], 16)
                if i == (3 if c in QC else NT - 1) and c - 1 in KC:
                    turn_keys(c - 1)
            for i in range(2):
                act.wait_ge(g_out[i], 16 * NT * len(GC) // 2)

        @block.vector
        def _(dve):
            def finish_chunk(c):
                if c < NA:
                    dve.wait_ge(ada_mm, c + 1)
                    if c >= 2:
                        dve.wait_ge(mod_out[c % 2], 64 * (c // 2))
                    dve.tensor_tensor(mod_q[:, c % 2], PS[:, 5, 0:P], b_q[:, c % 2], ALU.add).then_inc(ada_ev, 1)

            constants.vector(dve)
            for n, (c, i) in enumerate(jobs):
                if i == 0 and c:
                    finish_chunk(c - 1)
                if c in QC:
                    continue
                dve.wait_ge(z_mm, n + 1)
                b = RC.index(c)
                dve.wait_ge(brow_in[b % 2], 16 * (b // 2 + 1))
                if c in GC:
                    m = NT * (c - GC[0]) + i
                    if m >= 2:
                        dve.wait_ge(g_out[m % 2], 16 * (m // 2))
                    dve.tensor_tensor(gate[:, m % 2], PS[:, n % 5], b_row[:, b % 2], ALU.add).then_inc(g_add, 1)
                    dve.wait_ge(g_add, m + 1)
                    dve.sem_inc(z_ev_dve, 1)
                    continue
                dst = keys[:, i, KC[c]:KC[c] + CW] if c in KC else t.V[:, i, VC[c]:VC[c] + CW]
                dve.tensor_tensor(dst, PS[:, n % 5], b_row[:, b % 2], ALU.add).then_inc(z_ev_dve, 1)


def attention_constants(nc, t, sb, keys):
    sem = t.phase_semaphore
    NR = 3 * CLIP
    table = sb("table", [HB, 2 * CLIP + 1])
    rev = sb("rev", [HB, NR])
    di = sb("di", [P, 256], I32)
    df = sb("df", [P, 256])
    xi = sb("xi", [P, PAST + NF], I32)
    xf = sb("xf", [P, PAST + NF])
    xn = sb("xn", [P, PAST + NF])
    qi = sb("qi", [P, 1], I32)
    qf = sb("qf", [P, 1])
    slope = sb("slope", [P, 2])
    lamv = sb("lamv", [P, 4, HD])
    lamp = sb("lamp", [P, 2, HD])
    lamd = sb("lamd", [P, 2])
    lame = sb("lame", [P, 2])
    fall_p = keys[:, :, :].rearrange("p n d -> p (n d)")[:, 0:HB * 256].rearrange("p (h x) -> p h x", h=HB)
    fall_s = sb("fall_s", [P, PAST + NF])
    flip, flip16 = sb("flip", [P, P]), sb("flip16", [P, P])
    flip_done, flip_mm, flip_ev = sem("flip_done"), sem("flip_mm"), sem("flip_ev")
    PS = t.PS
    table_in, rev_done, rev_out, band_in = sem("table_in"), sem("rev_done"), sem("rev_out"), sem("band_in")
    lam_in, g_in, iota_done, lamd_done, lame_done = sem("lam_in"), sem("g_in"), sem("iota_done"), sem("lamd_done"), sem("lame_done")
    dve_step = sem("const_dve")

    def sync(sp):
        sp.dma_start(table[:, :], t.rel_bias[0]).then_inc(table_in, 16)
        for i, v in enumerate((t.lq1, t.lk1, t.lq2, t.lk2)):
            sp.dma_start(lamv[:, i], v.to_broadcast([P, HD])).then_inc(lam_in, 16)
        sp.dma_start(t.sub_g[:, :], t.subln_g.to_broadcast([P, 2 * HD])).then_inc(g_in, 16)
        sp.wait_ge(rev_done, 1)
        sp.dma_start(t.rev_dram, rev[:, :]).then_inc(rev_out, 16)
        sp.wait_ge(rev_out, 16)
        h = t.rev_dram.tensor
        sp.dma_start(fall_p[:, :, :], bass.AP(h, 0, [[1, P], [NR, HB], [1, 256]])).then_inc(band_in, 16)
        sp.dma_start(fall_s[:, :], bass.AP(h, P - NF, [[NR, HB], [1, NF], [1, PAST + NF]])).then_inc(band_in, 16)

    def gpsimd(pool):
        pool.iota(di[:, :], pattern=[[-1, 256]], base=PAST, channel_multiplier=1).then_inc(iota_done, 1)
        pool.iota(xi[:, :], pattern=[[-1, PAST + NF]], base=PAST, channel_multiplier=0).then_inc(iota_done, 1)
        pool.iota(qi[:, :], pattern=[[0, 1]], base=0, channel_multiplier=1).then_inc(iota_done, 1)

    def tensor(pe):
        pe.wait_ge(flip_done, 1)
        pe.wait_ge(band_in, 32)
        for n in range(5):
            if n >= 2:
                pe.wait_ge(flip_ev, n - 1)
            if n < 4:
                pe.matmul(PS[:, 6 + n % 2], flip[:, :], fall_p[:, 2 * n:2 * n + 2].rearrange("p h x -> p (h x)"),
                          start=True, stop=True).then_inc(flip_mm, 1)
            else:
                pe.matmul(PS[:, 6, 0:PAST + NF], flip16[:, :], fall_s[:, :], start=True, stop=True).then_inc(flip_mm, 1)
        pe.wait_ge(flip_ev, 5)

    def scalar(act):
        act.wait_ge(lamd_done, 1)
        act.activation(lame[:, :], lamd[:, :], ACT.Exp).then_inc(lame_done, 1)

    def vector(dve):
        link = make_link(dve, dve_step)
        dve.wait_ge(lam_in, 64)
        for i in range(2):
            link(dve.tensor_tensor(lamp[:, i], lamv[:, 2 * i], lamv[:, 2 * i + 1], ALU.mult))
        dve.tensor_reduce(lamd[:, :], lamp[:, :, :], AX.X, ALU.add).then_inc(lamd_done, 1)
        dve.wait_ge(table_in, 16)
        dve.tensor_copy(rev[:, 0:P - 1], table[:, 2 * CLIP:2 * CLIP + 1].to_broadcast([HB, P - 1]))
        dve.tensor_copy(rev[:, P - 1:NR], table[:, ::-1]).then_inc(rev_done, 1)
        dve.tensor_copy(flip[:, :], t.ident[:, ::-1])
        dve.tensor_copy(flip16[:, :].rearrange("p (h q) -> p h q", q=NF),
                        t.ident[:, :].rearrange("p (h q) -> p h q", q=NF)[:, :, ::-1]).then_inc(flip_done, 1)
        dve.wait_ge(iota_done, 3)
        link(dve.tensor_copy(df[:, :], di[:, :]))
        link(dve.scalar_tensor_tensor(df[:, :], df[:, :], -1.0, df[:, :], ALU.mult, ALU.max))
        link(dve.tensor_scalar(df[0:CHUNK, 192:256], df[0:CHUNK, 192:256], 1e9, None, ALU.add))
        for h in range(HA):
            dve.tensor_scalar(t.alibi_p[:, h], df[:, :], -2.0 ** -(h + 1), None, ALU.mult)
        link(dve.tensor_scalar(qi[:, :], qi[:, :], NF - 1, None, ALU.bitwise_and))
        link(dve.tensor_copy(qf[:, :], qi[:, :]))
        link(dve.tensor_copy(xf[:, :], xi[:, :]))
        link(dve.tensor_scalar(xf[:, :], xf[:, :], qf[:, 0:1], None, ALU.add))
        link(dve.scalar_tensor_tensor(xn[:, :], xf[:, :], -1.0, xf[:, :], ALU.mult, ALU.max))
        for g in range(2):
            for i in range(4):
                link(dve.memset(slope[32 * i:32 * i + 32, g:g + 1], -2.0 ** -(4 * g + i + 1)))
        for g in range(2):
            dve.tensor_scalar(t.sbias[:, g], xn[:, :], slope[:, g:g + 1], None, ALU.mult)
        dve.wait_ge(lame_done, 1)
        link(dve.tensor_tensor(t.neg_lam[:, :], lame[:, 1:2], lame[:, 0:1], ALU.subtract))
        link(dve.tensor_scalar(t.neg_lam[:, :], t.neg_lam[:, :], -LAM_INIT, None, ALU.add))
        idv = t.ident[:, :].rearrange("p (i j q) -> p i j q", i=4, j=2)
        dve.scalar_tensor_tensor(t.join[:, :].rearrange("p (i q) -> p i q", i=4), idv[:, :, 1], t.neg_lam[:, 0:1],
                                 idv[:, :, 0], ALU.mult, ALU.add)
        dve.wait_ge(g_in, 16)
        dve.tensor_scalar(t.sub_g[:, :], t.sub_g[:, :], 1.0 - LAM_INIT, None, ALU.mult)
        for n in range(5):
            dve.wait_ge(flip_mm, n + 1)
            if n < 4:
                ins = dve.tensor_copy(t.band_p[:, 2 * n:2 * n + 2].rearrange("p h x -> p (h x)"), PS[:, 6 + n % 2])
            else:
                ins = dve.tensor_copy(t.sbias[:, 2], PS[:, 6, 0:PAST + NF])
            ins.then_inc(flip_ev, 1)
        dve.wait_ge(flip_ev, 5)
        dve.memset(t.band_p[0:CHUNK, :, 192:256], -1e30)

    part = Shared()
    part.sync, part.gpsimd, part.tensor, part.scalar, part.vector = sync, gpsimd, tensor, scalar, vector
    return part


def attention_prompt(nc, t):
    PS = t.PS
    GR = [(tile, g) for tile in range(2) for g in range(6)]
    with ExitStack() as ctx:
        sb = lambda n, s, d=F32: ctx.enter_context(nc.sbuf_tensor(n, s, d))
        sem = t.phase_semaphore
        L = sb("L", [P, 2, 2, 2, 256])
        mx = sb("mx", [P, 2, 4])
        lsum = sb("lsum", [P, 2, 4])
        A = sb("A", [P, 2, 4, 256])
        AT = sb("AT", [P, 2, 8, P])
        O = sb("O", [P, 2, DA])
        OBt = sb("OBt", [P, 2, DB])
        sq = sb("sq", [P, DA])
        ss = sb("ss", [P, HA])
        sc_mm, lg_done, exp_done, a_done = sem("sc_mm"), sem("lg_done"), sem("exp_done"), sem("a_done")
        at_mm, at_ev, pv_mm, o_done, o_norm, ot_mm, ot_ev = (sem(x) for x in
            ("at_mm", "at_ev", "pv_mm", "o_done", "o_norm", "ot_mm", "ot_ev"))
        dve_step = sem("prompt_dve")
        ms_done, rms_done = sem("ms_done"), sem("rms_done")
        block = ctx.enter_context(nc.Block())

        def heads(g, j, hh):
            return (slice(64 * j, 64 * j + 64), 2 * g + hh)


        @block.gpsimd
        def _(pool):
            for tile in range(2):
                pool.wait_ge(ms_done, tile + 1)
                pool.tensor_tensor(ss[:, :], ss[:, :], t.power[:, 0:HA], ALU.pow).then_inc(rms_done, 1)

        nmat = lambda tile, g: (2 if g < 4 else 4) * (tile + 1)

        @block.tensor
        def _(pe):
            def scores(n):
                tile, g = GR[n]
                S = P * (tile + 1)
                if n >= 2:
                    pe.wait_ge(lg_done, n - 1)
                for hh in range(2):
                    for j in range(2):
                        rows, u = heads(g, j, hh)
                        mm = pe.matmul(PS[:, 6 * (n % 2) + j, 256 * hh:256 * hh + S], t.qT[rows, u, P * tile:P * tile + P],
                                       t.kT[rows, u, 0:S], start=True, stop=True)
                mm.then_inc(sc_mm, 1)

            def turn(n):
                tile, g = GR[n]
                pe.wait_ge(a_done, n + 1)
                if n >= 1:
                    pe.wait_ge(at_ev, n)
                for m in range(nmat(tile, g)):
                    hd, st = m // (tile + 1), m % (tile + 1)
                    mm = pe.transpose(PS[:, 2 + m // 4, P * (m % 4):P * (m % 4) + P], A[:, n % 2, hd, P * st:P * st + P], t.ident[:, :])
                mm.then_inc(at_mm, 1)

            def values(n):
                tile, g = GR[n]
                pe.wait_ge(at_ev, n + 1)
                if n >= 1:
                    pe.wait_ge(o_done, n)
                for hd in range(2 if g < 4 else 4):
                    for st in range(tile + 1):
                        if g < 4:
                            v = t.V[:, st, P * (2 * g + hd):P * (2 * g + hd) + P]
                            o = PS[:, 4, P * hd:P * hd + P]
                        else:
                            h = 4 * (g - 4) + hd
                            v = t.V[:, st, DA + HD * h:DA + HD * h + HD]
                            o = PS[:, 4, HD * hd:HD * hd + HD]
                        mm = pe.matmul(o, AT[:, n % 2, hd * (tile + 1) + st], v, start=st == 0, stop=st == tile)
                mm.then_inc(pv_mm, 1)

            def turn_out(tile):
                pe.wait_ge(o_norm, tile + 1)
                for b in range(3):
                    n = 3 * tile + b
                    if n >= 1:
                        pe.wait_ge(ot_ev, n)
                    for m in range(4):
                        src = O[:, tile, P * (4 * b + m):P * (4 * b + m) + P] if b < 2 else OBt[:, tile, P * m:P * m + P]
                        mm = pe.transpose(PS[:, 5, P * m:P * m + P], src, t.ident[:, :])
                    mm.then_inc(ot_mm, 1)

            scores(0)
            for n in range(len(GR) + 2):
                if n + 1 < len(GR):
                    scores(n + 1)
                if 1 <= n <= len(GR):
                    turn(n - 1)
                if n >= 2:
                    values(n - 2)
                if n == 9:
                    turn_out(0)
            turn_out(1)

        @block.vector
        def _(dve):
            link = make_link(dve, dve_step)

            def logits(n):
                tile, g = GR[n]
                S, x0 = P * (tile + 1), P * (1 - tile)
                dve.wait_ge(sc_mm, n + 1)
                if n >= 2:
                    dve.wait_ge(a_done, n - 1)
                for j in range(2):
                    bias = t.alibi_p[:, 2 * g:2 * g + 2, x0:256] if g < 4 else \
                        t.band_p[:, :, x0:256].rearrange("p (u j) x -> p u j x", j=2)[:, 2 * (g - 4):2 * (g - 4) + 2, j]
                    ins = dve.scalar_tensor_tensor(L[:, n % 2, j, :, 0:S], PS[:, 6 * (n % 2) + j].rearrange("p (h x) -> p h x", h=2)[:, :, 0:S],
                                                   SM, bias, ALU.mult, ALU.add)
                    link(ins)
                link(dve.tensor_reduce(mx[:, n % 2], L[:, n % 2, :, :, 0:S], AX.X, ALU.max))
                dve.tensor_scalar(mx[:, n % 2], mx[:, n % 2], -1.0, None, ALU.mult).then_inc(lg_done, 1)

            def weights(n):
                tile, g = GR[n]
                S = P * (tile + 1)
                dve.wait_ge(exp_done, n + 1)
                link(dve.reciprocal(lsum[:, n % 2], lsum[:, n % 2]))
                if n >= 2:
                    dve.wait_ge(at_mm, n - 1)
                if g < 4:
                    link(dve.tensor_scalar(lsum[:, n % 2, 2:4], lsum[:, n % 2, 2:4], t.neg_lam[:, 0:1], None, ALU.mult))
                    for hh in range(2):
                        link(dve.tensor_scalar(A[:, n % 2, hh, 0:S], L[:, n % 2, 0, hh, 0:S], lsum[:, n % 2, hh:hh + 1], None, ALU.mult))
                        ins = dve.scalar_tensor_tensor(A[:, n % 2, hh, 0:S], L[:, n % 2, 1, hh, 0:S], lsum[:, n % 2, 2 + hh:3 + hh],
                                                       A[:, n % 2, hh, 0:S], ALU.mult, ALU.add)
                        if hh == 0:
                            link(ins)
                else:
                    for m in range(4):
                        ins = dve.tensor_scalar(A[:, n % 2, m, 0:S], L[:, n % 2, m % 2, m // 2, 0:S],
                                                lsum[:, n % 2, 2 * (m % 2) + m // 2:2 * (m % 2) + m // 2 + 1], None, ALU.mult)
                ins.then_inc(a_done, 1)

            def normalise(tile):
                dve.wait_ge(o_done, 6 * tile + 4)
                link(dve.tensor_tensor(sq[:, :], O[:, tile], O[:, tile], ALU.mult))
                link(dve.tensor_reduce(ss[:, :], sq[:, :].rearrange("p (h e) -> p h e", h=HA), AX.X, ALU.add))
                dve.tensor_scalar(ss[:, :], ss[:, :], 1.0 / P, EPS, ALU.mult, ALU.add).then_inc(ms_done, 1)
                dve.wait_ge(rms_done, tile + 1)
                o3 = O[:, tile].rearrange("p (h e) -> p h e", h=HA)
                link(dve.tensor_tensor(o3, o3, ss[:, :].unsqueeze(2).to_broadcast([P, HA, P]), ALU.mult))
                dve.wait_ge(o_done, 6 * tile + 6)
                dve.tensor_tensor(o3, o3, t.sub_g[:, :].unsqueeze(1).to_broadcast([P, HA, P]), ALU.mult).then_inc(o_norm, 1)

            for n in range(len(GR) + 1):
                if n < len(GR):
                    logits(n)
                if n >= 1:
                    weights(n - 1)
                if n == 9:
                    normalise(0)
            normalise(1)

        @block.scalar
        def _(act):
            outs = [0]

            def out_turned(tile):
                for b in range(3):
                    outs[0] += 1
                    act.wait_ge(ot_mm, outs[0])
                    dst = t.oaT[:, 4 * b:4 * b + 4] if b < 2 else t.obT[:, :]
                    act.copy(dst[:, :, P * tile:P * tile + P], PS[:, 5].rearrange("p (k q) -> p k q", k=4)).then_inc(ot_ev, 1)

            for n in range(len(GR) + 2):
                if n < len(GR):
                    tile, g = GR[n]
                    S = P * (tile + 1)
                    act.wait_ge(lg_done, n + 1)
                    for j in range(2):
                        for hh in range(2):
                            r = L[:, n % 2, j, hh, 0:S]
                            ins = act.activation(r, r, ACT.Exp, bias=mx[:, n % 2, 2 * j + hh:2 * j + hh + 1],
                                                 accum_out=lsum[:, n % 2, 2 * j + hh:2 * j + hh + 1])
                    ins.then_inc(exp_done, 1)
                if 1 <= n <= len(GR):
                    tile, g = GR[n - 1]
                    act.wait_ge(at_mm, n)
                    if n >= 3:
                        act.wait_ge(pv_mm, n - 2)
                    m = nmat(tile, g)
                    act.copy(AT[:, (n - 1) % 2, 0:m].rearrange("p m q -> p (m q)"),
                             PS[:, 2:4].rearrange("p b x -> p (b x)")[:, 0:P * m]).then_inc(at_ev, 1)
                if n >= 2:
                    tile, g = GR[n - 2]
                    act.wait_ge(pv_mm, n - 1)
                    dst = O[:, tile, 256 * g:256 * g + 256] if g < 4 else OBt[:, tile, 256 * (g - 4):256 * (g - 4) + 256]
                    act.copy(dst, PS[:, 4, 0:256]).then_inc(o_done, 1)
                if n == 9:
                    out_turned(0)
            out_turned(1)


def attention_sample(nc, t):
    PS = t.PS
    SW = PAST + NF
    with ExitStack() as ctx:
        sb = lambda n, s, d=F32: ctx.enter_context(nc.sbuf_tensor(n, s, d))
        sem = t.phase_semaphore
        kc = sb("kc", [P, 2, NU, P])
        vc = sb("vc", [P, 2, NU, P])
        kcT = sb("kcT", [P, NU, P])
        qbd = sb("qbd", [P, 2, NU, 32])
        Ls = sb("Ls", [P, 2, 3, SW])
        Pn = sb("Pn", [P, 2, 3, P])
        mxs = sb("mxs", [P, 2, 3])
        sums = sb("sums", [P, 2, 3])
        PT = sb("PT", [P, 6, P])
        Os = sb("Os", [P, 3, NSEQ, P])
        On = sb("On", [64, 2 * NSEQ, P])
        sqs = sb("sqs", [64, 2 * NSEQ, P])
        sss = sb("sss", [64, 2 * NSEQ])
        kcache_in = [sem(f"kcache_in{i}") for i in range(2)]
        vcache_in = [sem(f"vcache_in{i}") for i in range(2)]
        q_done, kct_mm, kct_ev, ssc_mm, slg_done, sexp_done, pn_done = (sem(x) for x in
            ("q_done", "kct_mm", "kct_ev", "ssc_mm", "slg_done", "sexp_done", "pn_done"))
        pt_mm, pt_ev, spv_mm, os_done, join_mm, join_ev, on_done, sot_mm, sot_ev = (sem(x) for x in
            ("pt_mm", "pt_ev", "spv_mm", "os_done", "join_mm", "join_ev", "on_done", "sot_mm", "sot_ev"))
        dve_step = sem("sample_dve")
        sms_done, srms_done = sem("sms_done"), sem("srms_done")
        block = ctx.enter_context(nc.Block())


        @block.gpsimd
        def _(pool):
            pool.wait_ge(sms_done, 1)
            pool.tensor_tensor(sss[:, :], sss[:, :], t.power[0:64, :], ALU.pow).then_inc(srms_done, 1)

        @block.sync
        def _(sp):
            def load_keys(b):
                if b >= 2:
                    sp.wait_ge(kct_mm, 3 * b - 3)
                sp.dma_start(kc[:, b % 2, 0:8], t.ckd[b]).then_inc(kcache_in[b % 2], 16)
                sp.dma_start(kc[:, b % 2, 8:12], t.ckb[b]).then_inc(kcache_in[b % 2], 16)

            load_keys(0)
            load_keys(1)
            for b in range(NSEQ):
                if 1 <= b and b + 1 < NSEQ:
                    load_keys(b + 1)
                if b >= 2:
                    sp.wait_ge(spv_mm, b - 1)
                sp.dma_start(vc[:, b % 2, 0:8], t.cvd[b]).then_inc(vcache_in[b % 2], 16)
                sp.dma_start(vc[:, b % 2, 8:12], t.cvb[b]).then_inc(vcache_in[b % 2], 16)

        @block.tensor
        def _(pe):
            def turn_cache(b, groups=range(3)):
                pe.wait_ge(kcache_in[b % 2], 32 * (b // 2 + 1))
                for g in groups:
                    n = 3 * b + g
                    if n >= 2:
                        pe.wait_ge(kct_ev, n - 1)
                    for i in range(4):
                        mm = pe.transpose(PS[:, n % 2, P * i:P * i + P], kc[:, b % 2, 4 * g + i], t.ident[:, :])
                    mm.then_inc(kct_mm, 1)

            def scores(b):
                pe.wait_ge(q_done, b + 1)
                pe.wait_ge(kct_ev, 3 * b + 3)
                if b >= 2:
                    pe.wait_ge(slg_done, b - 1)
                for g in range(3):
                    for i in range(4):
                        u = 4 * g + i
                        rows = slice(32 * i, 32 * i + 32)
                        pe.matmul(PS[rows, 2 + 4 * (b % 2), SW * g:SW * g + PAST], qbd[:, b % 2, u], kcT[:, u], start=True, stop=True)
                        mm = pe.matmul(PS[rows, 2 + 4 * (b % 2), SW * g + PAST:SW * g + SW], qbd[:, b % 2, u],
                                       t.kT[:, u, 256 + NF * b:256 + NF * b + NF], start=True, stop=True)
                mm.then_inc(ssc_mm, 1)

            def turn_p(b):
                pe.wait_ge(pn_done, b + 1)
                if b >= 1:
                    pe.wait_ge(pt_ev, b)
                for m in range(6):
                    src = Ls[:, b % 2, m // 2, 0:PAST] if m % 2 == 0 else Pn[:, b % 2, m // 2]
                    mm = pe.transpose(PS[:, 3 + m // 4, P * (m % 4):P * (m % 4) + P], src, t.ident[:, :])
                mm.then_inc(pt_mm, 1)

            def values(b):
                pe.wait_ge(vcache_in[b % 2], 32 * (b // 2 + 1))
                pe.wait_ge(pt_ev, b + 1)
                if b >= 1:
                    pe.wait_ge(os_done, b)
                for g in range(3):
                    for i in range(4):
                        u = 4 * g + i
                        o = PS[32 * i:32 * i + 32, 5, P * g:P * g + P]
                        pe.matmul(o, PT[:, 2 * g, 32 * i:32 * i + 32], vc[:, b % 2, u], start=True, stop=False)
                        mm = pe.matmul(o, PT[:, 2 * g + 1, 32 * i:32 * i + 32], t.V[:, 2, P * u:P * u + P], start=False, stop=True)
                mm.then_inc(spv_mm, 1)

            turn_cache(0)
            scores(0)
            turn_cache(1)
            for b in range(NSEQ):
                if b + 1 < NSEQ:
                    scores(b + 1)
                turn_p(b)
                if b + 2 < NSEQ:
                    turn_cache(b + 2, range(2))
                values(b)
                if b + 2 < NSEQ:
                    turn_cache(b + 2, range(2, 3))
            pe.wait_ge(os_done, NSEQ)
            for n in range(2):
                for i in range(4):
                    mm = pe.transpose(PS[:, n, P * i:P * i + P], Os[:, 2, 4 * n + i], t.ident[:, :])
                mm.then_inc(sot_mm, 1)
            for n in range(4):
                g, b0 = n // 2, 4 * (n % 2)
                if n >= 2:
                    pe.wait_ge(join_ev, n - 1)
                pe.matmul(PS[0:64, 2 + n % 2], t.join[:, :], Os[:, g, b0:b0 + 4].rearrange("p b e -> p (b e)"),
                          start=True, stop=True).then_inc(join_mm, 1)
            pe.wait_ge(on_done, 1)
            pe.wait_ge(sot_ev, 2)
            for n in range(2):
                for i in range(NSEQ):
                    mm = pe.transpose(PS[:, n, 64 * i:64 * i + 64], On[:, NSEQ * n + i], t.ident[0:64, 0:64])
                mm.then_inc(sot_mm, 1)

        @block.scalar
        def _(act):
            def keys(b):
                for g in range(3):
                    n = 3 * b + g
                    act.wait_ge(kct_mm, n + 1)
                    if g == 0 and b >= 1:
                        act.wait_ge(ssc_mm, b)
                    act.copy(kcT[:, 4 * g:4 * g + 4].rearrange("p u s -> p (u s)"), PS[:, n % 2]).then_inc(kct_ev, 1)

            def exponents(b):
                act.wait_ge(slg_done, b + 1)
                for g in range(3):
                    r = Ls[:, b % 2, g]
                    ins = act.activation(r, r, ACT.Exp, bias=mxs[:, b % 2, g:g + 1], accum_out=sums[:, b % 2, g:g + 1])
                ins.then_inc(sexp_done, 1)

            keys(0)
            keys(1)
            exponents(0)
            for b in range(NSEQ):
                act.wait_ge(pt_mm, b + 1)
                if b >= 1:
                    act.wait_ge(spv_mm, b)
                act.copy(PT[:, :, :].rearrange("p m s -> p (m s)"), PS[:, 3:5].rearrange("p b x -> p (b x)")[:, 0:6 * P]).then_inc(pt_ev, 1)
                if b + 1 < NSEQ:
                    exponents(b + 1)
                if b + 2 < NSEQ:
                    keys(b + 2)
            for n in range(2):
                act.wait_ge(sot_mm, n + 1)
                ob = t.obT[:, :, 256 + 64 * n:320 + 64 * n].rearrange("p i (b q) -> p b i q", q=NF)
                src = PS[:, n].rearrange("p (b i j q) -> p b i j q", b=4, i=4, j=2)
                for b in range(4):
                    for j in range(2):
                        rows = slice(64 * j, 64 * j + 64)
                        ins = act.copy(ob[rows, b], src[rows, b, :, j])
                ins.then_inc(sot_ev, 1)
            for n in range(4):
                act.wait_ge(join_mm, n + 1)
                act.copy(On[:, NSEQ * (n // 2) + 4 * (n % 2):NSEQ * (n // 2) + 4 * (n % 2) + 4].rearrange("p b e -> p (b e)"),
                         PS[0:64, 2 + n % 2]).then_inc(join_ev, 1)
            for n in range(2):
                act.wait_ge(sot_mm, 3 + n)
                src = PS[:, n].rearrange("p (b i q) -> p i b q", b=NSEQ, i=4)
                for i in range(4):
                    act.copy(t.oaT[:, 4 * n + i, 256:TOK].rearrange("p (b q) -> p b q", q=NF), src[:, i])

        @block.vector
        def _(dve):
            link = make_link(dve, dve_step)
            link(dve.memset(qbd[:, :, :, :], 0.0))
            link(dve.memset(Pn[:, :, :, :], 0.0))

            def queries(b):
                if b >= 2:
                    dve.wait_ge(ssc_mm, b - 1)
                for j in range(2):
                    rows = slice(64 * j, 64 * j + 64)
                    ins = dve.tensor_copy(qbd[rows, b % 2, :, NF * j:NF * j + NF], t.qT[rows, :, 256 + NF * b:256 + NF * b + NF])
                ins.then_inc(q_done, 1)

            def logits(b):
                r = Ls[:, b % 2]
                dve.wait_ge(ssc_mm, b + 1)
                if b >= 2:
                    dve.wait_ge(pt_mm, b - 1)
                    link(dve.memset(Pn[:, b % 2, :, NF * (b - 2):NF * (b - 2) + NF], 0.0))
                link(dve.scalar_tensor_tensor(r.rearrange("p g s -> p (g s)"), PS[:, 2 + 4 * (b % 2), 0:3 * SW], SM,
                                              t.sbias[:, :, :].rearrange("p g s -> p (g s)"), ALU.mult, ALU.add))
                link(dve.tensor_reduce(mxs[:, b % 2], r, AX.X, ALU.max))
                dve.tensor_scalar(mxs[:, b % 2], mxs[:, b % 2], -1.0, None, ALU.mult).then_inc(slg_done, 1)

            queries(0)
            queries(1)
            logits(0)
            for b in range(NSEQ):
                dve.wait_ge(sexp_done, b + 1)
                dve.tensor_copy(Pn[:, b % 2, :, NF * b:NF * b + NF], Ls[:, b % 2, :, PAST:SW]).then_inc(pn_done, 1)
                link(dve.reciprocal(sums[:, b % 2], sums[:, b % 2]))
                if b + 1 < NSEQ:
                    logits(b + 1)
                if b + 2 < NSEQ:
                    queries(b + 2)
                dve.wait_ge(spv_mm, b + 1)
                dve.tensor_tensor(Os[:, :, b], PS[:, 5, 0:3 * P].rearrange("p (g e) -> p g e", g=3),
                                  sums[:, b % 2].unsqueeze(2).to_broadcast([P, 3, P]), ALU.mult).then_inc(os_done, 1)
            dve.wait_ge(join_ev, 4)
            link(dve.tensor_tensor(sqs[:, :, :], On[:, :, :], On[:, :, :], ALU.mult))
            link(dve.tensor_reduce(sss[:, :], sqs[:, :, :], AX.X, ALU.add))
            dve.tensor_scalar(sss[:, :], sss[:, :], 1.0 / P, EPS, ALU.mult, ALU.add).then_inc(sms_done, 1)
            dve.wait_ge(srms_done, 1)
            link(dve.tensor_tensor(On[:, :, :], On[:, :, :], sss[:, :].unsqueeze(2).to_broadcast([64, 2 * NSEQ, P]), ALU.mult))
            dve.tensor_tensor(On[:, :, :], On[:, :, :], t.sub_g[0:64, :].unsqueeze(1).to_broadcast([64, 2 * NSEQ, P]),
                              ALU.mult).then_inc(on_done, 1)


def projection_out(nc, t):
    PS = t.PS
    with ExitStack() as ctx:
        sb = lambda n, s, d=F32: ctx.enter_context(nc.sbuf_tensor(n, s, d))
        sem = t.phase_semaphore
        M = sb("M", [P, NT, D])
        MT = sb("MT", [P, KD, TOK])
        U2 = sb("U2", [P, NT, D])
        Wa = sb("Wa", [P, 2, KD, CW])
        Wb = sb("Wb", [P, 2, DB // P, CW])
        G = sb("gates_sb", [P, NT, 2, CW])
        gated = sb("gated", [P, 2, CW])
        gate1, shift2, scale2 = sb("gate1", [P, 2, D]), sb("shift2", [P, 2, D]), sb("scale2", [P, 2, D])
        ln1 = sb("ln1", [P, 2, D])
        ln = layer_norm_state(t, sb, sem, "_4")
        wa_in = [sem(f"wa_in{i}") for i in range(2)]
        wb_in = [sem(f"wb_in{i}") for i in range(2)]
        gt_in = [sem(f"gt_in{i}") for i in range(NT)]
        vec_in = sem("vec_in")
        p_mm, m_ev, mt_mm, mt_ev, y_mm, y_ev = (sem(x) for x in ("p_mm", "m_ev", "mt_mm", "mt_ev", "y_mm", "y_ev"))
        u2_done, u2_out, u2t_mm, u2t_ev = (sem(x) for x in ("u2_done", "u2_out", "u2t_mm", "u2t_ev"))
        dve_step = sem("proj_dve")
        block = ctx.enter_context(nc.Block())
        jobs = [(c, n) for c in range(2) for n in range(NT)]

        @block.sync
        def _(sp):
            def load_gates(m):
                c, n = jobs[m]
                for g in range(2):
                    sp.dma_start(G[:, m % NT, g], t.gates[2 * g + c, P * n:P * n + P]).then_inc(gt_in[m % NT], 16)

            for c in range(2):
                cols = slice(CW * c, CW * c + CW)
                sp.dma_start(Wa[:, c], t.p_a[0].rearrange("(k p) n -> p k n", p=P)[:, :, cols]).then_inc(wa_in[c], 16)
                sp.dma_start(Wb[:, c], t.p_b[0].rearrange("(k p) n -> p k n", p=P)[:, :, cols]).then_inc(wb_in[c], 16)
                if c == 0:
                    for m in range(NT):
                        load_gates(m)
            t.load_mod(sp, gate1, 2, vec_in)
            sp.dma_start(ln1[:, 0], t.ln1_g.to_broadcast([P, D])).then_inc(vec_in, 16)
            sp.dma_start(ln1[:, 1], t.ln1_b.to_broadcast([P, D])).then_inc(vec_in, 16)
            t.load_mod(sp, shift2, 3, vec_in)
            t.load_mod(sp, scale2, 4, vec_in)
            for m in range(NT, 2 * NT):
                sp.wait_ge(m_ev, m - NT + 1)
                load_gates(m)
            for c in range(2):
                sp.wait_ge(p_mm, NT * (c + 1))
                sp.dma_start(Wa[:, c], t.w_out[0].rearrange("(k p) n -> p k n", p=P)[:, :, CW * c:CW * c + CW]).then_inc(wa_in[c], 16)
            for n in range(NT):
                sp.wait_ge(u2_done, n + 1)
                sp.dma_start(t.h_dram[P * n:P * n + P], U2[:, n]).then_inc(u2_out, 16)
            sp.wait_ge(u2_out, 16 * NT)

        @block.tensor
        def _(pe):
            def project(m):
                c, n = jobs[m]
                if m >= 2:
                    pe.wait_ge(m_ev, m - 1)
                q = slice(P * n, P * n + P)
                pe.wait_ge(wa_in[c], 16)
                for k in range(KD):
                    pe.matmul(PS[:, 2 * (m % 2)], t.oaT[:, k, q], Wa[:, c, k], start=k == 0, stop=k == KD - 1)
                pe.wait_ge(wb_in[c], 16)
                for k in range(DB // P):
                    mm = pe.matmul(PS[:, 2 * (m % 2) + 1], t.obT[:, k, q], Wb[:, c, k], start=k == 0, stop=k == DB // P - 1)
                mm.then_inc(p_mm, 1)

            def turn(n):
                pe.wait_ge(m_ev, NT + 1 + n)
                for half in range(2):
                    j = 2 * n + half
                    if j >= 2:
                        pe.wait_ge(mt_ev, j - 1)
                    for k in range(4):
                        mm = pe.transpose(PS[:, 4 + j % 2, P * k:P * k + P], M[:, n, P * (4 * half + k):P * (4 * half + k) + P], t.ident[:, :])
                    mm.then_inc(mt_mm, 1)

            def out(n):
                pe.wait_ge(mt_ev, 2 * n + 2)
                if n < 2:
                    pe.wait_ge(m_ev, NT + 2 + n)
                else:
                    pe.wait_ge(y_ev, n - 1)
                for c in range(2):
                    pe.wait_ge(wa_in[c], 32)
                    for k in range(KD):
                        mm = pe.matmul(PS[:, 2 * (n % 2) + c], MT[:, k, P * n:P * n + P], Wa[:, c, k], start=k == 0, stop=k == KD - 1)
                mm.then_inc(y_mm, 1)

            def turn_u2(n):
                pe.wait_ge(u2_done, n + 1)
                for half in range(2):
                    j = 2 * n + half
                    if j >= 2:
                        pe.wait_ge(u2t_ev, j - 1)
                    for k in range(4):
                        mm = pe.transpose(PS[:, 4 + j % 2, P * k:P * k + P], U2[:, n, P * (4 * half + k):P * (4 * half + k) + P], t.ident[:, :])
                    mm.then_inc(u2t_mm, 1)

            for m in range(2 * NT):
                project(m)
                if m > NT:
                    turn(m - NT - 1)
            out(0)
            turn(2)
            for n in range(1, NT):
                out(n)
            for n in range(NT):
                turn_u2(n)

        @block.gpsimd
        def _(pool):
            rsqrts(pool, ln, *range(2 * NT))

        @block.scalar
        def _(act):
            for mm, ev, dst in ((mt_mm, mt_ev, MT), (u2t_mm, u2t_ev, t.hT)):
                for j in range(6):
                    act.wait_ge(mm, j + 1)
                    act.copy(dst[:, 4 * (j % 2):4 * (j % 2) + 4, P * (j // 2):P * (j // 2) + P],
                             PS[:, 4 + j % 2].rearrange("p (k q) -> p k q", k=4)).then_inc(ev, 1)

        @block.vector
        def _(dve):
            link = make_link(dve, dve_step)
            for m, (c, n) in enumerate(jobs):
                dve.wait_ge(p_mm, m + 1)
                dve.wait_ge(gt_in[m % NT], 32 * (m // NT + 1))
                link(dve.tensor_tensor(gated[:, :, :], PS[:, 2 * (m % 2):2 * (m % 2) + 2], G[:, m % NT], ALU.mult))
                link(dve.tensor_tensor(M[:, n, CW * c:CW * c + CW], gated[:, 0], gated[:, 1], ALU.add))
                dve.sem_inc(m_ev, 1)
            dve.wait_ge(vec_in, 96 + 32)
            for n in range(NT):
                dve.wait_ge(y_mm, n + 1)
                dve.wait_ge(mt_mm, 2 * n + 2)
                r = M[:, n]
                y = PS[:, 2 * (n % 2):2 * (n % 2) + 2].rearrange("p b x -> p (b x)")
                link(dve.tensor_tensor(r, y, gate1[:, n // 2], ALU.mult))
                dve.sem_inc(y_ev, 1)
                link(dve.scalar_tensor_tensor(r, t.X[:, n], ALPHA, r, ALU.mult, ALU.add))
                layer_norm(dve, link, ln, t.X[:, n], r)
                link(dve.tensor_tensor(t.X[:, n], t.X[:, n], ln1[:, 0], ALU.mult))
                link(dve.tensor_tensor(t.X[:, n], t.X[:, n], ln1[:, 1], ALU.add))
                layer_norm(dve, link, ln, r, t.X[:, n])
                link(dve.scalar_tensor_tensor(r, scale2[:, n // 2], 1.0, r, ALU.add, ALU.mult))
                dve.tensor_tensor(U2[:, n].rearrange("r (k p) -> r p k", k=KD), r.rearrange("r (p k) -> r p k", k=KD),
                                  shift2[:, n // 2].rearrange("r (p k) -> r p k", k=KD), ALU.add).then_inc(u2_done, 1)


def load_expert(sp, t, e, i):
    s = t.wexp_in[i]
    sp.dma_start(t.W13[:, i, 0], t.w1v[e] if isinstance(e, int) else t.w1v[bass.ds(e, 1)].rearrange("e p k n -> (e p) k n")).then_inc(s, 16)
    sp.dma_start(t.W13[:, i, 1], t.w3v[e] if isinstance(e, int) else t.w3v[bass.ds(e, 1)].rearrange("e p k n -> (e p) k n")).then_inc(s, 16)
    sp.dma_start(t.W2[:, i], t.w2v[e] if isinstance(e, int) else t.w2v[bass.ds(e, 1)].rearrange("e p k n -> (e p) k n")).then_inc(s, 16)


def routing(nc, t):
    PS = t.PS
    with ExitStack() as ctx:
        sb = lambda n, s, d=F32: ctx.enter_context(nc.sbuf_tensor(n, s, d))
        sem = t.phase_semaphore
        wr = sb("wr", [P, KD, E])
        ws13 = sb("ws13", [P, KD, 2, F])
        ws2 = sb("ws2_sb", [P, 2, D])
        ebias = sb("ebias", [P, E])
        sc = sb("sc", [P, NT, E])
        bi = sb("bi", [P, E])
        g8 = sb("g8", [P, NG, 8])
        gs, gm, gn = sb("gs", [P, NG]), sb("gm", [P, NG]), sb("gn", [P, NG])
        cmp, tie, gi = sb("cmp", [P, NG, NG]), sb("tie", [P, NG, NG]), sb("gi", [P, NG, NG], I32)
        t8, i8, i8f = sb("t8", [P, 8]), sb("i8", [P, 8], U32), sb("i8f", [P, 8])
        oh = sb("oh", [P, NT, TOPK, E])
        tmp = sb("tmp", [P, TOPK, E])
        mask = sb("mask", [P, NT, E], F16)
        wsum = sb("wsum", [P, 1])
        tri, ones = sb("tri", [P, P], F16), sb("ones", [P, P], F16)
        tri_f = sb("tri_f", [P, P])
        io_i, io = sb("io_i", [P, P], I32), sb("io", [P, P])
        tk_i, tk = sb("tk_i", [P, NT], I32), sb("tk", [P, NT])
        cnt, ext, inc, base = sb("cnt", [P, E]), sb("ext", [P, E]), sb("inc", [P, E]), sb("base", [P, E])
        one_e = sb("one_e", [P, E])
        code, code2 = sb("code", [P, E]), sb("code2", [P, E])
        ck, si, ci = sb("ck", [P, TOPK]), sb("si", [P, TOPK], I32), sb("ci", [P, TOPK], I32)
        sf, cf = sb("sf", [P, TOPK]), sb("cf", [P, TOPK])
        SL = sb("SL", [P, 2, TOPK, SLOTS], F16)
        CB = sb("CB", [P, 2, TOPK, NBLK], F16)
        CBf = sb("CBf", [P, TOPK, NBLK])
        sh_g, sh_h, sh_T = sb("sh_g", [P, 2, F]), sb("sh_h", [P, NT, F]), sb("sh_T", [P, 2, 2, P])
        wr_in, ws_in, eb_in = sem("wr_in"), sem("ws_in"), sem("eb_in")
        r_mm, sig_done, mask_done, rank_mm, cnt_mm, code_done, list_mm, iota_done = (sem(x) for x in
            ("r_mm", "sig_done", "mask_done", "rank_mm", "cnt_mm", "code_done", "list_mm", "riota_done"))
        s_mm, s_silu, s_hid, st_mm, st_ev, sy_mm, sy_ev, rc_done = (sem(x) for x in
            ("s_mm", "s_silu", "s_hid", "st_mm", "st_ev", "sy_mm", "sy_ev", "rc_done"))
        dve_step = sem("route_dve")
        block = ctx.enter_context(nc.Block())

        @block.sync
        def _(sp):
            sp.dma_start(wr[:, :, :], t.w_router[0].rearrange("(p k) e -> p k e", k=KD)).then_inc(wr_in, 16)
            sp.dma_start(ebias[:, :], t.e_bias.to_broadcast([P, E])).then_inc(eb_in, 16)
            sp.dma_start(ws13[:, :, 0], t.ws1[0].rearrange("(p k) n -> p k n", k=KD)).then_inc(ws_in, 16)
            sp.dma_start(ws13[:, :, 1], t.ws3[0].rearrange("(p k) n -> p k n", k=KD)).then_inc(ws_in, 16)
            sp.dma_start(ws2[:, :, :], t.ws2[0].rearrange("(p k) n -> p k n", k=2)).then_inc(ws_in, 16)
            for i in range(WB):
                load_expert(sp, t, i, i)

        @block.gpsimd
        def _(pool):
            pool.iota(io_i[:, :], pattern=[[1, P]], base=0, channel_multiplier=0).then_inc(iota_done, 1)
            pool.iota(tk_i[:, :], pattern=[[P, NT]], base=0, channel_multiplier=1).then_inc(iota_done, 1)
            pool.iota(gi[:, :, :], pattern=[[1, NG], [-1, NG]], base=0, channel_multiplier=0).then_inc(iota_done, 1)

        @block.tensor
        def _(pe):
            pe.wait_ge(wr_in, 16)
            for n in range(NT):
                for k in range(KD):
                    mm = pe.matmul(PS[:, n, 0:E], t.hT[:, k, P * n:P * n + P], wr[:, k], start=k == 0, stop=k == KD - 1)
                mm.then_inc(r_mm, 1)
            pe.wait_ge(ws_in, 48)
            for n in range(NT):
                if n >= 2:
                    pe.wait_ge(s_hid, n - 1)
                for k in range(KD):
                    mm = pe.matmul(PS[:, 4 + n % 2], t.hT[:, k, P * n:P * n + P], ws13[:, k].rearrange("p j n -> p (j n)"),
                                   start=k == 0, stop=k == KD - 1)
                mm.then_inc(s_mm, 1)
                pe.wait_ge(mask_done, n + 1)
                for m in range(n):
                    pe.matmul(PS[:, n, 64:64 + E], ones[:, :], mask[:, m], start=m == 0, stop=False)
                pe.matmul(PS[:, n, 64:64 + E], tri[:, :], mask[:, n], start=n == 0, stop=True).then_inc(rank_mm, 1)
            for m in range(NT):
                mm = pe.matmul(PS[:, 3, 0:E], ones[:, :], mask[:, m], start=m == 0, stop=m == NT - 1)
            mm.then_inc(cnt_mm, 1)
            for n in range(NT):
                pe.wait_ge(s_hid, NT)
                if n:
                    pe.wait_ge(st_ev, n)
                for j in range(2):
                    mm = pe.transpose(PS[:, 6, P * j:P * j + P], sh_h[:, n, P * j:P * j + P], t.ident[:, :])
                mm.then_inc(st_mm, 1)
                pe.wait_ge(st_ev, n + 1)
                if n:
                    pe.wait_ge(sy_ev, n)
                for c in range(2):
                    for j in range(2):
                        mm = pe.matmul(PS[:, 4 + 3 * c], sh_T[:, n % 2, j], ws2[:, j, CW * c:CW * c + CW], start=j == 0, stop=j == 1)
                mm.then_inc(sy_mm, 1)
            for n in range(NT):
                pe.wait_ge(code_done, n + 1)
                for k in range(TOPK):
                    mm = pe.matmul(PS[0:SLOTS, 5, 0:NBLK], SL[:, n % 2, k], CB[:, n % 2, k], start=n + k == 0, stop=n == NT - 1 and k == TOPK - 1)
                mm.then_inc(list_mm, 1)

        @block.scalar
        def _(act):
            for n in range(NT):
                act.wait_ge(r_mm, n + 1)
                act.activation(sc[:, n], PS[:, n, 0:E], ACT.Sigmoid).then_inc(sig_done, 1)
            for n in range(NT):
                act.wait_ge(s_mm, n + 1)
                if n >= 2:
                    act.wait_ge(s_hid, n - 1)
                act.activation(sh_g[:, n % 2], PS[:, 4 + n % 2, 0:F], ACT.Silu).then_inc(s_silu, 1)
            for n in range(NT):
                act.wait_ge(st_mm, n + 1)
                if n >= 2:
                    act.wait_ge(sy_mm, n - 1)
                act.copy(sh_T[:, n % 2].rearrange("p j q -> p (j q)"), PS[:, 6, 0:2 * P]).then_inc(st_ev, 1)
                act.wait_ge(sy_mm, n + 1)
                for c in range(2):
                    ins = act.copy(t.acc[:, n, CW * c:CW * c + CW], PS[:, 4 + 3 * c])
                ins.then_inc(sy_ev, 1)

        @block.vector
        def _(dve):
            link = make_link(dve, dve_step)
            dve.wait_ge(iota_done, 3)
            link(dve.tensor_copy(io[:, :], io_i[:, :]))
            link(dve.tensor_copy(tk[:, :], tk_i[:, :]))
            link(dve.tensor_scalar(tie[:, :, :], gi[:, :, :], 0.0, None, ALU.is_gt))
            link(dve.tensor_scalar(tri[:, :], io[:, :], tk[:, 0:1], None, ALU.is_gt))
            link(dve.memset(ones[:, :], 1.0))
            link(dve.memset(one_e[:, :], 1.0))
            dve.wait_ge(eb_in, 16)

            def hidden(n):
                dve.wait_ge(s_silu, n + 1)
                dve.tensor_tensor(sh_h[:, n].rearrange("r (j p) -> r p j", j=2), sh_g[:, n % 2].rearrange("r (p j) -> r p j", j=2),
                                  PS[:, 4 + n % 2, F:2 * F].rearrange("r (p j) -> r p j", j=2), ALU.mult).then_inc(s_hid, 1)

            for n in range(NT):
                dve.wait_ge(sig_done, n + 1)
                link(dve.tensor_tensor(bi[:, :], sc[:, n], ebias[:, :], ALU.add))
                for g in range(NG):
                    ins = dve.max(g8[:, g], bi[:, 8 * g:8 * g + 8])
                link(ins)
                link(dve.tensor_tensor(gs[:, :], g8[:, :, 0], g8[:, :, 1], ALU.add))
                mine = gs[:, :].unsqueeze(2).to_broadcast([P, NG, NG])
                other = gs[:, :].unsqueeze(1).to_broadcast([P, NG, NG])
                link(dve.tensor_tensor(cmp[:, :, :], other, mine, ALU.is_equal))
                link(dve.tensor_tensor(cmp[:, :, :], cmp[:, :, :], tie[:, :, :], ALU.mult))
                link(dve.tensor_reduce(gm[:, :], cmp[:, :, :], AX.X, ALU.add))
                link(dve.tensor_tensor(cmp[:, :, :], other, mine, ALU.is_gt))
                link(dve.tensor_reduce(gn[:, :], cmp[:, :, :], AX.X, ALU.add))
                link(dve.tensor_tensor(gm[:, :], gm[:, :], gn[:, :], ALU.add))
                link(dve.tensor_scalar(gm[:, :], gm[:, :], float(TOPG), None, ALU.is_lt))
                link(dve.tensor_scalar(gn[:, :], gm[:, :], -1.0, 1e30, ALU.add, ALU.mult))
                b3 = bi[:, :].rearrange("p (g e) -> p g e", g=NG)
                link(dve.tensor_tensor(b3, b3, gm[:, :].unsqueeze(2).to_broadcast([P, NG, 8]), ALU.mult))
                link(dve.tensor_tensor(b3, b3, gn[:, :].unsqueeze(2).to_broadcast([P, NG, 8]), ALU.add))
                link(dve.max(t8[:, :], bi[:, :]))
                link(dve.max_index(i8[:, :], t8[:, :], bi[:, :]))
                link(dve.tensor_copy(i8f[:, :], i8[:, :]))
                link(dve.tensor_tensor(oh[:, n], io[:, 0:E].unsqueeze(1).to_broadcast([P, TOPK, E]),
                                       i8f[:, :].unsqueeze(2).to_broadcast([P, TOPK, E]), ALU.is_equal))
                with nc.allow_low_precision("a count of at most one"):
                    dve.tensor_reduce(mask[:, n], oh[:, n].rearrange("p k e -> p e k"), AX.X, ALU.add).then_inc(mask_done, 1)
                link(dve.tensor_tensor(tmp[:, :, :], oh[:, n], sc[:, n].unsqueeze(1).to_broadcast([P, TOPK, E]), ALU.mult))
                link(dve.tensor_reduce(t.wts[:, n], tmp[:, :, :], AX.X, ALU.add))
                link(dve.tensor_reduce(wsum[:, :], t.wts[:, n], AX.X, ALU.add))
                link(dve.reciprocal(wsum[:, :], wsum[:, :]))
                link(dve.tensor_scalar(t.wts[:, n], t.wts[:, n], wsum[:, 0:1], ROUTED_SCALE, ALU.mult, ALU.mult))
                hidden(n)
            dve.wait_ge(cnt_mm, 1)
            link(dve.tensor_copy(cnt[:, :], PS[:, 3, 0:E]))
            link(dve.tensor_scalar(ext[:, :], cnt[:, :], float(SLOTS), None, ALU.is_gt))
            for m in range(2, TOK // SLOTS):
                link(dve.scalar_tensor_tensor(ext[:, :], cnt[:, :], float(SLOTS * m), ext[:, :], ALU.is_gt, ALU.add))
            link(dve.tensor_tensor_scan(inc[:, :], one_e[:, :], ext[:, :], 0.0, ALU.mult, ALU.add))
            link(dve.memset(t.ov[:, 0:1], 0))
            link(dve.tensor_copy(t.ov[:, 1:E + 1], inc[0:1, :]))
            link(dve.tensor_tensor(base[:, :], inc[:, :], ext[:, :], ALU.subtract))
            link(dve.tensor_tensor(base[:, :], base[:, :], io[:, 0:E], ALU.subtract))
            link(dve.tensor_scalar(base[:, :], base[:, :], float(E - 1), None, ALU.add))
            for n in range(NT):
                dve.wait_ge(rank_mm, n + 1)
                link(dve.tensor_copy(code2[:, :], PS[:, n, 64:64 + E]))
                link(dve.scalar_tensor_tensor(code[:, :], code2[:, :], float(SLOTS), base[:, :], ALU.is_ge, ALU.mult))
                link(dve.tensor_tensor(code[:, :], code[:, :], io[:, 0:E], ALU.add))
                link(dve.scalar_tensor_tensor(code[:, :], code[:, :], float(SLOTS), code2[:, :], ALU.mult, ALU.add))
                link(dve.tensor_tensor(tmp[:, :, :], oh[:, n], code[:, :].unsqueeze(1).to_broadcast([P, TOPK, E]), ALU.mult))
                link(dve.tensor_reduce(ck[:, :], tmp[:, :, :], AX.X, ALU.add))
                link(dve.tensor_copy(t.rows[:, n], ck[:, :]))
                link(dve.tensor_scalar(si[:, :], t.rows[:, n], SLOTS - 1, None, ALU.bitwise_and))
                link(dve.tensor_scalar(ci[:, :], t.rows[:, n], 6, None, ALU.logical_shift_right))
                link(dve.tensor_copy(sf[:, :], si[:, :]))
                link(dve.tensor_copy(cf[:, :], ci[:, :]))
                if n >= 2:
                    dve.wait_ge(list_mm, n - 1)
                link(dve.tensor_tensor(SL[:, n % 2], io[:, 0:SLOTS].unsqueeze(1).to_broadcast([P, TOPK, SLOTS]),
                                       sf[:, :].unsqueeze(2).to_broadcast([P, TOPK, SLOTS]), ALU.is_equal))
                link(dve.tensor_tensor(CBf[:, :, :], io[:, 0:NBLK].unsqueeze(1).to_broadcast([P, TOPK, NBLK]),
                                       cf[:, :].unsqueeze(2).to_broadcast([P, TOPK, NBLK]), ALU.is_equal))
                dve.tensor_scalar(CB[:, n % 2], CBf[:, :, :], tk[:, n:n + 1], None, ALU.mult).then_inc(code_done, 1)
            dve.wait_ge(list_mm, NT)
            link(dve.memset(t.tokens[:, NBLK:NBLK + 1], 0))
            dve.tensor_copy(t.tokens[:, 0:NBLK], PS[0:SLOTS, 5, 0:NBLK])


def experts(nc, t):
    PS = t.PS
    with ExitStack() as ctx:
        sb = lambda n, s, d=F32: ctx.enter_context(nc.sbuf_tensor(n, s, d))
        sem = t.phase_semaphore
        XG = sb("XG", [SLOTS, WB, D])
        XT = sb("XT", [P, 2, KD, SLOTS])
        sg, hid, hidT = sb("sg", [SLOTS, 2, F]), sb("hid", [SLOTS, 2, F]), sb("hidT", [P, 2, 2, SLOTS])
        Y = sb("Y", [P, 2, CW])
        ix = sb("ix", [SLOTS, WB], I32)
        XGo, XTo = sb("XGo", [SLOTS, D]), sb("XTo", [P, KD, SLOTS])
        sgo, hido, hidTo = sb("sgo", [SLOTS, F]), sb("hido", [SLOTS, F]), sb("hidTo", [P, 2, SLOTS])
        Yo = sb("Yo", [P, CW])
        ixo = sb("ixo", [SLOTS, 1], I32)
        g_in = [sem(f"g_in{i}") for i in range(WB)]
        y_out = [sem(f"y_out{i}") for i in range(2)]
        ix_done, xt_mm, xt_ev, h_mm, silu_done, hid_done, ht_mm, ht_ev, yy_mm, yy_ev = (sem(x) for x in
            ("ix_done", "xt_mm", "xt_ev", "h_mm", "esilu_done", "hid_done", "ht_mm", "ht_ev", "yy_mm", "yy_ev"))
        o_ix, o_in, o_xt, o_xe, o_h, o_silu, o_hid, o_ht, o_he, o_y, o_ye, o_out = (sem(x) for x in
            ("o_ix", "o_in", "o_xt", "o_xe", "o_h", "o_silu", "o_hid", "o_ht", "o_he", "o_y", "o_ye", "o_out"))
        waited = sem("waited")
        block = ctx.enter_context(nc.Block())

        def at(it, i, off=0):
            return it * WB + (i + off)

        def extra(eng, e, step):
            lo = eng.value_load(t.ov[0:1, bass.ds(e, 1)], min_val=0, max_val=XB)
            hi = eng.value_load(t.ov[0:1, bass.ds(e + 1, 1)], min_val=0, max_val=XB)
            with eng.If(lo < hi):
                with eng.Fori(lo, hi) as g:
                    step(g)

        def once_above(eng, semaphore, count):
            if not isinstance(count, int) or count > 0:
                eng.wait_ge(semaphore, count)

        def stand_alone(eng):
            eng.sem_inc(waited, 1)

        def loops(eng, body):
            for i in range(WB):
                body(0, i, False)
            with eng.Fori(1, E // WB - 1) as it:
                for i in range(WB):
                    body(it, i, False)
            for i in range(WB):
                body(E // WB - 1, i, True)

        @block.sync
        def _(sp):
            def store_extra(g):
                sp.wait_ge(o_ye, g + 2)
                for h in range(2):
                    sp.dma_start(t.y_dram[bass.ds((g + E) * SLOTS, SLOTS), CW * h:CW * h + CW], Yo[64 * h:64 * h + 64, :]).then_inc(o_out, 16)

            def body(it, i, last):
                sp.wait_ge(yy_ev, at(it, i, 1))
                for h in range(2):
                    sp.dma_start(t.y_dram[bass.ds(at(it, i) * SLOTS, SLOTS), CW * h:CW * h + CW], Y[64 * h:64 * h + 64, i % 2]).then_inc(y_out[i % 2], 16)
                extra(sp, at(it, i), store_extra)
                if not last:
                    load_expert(sp, t, at(it, i, WB), i)
            sp.sem_inc(o_out, 32)
            loops(sp, body)
            for i in range(2):
                sp.wait_ge(y_out[i], 32 * E // 2)
            total = sp.value_load(t.ov[0:1, E:E + 1], min_val=0, max_val=XB)
            sp.wait_ge(o_out, total * 32 + 32)
            stand_alone(sp)

        @block.gpsimd
        def _(pool):
            def gather(e, i, n):
                pool.tensor_copy(ix[:, i:i + 1], t.tokens[:, bass.ds(e, 1)]).then_inc(ix_done, 1)
                pool.wait_ge(ix_done, n)
                stand_alone(pool)
                pool.indirect_dma_start(XG[:, i], None, t.h_dram, bass.IndirectOffsetOnAxis(ap=ix[:, i:i + 1], axis=0)).then_inc(g_in[i], 16)

            def gather_next(g):
                pool.wait_ge(o_xt, g + 1)
                pool.tensor_copy(ixo[:, 0:1], t.tokens[:, bass.ds(g + E + 1, 1)]).then_inc(o_ix, 1)
                pool.wait_ge(o_ix, g + 2)
                stand_alone(pool)
                pool.indirect_dma_start(XGo[:, :], None, t.h_dram, bass.IndirectOffsetOnAxis(ap=ixo[:, 0:1], axis=0)).then_inc(o_in, 16)

            for i in range(WB):
                gather(i, i, i + 1)
            pool.tensor_copy(ixo[:, 0:1], t.tokens[:, E:E + 1]).then_inc(o_ix, 1)
            pool.wait_ge(o_ix, 1)
            pool.indirect_dma_start(XGo[:, :], None, t.h_dram, bass.IndirectOffsetOnAxis(ap=ixo[:, 0:1], axis=0)).then_inc(o_in, 16)

            def body(it, i, last):
                extra(pool, at(it, i), gather_next)
                if not last:
                    pool.wait_ge(xt_mm, at(it, i, 1))
                    gather(at(it, i, WB), i, at(it, i, WB + 1))
            loops(pool, body)

        @block.tensor
        def _(pe):
            def turn(n, i, it):
                pe.wait_ge(g_in[i], (it + 1) * 16)
                once_above(pe, xt_ev, n)
                stand_alone(pe)
                for k in range(KD):
                    mm = pe.transpose(PS[:, 0, SLOTS * k:SLOTS * k + SLOTS], XG[:, i, P * k:P * k + P], t.ident[0:SLOTS, 0:SLOTS])
                mm.then_inc(xt_mm, 1)

            def up(n, i, it):
                pe.wait_ge(t.wexp_in[i], (it + 1) * 48)
                pe.wait_ge(xt_ev, n + 1)
                once_above(pe, hid_done, n - 1)
                for k in range(KD):
                    for h in range(2):
                        mm = pe.matmul(PS[64 * h:64 * h + 64, 2 + i % 2, 0:F], XT[:, i % 2, k], t.W13[:, i, h, k], start=k == 0, stop=k == KD - 1)
                mm.then_inc(h_mm, 1)

            def turn_extra():
                for k in range(KD):
                    mm = pe.transpose(PS[:, 1, SLOTS * k:SLOTS * k + SLOTS], XGo[:, P * k:P * k + P], t.ident[0:SLOTS, 0:SLOTS])
                mm.then_inc(o_xt, 1)

            def extra_block(i):
                def step(g):
                    pe.wait_ge(o_xe, g + 1)
                    pe.wait_ge(o_ye, g + 1)
                    for k in range(KD):
                        for h in range(2):
                            mm = pe.matmul(PS[64 * h:64 * h + 64, 7, 0:F], XTo[:, k], t.W13[:, i, h, k], start=k == 0, stop=k == KD - 1)
                    mm.then_inc(o_h, 1)
                    pe.wait_ge(o_in, (g + 2) * 16)
                    stand_alone(pe)
                    turn_extra()
                    pe.wait_ge(o_hid, g + 1)
                    stand_alone(pe)
                    for j in range(2):
                        mm = pe.transpose(PS[:, 7, SLOTS * j:SLOTS * j + SLOTS], hido[:, P * j:P * j + P], t.ident[0:SLOTS, 0:SLOTS])
                    mm.then_inc(o_ht, 1)
                    pe.wait_ge(o_he, g + 1)
                    for j in range(2):
                        for h in range(2):
                            mm = pe.matmul(PS[64 * h:64 * h + 64, 7], hidTo[:, j], t.W2[:, i, j, CW * h:CW * h + CW], start=j == 0, stop=j == 1)
                    mm.then_inc(o_y, 1)
                return step

            def body(it, i, last):
                n = at(it, i)
                nxt = (it + (i + 1) // WB, (i + 1) % WB)
                nx2 = (it + (i + 2) // WB, (i + 2) % WB)
                if not last or i + 1 < WB:
                    up(at(it, i, 1), nxt[1], nxt[0])
                pe.wait_ge(hid_done, n + 1)
                once_above(pe, ht_ev, n)
                stand_alone(pe)
                for j in range(2):
                    mm = pe.transpose(PS[:, 4, SLOTS * j:SLOTS * j + SLOTS], hid[:, i % 2, P * j:P * j + P], t.ident[0:SLOTS, 0:SLOTS])
                mm.then_inc(ht_mm, 1)
                if not last or i + 2 < WB:
                    turn(at(it, i, 2), nx2[1], nx2[0])
                pe.wait_ge(ht_ev, n + 1)
                once_above(pe, yy_ev, at(it, i, -1))
                for j in range(2):
                    for h in range(2):
                        mm = pe.matmul(PS[64 * h:64 * h + 64, 5 + i % 2], hidT[:, i % 2, j], t.W2[:, i, j, CW * h:CW * h + CW], start=j == 0, stop=j == 1)
                mm.then_inc(yy_mm, 1)
                extra(pe, n, extra_block(i))

            turn(0, 0, 0)
            turn(1, 1, 0)
            up(0, 0, 0)
            pe.wait_ge(o_in, 16)
            turn_extra()
            loops(pe, body)

        @block.scalar
        def _(act):
            def evict(n, i):
                act.wait_ge(xt_mm, n + 1)
                once_above(act, h_mm, n - 1)
                act.copy(XT[:, i % 2].rearrange("p k s -> p (k s)"), PS[:, 0]).then_inc(xt_ev, 1)

            def silu(n, i):
                act.wait_ge(h_mm, n + 1)
                once_above(act, hid_done, n - 1)
                act.activation(sg[:, i % 2], PS[0:SLOTS, 2 + i % 2, 0:F], ACT.Silu).then_inc(silu_done, 1)

            def turned_extra(count):
                act.wait_ge(o_xt, count)
                act.copy(XTo[:, :, :].rearrange("p k s -> p (k s)"), PS[:, 1]).then_inc(o_xe, 1)

            def step(g):
                act.wait_ge(o_h, g + 1)
                act.activation(sgo[:, :], PS[0:SLOTS, 7, 0:F], ACT.Silu).then_inc(o_silu, 1)
                turned_extra(g + 2)

            def body(it, i, last):
                if not last or i + 1 < WB:
                    silu(at(it, i, 1), i + 1)
                if not last or i + 2 < WB:
                    evict(at(it, i, 2), i)
                extra(act, at(it, i), step)

            evict(0, 0)
            evict(1, 1)
            silu(0, 0)
            turned_extra(1)
            loops(act, body)

        @block.vector
        def _(dve):
            def hidden(n, i):
                dve.wait_ge(silu_done, n + 1)
                once_above(dve, ht_mm, n - 1)
                dve.tensor_tensor(hid[:, i % 2].rearrange("r (j p) -> r p j", j=2), sg[:, i % 2].rearrange("r (p j) -> r p j", j=2),
                                  PS[SLOTS:P, 2 + i % 2, 0:F].rearrange("r (p j) -> r p j", j=2), ALU.mult).then_inc(hid_done, 1)

            def step(g):
                dve.wait_ge(o_silu, g + 1)
                dve.tensor_tensor(hido[:, :].rearrange("r (j p) -> r p j", j=2), sgo[:, :].rearrange("r (p j) -> r p j", j=2),
                                  PS[SLOTS:P, 7, 0:F].rearrange("r (p j) -> r p j", j=2), ALU.mult).then_inc(o_hid, 1)
                dve.wait_ge(o_ht, g + 1)
                dve.tensor_copy(hidTo[:, :, :].rearrange("p j s -> p (j s)"), PS[:, 7, 0:P]).then_inc(o_he, 1)
                dve.wait_ge(o_out, g * 32 + 32)
                dve.wait_ge(o_y, g + 1)
                dve.tensor_copy(Yo[:, :], PS[:, 7]).then_inc(o_ye, 1)

            def body(it, i, last):
                n = at(it, i)
                dve.wait_ge(ht_mm, n + 1)
                once_above(dve, yy_mm, at(it, i, -1))
                dve.tensor_copy(hidT[:, i % 2].rearrange("p j s -> p (j s)"), PS[:, 4, 0:P]).then_inc(ht_ev, 1)
                if not last or i + 1 < WB:
                    hidden(at(it, i, 1), i + 1)
                dve.wait_ge(yy_mm, n + 1)
                once_above(dve, y_out[i % 2], (it * (WB // 2) + i // 2) * 32)
                dve.tensor_copy(Y[:, i % 2], PS[:, 5 + i % 2]).then_inc(yy_ev, 1)
                extra(dve, n, step)

            dve.sem_inc(o_ye, 1)
            hidden(0, 0)
            loops(dve, body)


def combine(nc, t):
    PS = t.PS
    HALF = TOPK // 2
    with ExitStack() as ctx:
        sb = lambda n, s, d=F32: ctx.enter_context(nc.sbuf_tensor(n, s, d))
        sem = t.phase_semaphore
        G = sb("G", [P, TOPK, D])
        diag = sb("diag", [P, NT, HALF, P])
        vec = sb("vec7", [P, 4, D])
        ln = layer_norm_state(t, sb, sem, "_7")
        row_in = [sem(f"row_in{k}") for k in range(TOPK)]
        vec_in, row_dve, row_pe, sum_ev = sem("vec7_in"), sem("row_dve"), sem("row_pe"), sem("sum_ev")
        diag_done, normed, scaled, y_done, fin_out = sem("diag_done"), sem("normed"), sem("scaled"), sem("y_done"), sem("fin_out")
        dve_step = sem("comb_dve")
        block = ctx.enter_context(nc.Block())

        @block.gpsimd
        def _(pool):
            def scale(n):
                a = t.acc[:, n]
                pool.wait_ge(normed, n + 1)
                pool.tensor_tensor(a, a, vec[:, 2], ALU.mult).then_inc(scaled, 1)
                pool.wait_ge(scaled, n + 1)
                pool.tensor_tensor(a, a, vec[:, 3], ALU.add).then_inc(y_done, 1)

            def gather(n):
                for i in range(HALF):
                    for k, used in ((i, row_dve), (HALF + i, row_pe)):
                        if n:
                            pool.wait_ge(used, HALF * (n - 1) + i + 1)
                        pool.indirect_dma_start(G[:, k], None, t.y_dram, bass.IndirectOffsetOnAxis(ap=t.rows[:, n, k:k + 1], axis=0)).then_inc(row_in[k], 16)
            gather(0)
            gather(1)
            for n in range(NT):
                rsqrts(pool, ln, n)
                if n < NT - 1:
                    scale(n)
                if n + 2 < NT:
                    gather(n + 2)

        @block.sync
        def _(sp):
            t.load_mod(sp, vec, 5, vec_in)
            sp.dma_start(vec[:, 2], t.ln2_g.to_broadcast([P, D])).then_inc(vec_in, 16)
            sp.dma_start(vec[:, 3], t.ln2_b.to_broadcast([P, D])).then_inc(vec_in, 16)
            for n in range(NT):
                sp.wait_ge(y_done, n + 1)
                dst = t.yp[P * n:P * n + P] if n < 2 else t.ys
                sp.dma_start(dst, t.acc[:, n]).then_inc(fin_out, 16)
            sp.wait_ge(fin_out, 16 * NT)

        @block.tensor
        def _(pe):
            pe.wait_ge(diag_done, 1)
            for n in range(NT):
                if n >= 2:
                    pe.wait_ge(sum_ev, n - 1)
                for i in range(HALF):
                    pe.wait_ge(row_in[HALF + i], 16 * (n + 1))
                    for c in range(2):
                        mm = pe.matmul(PS[:, 2 * (n % 2) + c], diag[:, n, i], G[:, HALF + i, CW * c:CW * c + CW],
                                       start=i == 0, stop=i == HALF - 1)
                    mm.then_inc(row_pe, 1)

        @block.vector
        def _(dve):
            link = make_link(dve, dve_step)
            for n in range(NT):
                for i in range(HALF):
                    ins = dve.tensor_scalar(diag[:, n, i], t.ident[:, :], t.wts[:, n, HALF + i:HALF + i + 1], None, ALU.mult)
            ins.then_inc(diag_done, 1)
            for n in range(NT):
                a = t.acc[:, n]
                for k in range(HALF):
                    dve.wait_ge(row_in[k], 16 * (n + 1))
                    link(dve.scalar_tensor_tensor(a, G[:, k], t.wts[:, n, k:k + 1], a, ALU.mult, ALU.add))
                    dve.sem_inc(row_dve, 1)
                dve.wait_ge(row_pe, HALF * (n + 1))
                link(dve.tensor_tensor(a, a, PS[:, 2 * (n % 2):2 * (n % 2) + 2].rearrange("p b x -> p (b x)"), ALU.add))
                dve.sem_inc(sum_ev, 1)
                if n == 0:
                    dve.wait_ge(vec_in, 64)
                link(dve.tensor_tensor(a, a, vec[:, n // 2], ALU.mult))
                link(dve.scalar_tensor_tensor(a, t.X[:, n], ALPHA, a, ALU.mult, ALU.add))
                layer_norm(dve, link, ln, a, a)
                if n < NT - 1:
                    dve.sem_inc(normed, 1)
                else:
                    dve.wait_ge(y_done, NT - 1)
                    link(dve.tensor_tensor(a, a, vec[:, 2], ALU.mult))
                    dve.tensor_tensor(a, a, vec[:, 3], ALU.add).then_inc(y_done, 1)


INS = ["x_prompt", "x_sample", "cache_k_diff", "cache_v_diff", "cache_k_band", "cache_v_band", "c_prompt",
       "c_sample", "w_ada", "b_ada", "w_in", "b_in", "lambda_q1", "lambda_k1", "lambda_q2", "lambda_k2",
       "subln_g", "rel_bias", "p_a", "p_b", "w_out", "ln1_g", "ln1_b", "w_router", "e_bias", "w1", "w3", "w2",
       "ws1", "ws3", "ws2", "ln2_g", "ln2_b"]
OUTS = [("y_prompt", (1, SEQ, D)), ("y_sample", (NSEQ, NF, D)),
        ("k_diff_prompt", (1, 1, SEQ, HA, 2, HD)), ("v_diff_prompt", (1, 1, SEQ, HA, 2 * HD)),
        ("k_band_prompt", (1, 1, SEQ, HB, HD)), ("v_band_prompt", (1, 1, SEQ, HB, HD)),
        ("k_diff_sample", (1, NSEQ, NF, HA, 2, HD)), ("v_diff_sample", (1, NSEQ, NF, HA, 2 * HD)),
        ("k_band_sample", (1, NSEQ, NF, HB, HD)), ("v_band_sample", (1, NSEQ, NF, HB, HD))]


class Shared:
    pass


def streaming_layer(nc, a, o):
    t = Shared()
    t.x_prompt, t.x_sample, t.c_prompt, t.c_sample = a["x_prompt"], a["x_sample"], a["c_prompt"], a["c_sample"]
    t.w_ada, t.b_ada, t.w_in, t.b_in = a["w_ada"], a["b_ada"], a["w_in"], a["b_in"]
    t.subln_g, t.rel_bias, t.p_a, t.p_b = a["subln_g"], a["rel_bias"], a["p_a"], a["p_b"]
    t.w_out, t.ln1_g, t.ln1_b, t.w_router = a["w_out"], a["ln1_g"], a["ln1_b"], a["w_router"]
    t.e_bias, t.ws1, t.ws3, t.ws2 = a["e_bias"], a["ws1"], a["ws3"], a["ws2"]
    t.ln2_g, t.ln2_b = a["ln2_g"], a["ln2_b"]
    t.lq1, t.lk1, t.lq2, t.lk2 = (a[n] for n in ("lambda_q1", "lambda_k1", "lambda_q2", "lambda_k2"))
    t.ckd = a["cache_k_diff"].rearrange("l b s h j d -> (l b) s h (j d)")
    t.cvd = a["cache_v_diff"].rearrange("l b s h d -> (l b) s h d")
    t.ckb = a["cache_k_band"].rearrange("l b s (u j) d -> (l b) s u (j d)", j=2)
    t.cvb = a["cache_v_band"].rearrange("l b s (u j) d -> (l b) s u (j d)", j=2)
    t.w1v = a["w1"].rearrange("l e (p k) n -> (l e) p k n", k=KD)
    t.w3v = a["w3"].rearrange("l e (p k) n -> (l e) p k n", k=KD)
    t.w2v = a["w2"].rearrange("l e (p k) n -> (l e) p k n", k=2)
    t.yp = o["y_prompt"].rearrange("b s d -> (b s) d")
    t.ys = o["y_sample"].rearrange("b s d -> (b s) d")
    t.kdp = o["k_diff_prompt"].rearrange("l b s h j d -> (l b s) (h j d)")
    t.kds = o["k_diff_sample"].rearrange("l b s h j d -> (l b s) (h j d)")
    t.vdp = o["v_diff_prompt"].rearrange("l b s h d -> (l b s) (h d)")
    t.vds = o["v_diff_sample"].rearrange("l b s h d -> (l b s) (h d)")
    t.kbp = o["k_band_prompt"].rearrange("l b s h d -> (l b s) (h d)")
    t.kbs = o["k_band_sample"].rearrange("l b s h d -> (l b s) (h d)")
    t.vbp = o["v_band_prompt"].rearrange("l b s h d -> (l b s) (h d)")
    t.vbs = o["v_band_sample"].rearrange("l b s h d -> (l b s) (h d)")
    t.mod = nc.dram_tensor("mod", (1 + NSEQ, 6 * D), F32, kind="Internal").ap()
    t.rev_dram = nc.dram_tensor("rev_table", (HB, 3 * CLIP), F32, kind="Internal").ap()
    t.gates = nc.dram_tensor("gates", (len(GC), TOK, CW), F32, kind="Internal").ap()
    t.h_dram = nc.dram_tensor("h_rows", (TOK, D), F32, kind="Internal").ap()
    t.y_dram = nc.dram_tensor("expert_rows", (NBLK * SLOTS, D), F32, kind="Internal").ap()

    with ExitStack() as ctx:
        t.PS = ctx.enter_context(nc.psum_tensor("PS", [P, 8, CW], F32))

        used = []

        def scoped(scope, name, shape, dtype=F32):
            used.append(name)
            return scope.enter_context(nc.sbuf_tensor(f"{name}_{len(used)}", shape, dtype))

        t.zeros = scoped(ctx, "zeros", [P, D])
        t.power = scoped(ctx, "power", [P, 2 * NSEQ])
        t.ident = scoped(ctx, "ident", [P, P])
        t.X = scoped(ctx, "X", [P, NT, D])
        t.uT = scoped(ctx, "uT", [P, KD, TOK])
        t.hT = t.uT
        t.zeros_done = ctx.enter_context(nc.semaphore("zeros_done"))
        t.ident_done = ctx.enter_context(nc.semaphore("ident_done"))
        t.wexp_in = [ctx.enter_context(nc.semaphore(f"wexp_in{i}")) for i in range(WB)]

        t.phase_sems = []

        def phase_semaphore(name):
            t.phase_sems.append(nc.alloc_semaphore(name=name))
            return t.phase_sems[-1]

        def recycle():
            nc.clear_and_free_semaphores(t.phase_sems)
            nc.all_engine_barrier()
            t.phase_sems = []
        t.phase_semaphore = phase_semaphore

        def build_identity(pool):
            pool.memset(t.power[:, :], -0.5)
            pool.memset(t.zeros[:, :], 0.0).then_inc(t.zeros_done, 1)
            pool.memset(t.ident[:, :], 0.0).then_inc(t.ident_done, 1)
            pool.wait_ge(t.ident_done, 1)
            pool.affine_select(out=t.ident[:, :], in_=t.ident[:, :], compare_op=ALU.not_equal, fill=1.0, base=0,
                               pattern=[[-1, P]], channel_multiplier=1).then_inc(t.ident_done, 1)
        t.build_identity = build_identity

        def load_mod(sp, dst, part, s):
            cols = slice(D * part, D * part + D)
            sp.dma_start(dst[:, 0], t.mod[0:1, cols].to_broadcast([P, D])).then_inc(s, 16)
            sp.dma_start(dst[:, 1], bass.AP(t.mod.tensor, 6 * D + D * part, [[6 * D, NSEQ], [0, NF], [1, D]])).then_inc(s, 16)
        t.load_mod = load_mod

        with ExitStack() as mixer:
            t.oaT = scoped(mixer, "oaT", [P, HA, TOK])
            t.obT = scoped(mixer, "obT", [P, 4, TOK])
            with ExitStack() as attention:
                t.qT = scoped(attention, "qT", [P, NU, TOK])
                t.kT = scoped(attention, "kT", [P, NU, TOK])
                t.V = scoped(attention, "V", [P, NT, DA + DB])
                t.alibi_p = scoped(attention, "alibi_p", [P, HA, 256])
                t.band_p = scoped(attention, "band_p", [P, HB, 256])
                t.sbias = scoped(attention, "sbias", [P, 3, PAST + NF])
                t.sub_g = scoped(attention, "sub_g", [P, 2 * HD])
                t.neg_lam = scoped(attention, "neg_lam", [P, 1])
                t.join = scoped(attention, "join", [P, 64])
                with ExitStack() as scope:
                    t.W = scoped(scope, "W", [P, 2, KD, CW])
                    t.cT = scoped(scope, "cT", [P, KD, 32])
                    t.win_in = [phase_semaphore(f"win_in{i}") for i in range(2)]
                    conditioning(nc, t)
                    projection_in(nc, t)
                attention_prompt(nc, t)
                attention_sample(nc, t)
            recycle()
            projection_out(nc, t)
        t.acc = scoped(ctx, "acc", [P, NT, D])
        t.wts = scoped(ctx, "wts", [P, NT, TOPK])
        t.rows = scoped(ctx, "rows", [P, NT, TOPK], I32)
        t.tokens = scoped(ctx, "tokens", [SLOTS, NBLK + 1], I32)
        t.ov = scoped(ctx, "ov", [1, E + 1], I32)
        with ExitStack() as scope:
            t.W13 = scoped(scope, "W13", [P, WB, 2, KD, F])
            t.W2 = scoped(scope, "W2", [P, WB, 2, D])
            routing(nc, t)
            experts(nc, t)
        combine(nc, t)


def kernel(**inputs):
    import concourse.bacc as bacc
    from concourse.bass_utils import run_bass_kernel_spmd

    nc = bacc.Bacc("TRN2", target_bir_lowering=False, num_devices=1)
    arrays, a, o = {}, {}, {}
    for name in INS:
        x = np.ascontiguousarray(inputs[name])
        arrays[name] = x
        a[name] = nc.dram_tensor(name, x.shape, mybir.dt.from_np(x.dtype), kind="ExternalInput").ap()
    for name, shape in OUTS:
        o[name] = nc.dram_tensor(name, shape, F32, kind="ExternalOutput").ap()
    streaming_layer(nc, a, o)
    r = run_bass_kernel_spmd(nc, [arrays], core_ids=[0])
    return tuple(r.results[0][name] for name, _ in OUTS)
```

```python
from contextlib import ExitStack

import concourse.bass as bass
import concourse.mybir as mybir
import numpy as np

ALU = mybir.AluOpType
ACT = mybir.ActivationFunctionType
AX = mybir.AxisListType
F32 = mybir.dt.float32
F16 = mybir.dt.float16
I32 = mybir.dt.int32
U32 = mybir.dt.uint32
F32R = mybir.dt.float32r

P = 128
D = 1024
KD = D // P
SEQ, NSEQ, NF, PAST = 256, 8, 16, 128
NC = 1 + NSEQ
NT = 3
TOK = NT * P
CHUNK = 64
HD = 64
HA = HB = 8
DA, DB = HA * 2 * HD, HB * HD
NU = 12
CLIP = 128
N_IN = 3 * DA + 3 * DB + 2 * D
CW = 512
E, TOPK, NG, TOPG, F = 64, 8, 8, 4, 256
SLOTS = 64
XB = (TOK * TOPK - 1) // SLOTS
NBLK = E + XB
ROUTED_SCALE = 2.5
ALPHA = 2.0 ** 0.25
LAM_INIT = 0.2
EPS = 1e-5
SM = HD ** -0.5
WB = 4
QC = {0: 0, 1: 4, 6: 8}
KC = {2: 0, 3: 512, 7: 1024}
VC = {4: 0, 5: 512, 8: 1024}
GC = (9, 10, 11, 12)


def layer_norm(dve, link, ln, out, x):
    stats, mv, rstd = ln.stats, ln.mv, ln.rstd
    for i in range(2):
        link(dve.bn_stats(stats[:, 6 * i:6 * i + 6], x[:, CW * i:CW * i + CW]))
    link(dve.bn_aggr(mv[:, :], stats[:, :]))
    dve.tensor_scalar(mv[:, 1:2], mv[:, 1:2], EPS, None, ALU.add).then_inc(ln.var_done, 1)
    ln.count += 1
    dve.wait_ge(ln.rstd_done, ln.count)
    link(dve.tensor_scalar(out, x, mv[:, 0:1], rstd[:, 0:1], ALU.subtract, ALU.mult))


def layer_norm_state(t, sb, sem, tag):
    ln = Shared()
    ln.stats, ln.mv, ln.rstd = sb("stats" + tag, [P, 12]), sb("mv" + tag, [P, 2]), sb("rstd" + tag, [P, 1])
    ln.power, ln.count = t.power, 0
    ln.var_done, ln.rstd_done = sem("var_done" + tag), sem("rstd_done" + tag)
    return ln


def rsqrts(pool, ln, *norms):
    for n in norms:
        pool.wait_ge(ln.var_done, n + 1)
        pool.tensor_tensor(ln.rstd[:, :], ln.mv[:, 1:2], ln.power[:, 0:1], ALU.pow).then_inc(ln.rstd_done, 1)


def make_link(eng, sem):
    count = [0]

    def link(ins):
        count[0] += 1
        ins.then_inc(sem, 1)
        eng.wait_ge(sem, count[0])
    return link


def half_of(w, i):
    c, h = i // 2, i % 2
    return w[0].rearrange("(k p) n -> p k n", p=P)[:, 4 * h:4 * h + 4, CW * c:CW * c + CW]


def conditioning(nc, t, constants):
    PS = t.PS
    with ExitStack() as ctx:
        sb = lambda n, s, d=F32: ctx.enter_context(nc.sbuf_tensor(n, s, d))
        sem = t.phase_semaphore
        NA = 2 * D // CW
        c_rows = sb("c_rows", [NC, D])
        cT = t.cT
        b_q = sb("b_q", [P, NA, P])
        mod_q = sb("mod_q", [P, NA, P])
        shift = t.hT[:, :, :].rearrange("p k q -> p (k q)")[:, 0:2 * D].rearrange("p (g d) -> p g d", g=2)
        scale = sb("scale", [P, 2, D])
        u = t.X
        ln = layer_norm_state(t, sb, sem, "_1")
        c_in, x_in, bada_in = sem("c_in"), sem("x_in"), sem("bada_in")
        ada_in = [sem(f"ada_in{i}") for i in range(2 * NA)]
        flat = [x[:, :, :].rearrange("p a b -> p (a b)") for x in (t.qT, t.kT, t.V)]
        ada = [x[:, 4 * CW * h:4 * CW * h + 4 * CW] for x in flat for h in range(2)]
        ada += [x[:, :, :].rearrange("p a b -> p (a b)")[:, 0:4 * CW] for x in (t.oaT, t.band_p)]
        ada = [x.rearrange("p (k n) -> p k n", k=4) for x in ada]
        silu_done, ct_mm, ct_zero, ct_done = sem("silu_done"), sem("ct_mm"), sem("ct_zero"), sem("ct_done")
        ada_mm, ada_ev, mod_out, mod_back = sem("ada_mm"), sem("ada_ev"), sem("mod_out"), [sem(f"mod_back{g}") for g in range(2)]
        u_done, ut_mm, ut_hi, ut_lo = sem("u_done"), sem("ut_mm"), sem("ut_hi"), sem("ut_lo")
        dve_step = sem("cond_dve")
        block = ctx.enter_context(nc.Block())

        @block.sync
        def _(sp):
            sp.dma_start(c_rows[0:1, :], t.c_prompt).then_inc(c_in, 16)
            sp.dma_start(c_rows[1:NC, :], t.c_sample).then_inc(c_in, 16)
            for j in range(4):
                src = t.b_ada.rearrange("l (c j n) -> l j c n", j=4, n=P)[:, j, 0:NA]
                sp.dma_start(b_q[32 * j:32 * j + 32], src.to_broadcast([32, NA, P])).then_inc(bada_in, 16)
            for n in range(2):
                sp.dma_start(t.X[:, n], t.x_prompt[0, P * n:P * n + P]).then_inc(x_in, 16)
            sp.dma_start(t.X[:, 2], t.x_sample.rearrange("b s d -> (b s) d")).then_inc(x_in, 16)
            constants.sync_early(sp)
            for i in range(2 * NA):
                sp.dma_start(ada[i], half_of(t.w_ada, i)).then_inc(ada_in[i], 16)
            sp.wait_ge(ada_ev, NA)
            for j in range(4):
                dst = t.mod.rearrange("r (c j n) -> r j c n", j=4, n=P)[:, j, 0:NA]
                sp.dma_start(dst, mod_q[32 * j:32 * j + NC]).then_inc(mod_out, 16)
            sp.wait_ge(mod_out, 64)
            for g in range(2):
                t.load_mod_of(sp, scale, g, 1, mod_back[g])
                t.load_mod_of(sp, shift, g, 0, mod_back[g])
            for i in range(2):
                sp.dma_start(t.raw[:, i], half_of(t.w_in, i)).then_inc(t.win_in[i], 16)
            constants.sync_rev(sp)

        @block.scalar
        def _(act):
            act.wait_ge(c_in, 32)
            act.activation(c_rows[:, :], c_rows[:, :], ACT.Silu).then_inc(silu_done, 1)
            constants.scalar(act)
            for n in range(6):
                act.wait_ge(ut_mm, n + 1)
                tile, half = n // 2, n % 2
                act.copy(t.u_hi[:, 4 * half:4 * half + 4, P * tile:P * tile + P],
                         PS[:, 2 + n % 2].rearrange("p (k q) -> p k q", k=4)).then_inc(ut_hi, 1)

        @block.vector
        def _(dve):
            link = make_link(dve, dve_step)
            dve.memset(cT[:, :, :], 0.0).then_inc(ct_zero, 1)
            dve.wait_ge(ct_zero, 1)
            dve.wait_ge(ct_mm, 1)
            dve.tensor_copy(cT[:, :, 0:NC], PS[:, 0, 0:KD * NC].rearrange("p (k r) -> p k r", k=KD)).then_inc(ct_done, 1)
            dve.wait_ge(x_in, 48)
            for n in range(NT):
                layer_norm(dve, link, ln, u[:, n], t.X[:, n])
            constants.vector_early(dve)
            dve.wait_ge(bada_in, 64)
            for i in range(NA):
                dve.wait_ge(ada_mm, 2 * i + 2)
                dve.tensor_tensor(mod_q[:, i], PS[:, i, 0:P], b_q[:, i], ALU.add).then_inc(ada_ev, 1)
            for n in range(NT):
                g = n // 2
                dve.wait_ge(mod_back[g], 32)
                link(dve.scalar_tensor_tensor(u[:, n], scale[:, g], 1.0, u[:, n], ALU.add, ALU.mult))
                dve.tensor_tensor(u[:, n], u[:, n], shift[:, g], ALU.add).then_inc(u_done, 1)
            for n in range(6):
                dve.wait_ge(ut_hi, n + 1)
                tile, half = n // 2, n % 2
                ks = slice(4 * half, 4 * half + 4)
                dve.tensor_tensor(t.u_lo[:, tile, ks], PS[:, 2 + n % 2].rearrange("p (k q) -> p k q", k=4),
                                  t.u_hi[:, ks, P * tile:P * tile + P].bitcast(F32), ALU.subtract).then_inc(ut_lo, 1)

        @block.gpsimd
        def _(pool):
            t.build_identity(pool)
            constants.gpsimd(pool)
            rsqrts(pool, ln, *range(NT))

        @block.tensor
        def _(pe):
            pe.wait_ge(t.ident_done, 2)
            pe.wait_ge(silu_done, 1)
            for k in range(KD):
                mm = pe.transpose(PS[:, 0, NC * k:NC * k + NC], c_rows[:, P * k:P * k + P], t.ident[0:NC, 0:NC])
            mm.then_inc(ct_mm, 1)
            pe.wait_ge(ct_done, 1)
            for i in range(2 * NA):
                c, h = i // 2, i % 2
                pe.wait_ge(ada_in[i], 16)
                for k in range(4):
                    for j in range(4):
                        mm = pe.matmul(PS[32 * j:32 * j + 32, c, 0:P], cT[:, 4 * h + k], ada[i][:, k, P * j:P * j + P],
                                       start=h + k == 0, stop=4 * h + k == KD - 1)
                mm.then_inc(ada_mm, 1)
            for n in range(6):
                tile, half = n // 2, n % 2
                pe.wait_ge(u_done, tile + 1)
                if n >= 2:
                    pe.wait_ge(ut_lo, n - 1)
                for k in range(4):
                    mm = pe.transpose(PS[:, 2 + n % 2, P * k:P * k + P], u[:, tile, P * (4 * half + k):P * (4 * half + k) + P], t.ident[:, :])
                mm.then_inc(ut_mm, 1)


def projection_in(nc, t, constants):
    PS = t.PS
    with ExitStack() as ctx:
        sb = lambda n, s, d=F32: ctx.enter_context(nc.sbuf_tensor(n, s, d))
        sem = t.phase_semaphore
        keys = t.X[:, :, :].rearrange("p n d -> p (n d)").rearrange("p (a n d) -> p a n d", a=2, n=NT)
        fall_p = t.X[:, :, :].rearrange("p n d -> p (n d)")[:, 0:HB * 256].rearrange("p (h x) -> p h x", h=HB)
        b_col = sb("b_col", [P, NU])
        lent = t.hT[:, :, :].rearrange("p k q -> p (k q)")
        b_row = lent[:, 0:2 * CW].rearrange("p (i n) -> p i n", i=2)
        gate = lent[:, 2 * CW:4 * CW].rearrange("p (i n) -> p i n", i=2)
        b_q = lent[:, 4 * CW:4 * CW + 2 * P].rearrange("p (i n) -> p i n", i=2)
        mod_q = lent[:, 5 * CW:5 * CW + 2 * P].rearrange("p (i n) -> p i n", i=2)
        w_hi, w_lo = sb("w_hi", [P, 2, 4, CW], F32R), sb("w_lo", [P, 2, 4, CW], F32R)
        win_in = t.win_in
        u_hi, u_lo = t.u_hi, t.u_lo
        wada = (t.oaT[:, :, :].rearrange("p k q -> p (k q)").rearrange("p (k n) -> p k n", n=CW),
                t.obT[:, :, :].rearrange("p k q -> p (k q)")[:, 0:2 * CW].rearrange("p (k n) -> p k n", n=CW))
        A0, NA = 2 * D // CW, 4 * D // CW
        ada_in, ada_mm, ada_ev = sem("ada2_in"), sem("ada2_mm"), sem("ada2_ev")
        mod_out = [sem(f"mod2_out{i}") for i in range(2)]
        brow_in = [sem(f"brow_in{i}") for i in range(2)]
        bin_in = sem("bin_in")
        g_add, g_sig = sem("g_add"), sem("g_sig")
        g_out = [sem(f"g_out{i}") for i in range(2)]
        hi_done, lo_done, half0_mm = sem("hi_done"), sem("lo_done"), sem("half0_mm")
        z_mm, z_ev_act, z_ev_dve = sem("z_mm"), sem("z_ev_act"), sem("z_ev_dve")
        kt_mm, kt_ev, v_out = sem("kt_mm"), sem("kt_ev"), sem("v_out")
        k_out = [sem(f"k_out{i}") for i in range(2)]
        NCH = N_IN // CW
        RC = [c for c in range(NCH) if c not in QC]
        KEYS = list(KC)
        jobs = [(c, i) for c in range(NCH) for i in range(4 if c in QC else NT)]
        of_chunk = [[n for n, j in enumerate(jobs) if j[0] == c] for c in range(NCH)]
        act_jobs = [n for n, (c, _) in enumerate(jobs) if c in QC]
        dve_jobs = [n for n, (c, _) in enumerate(jobs) if c not in QC]
        block = ctx.enter_context(nc.Block())

        def half_used(eng, i):
            if i % 2:
                eng.wait_ge(z_mm, of_chunk[i // 2][-1] + 1)
            else:
                eng.wait_ge(half0_mm, i // 2 + 1)

        @block.sync
        def _(sp):
            with nc.allow_non_contiguous_dma(reason="128 x 12 bias values, one column each"):
                for u0, c0, n in ((0, 0, 8), (8, 3 * DA, 4)):
                    sp.dma_start(b_col[:, u0:u0 + n], t.b_in[0, c0:c0 + P * n].rearrange("(u p) -> p u", p=P)).then_inc(bin_in, 16)
            for c in range(NCH):
                if c not in QC:
                    b = RC.index(c)
                    if b >= 2:
                        sp.wait_ge(z_ev_dve, NT * (b - 1))
                    sp.dma_start(b_row[:, b % 2], t.b_in[:, CW * c:CW * c + CW].to_broadcast([P, CW])).then_inc(brow_in[b % 2], 16)
                if c < NA:
                    if c:
                        sp.wait_ge(ada_mm, c)
                    src = t.w_ada[0].rearrange("(k p) n -> p k n", p=P)[:, :, CW * (A0 + c):CW * (A0 + c) + CW]
                    sp.dma_start(wada[0], src[:, 0:6]).then_inc(ada_in, 16)
                    sp.dma_start(wada[1], src[:, 6:8]).then_inc(ada_in, 16)
                    for j in range(4):
                        sp.dma_start(b_q[32 * j:32 * j + 32, c % 2], t.b_ada[:, CW * (A0 + c) + P * j:CW * (A0 + c) + P * j + P].to_broadcast([32, P])).then_inc(ada_in, 16)
                if c == 0:
                    constants.sync_late(sp, fall_p)
                for i in (2 * c + 2, 2 * c + 3):
                    if i < 2 * NCH:
                        sp.wait_ge(lo_done, i - 1)
                        sp.dma_start(t.raw[:, i % 2], half_of(t.w_in, i)).then_inc(win_in[i % 2], 16)

        @block.gpsimd
        def _(pool):
            for c in range(NCH):
                if c in KC or c in VC:
                    c0 = KC[c] if c in KC else VC[c]
                    outs = ((t.kdp, t.kds) if c in KC else (t.vdp, t.vds)) if c0 < DA else ((t.kbp, t.kbs) if c in KC else (t.vbp, t.vbs))
                    src = keys[:, KEYS.index(c) % 2] if c in KC else t.V[:, :, c0:c0 + CW]
                    done = k_out[KEYS.index(c) % 2] if c in KC else v_out
                    cols = slice(c0 % DA, c0 % DA + CW)
                    pool.wait_ge(z_ev_dve, 1 + dve_jobs.index(of_chunk[c][-1]))
                    for n in range(2):
                        pool.dma_start(outs[0][P * n:P * n + P, cols], src[:, n]).then_inc(done, 16)
                    pool.dma_start(outs[1][:, cols], src[:, 2]).then_inc(done, 16)
                if c < NA:
                    pool.wait_ge(ada_ev, c + 1)
                    for j in range(4):
                        n0 = CW * (A0 + c) + P * j
                        pool.dma_start(t.mod[:, n0:n0 + P], mod_q[32 * j:32 * j + NC, c % 2]).then_inc(mod_out[c % 2], 16)
            for i in range(2):
                pool.wait_ge(mod_out[i], 64 * (NA // 2))
            pool.wait_ge(k_out[0], 96)
            pool.wait_ge(k_out[1], 48)
            pool.wait_ge(v_out, 16 * NT * len(VC))

        @block.tensor
        def _(pe):
            def transpose_keys(c):
                for i in range(NT):
                    n = NT * KEYS.index(c) + i
                    pe.wait_ge(z_ev_dve, 1 + dve_jobs.index(jobs.index((c, i))))
                    if n >= 2:
                        pe.wait_ge(kt_ev, n - 1)
                    for m in range(4):
                        mm = pe.transpose(PS[:, 6 + n % 2, P * m:P * m + P], keys[:, KEYS.index(c) % 2, i, P * m:P * m + P], t.ident[:, :])
                    mm.then_inc(kt_mm, 1)

            for c in range(NCH):
                for h in range(2):
                    g = 2 * c + h
                    pe.wait_ge(lo_done, g + 1)
                    for n in of_chunk[c]:
                        i = jobs[n][1]
                        if n >= 5 and h == 0:
                            o = n - 5
                            if o in act_jobs:
                                pe.wait_ge(z_ev_act, act_jobs.index(o) + 1)
                            else:
                                pe.wait_ge(z_ev_dve, dve_jobs.index(o) + 1)
                        for k in range(4):
                            K = 4 * h + k
                            for part, (u_part, w_part) in enumerate(((0, 0), (0, 1), (1, 0))):
                                w = w_lo[:, g % 2, k] if w_part else w_hi[:, g % 2, k]
                                start, stop = K + part == 0, K == KD - 1 and part == 2
                                if c in QC:
                                    u = u_lo[:, :, K] if u_part else u_hi[:, K].rearrange("p (n q) -> p n q", n=NT)
                                    mm = pe.matmul(PS[:, n % 5, 0:TOK].rearrange("p (n q) -> p n q", n=NT), w[:, P * i:P * i + P], u, start=start, stop=stop)
                                else:
                                    u = u_lo[:, i, K] if u_part else u_hi[:, K, P * i:P * i + P]
                                    mm = pe.matmul(PS[:, n % 5], u, w, start=start, stop=stop)
                        if h:
                            mm.then_inc(z_mm, 1)
                    if h == 0:
                        mm.then_inc(half0_mm, 1)
                if c == 1:
                    constants.tensor(pe, fall_p)
                if c - 1 in KC:
                    transpose_keys(c - 1)
                if c < NA:
                    pe.wait_ge(ada_in, 96 * (c + 1))
                    if c:
                        pe.wait_ge(ada_ev, c)
                    for k in range(KD):
                        w = wada[0][:, k] if k < 6 else wada[1][:, k - 6]
                        for m in range(4):
                            mm = pe.matmul(PS[32 * m:32 * m + 32, 5, 0:P], t.cT[:, k], w[:, P * m:P * m + P], start=k == 0, stop=k == KD - 1)
                    mm.then_inc(ada_mm, 1)

        @block.scalar
        def _(act):
            k_done = [0]

            def hi_part(i):
                if i < 2 * NCH:
                    act.wait_ge(win_in[i % 2], 16 * (i // 2 + 1))
                    if i >= 2:
                        half_used(act, i - 2)
                    act.copy(w_hi[:, i % 2].rearrange("p k n -> p (k n)"), t.raw[:, i % 2].rearrange("p k n -> p (k n)")).then_inc(hi_done, 1)

            def turn_keys(c):
                for i in range(NT):
                    k_done[0] += 1
                    act.wait_ge(kt_mm, k_done[0])
                    u0 = KC[c] // P
                    act.copy(t.kT[:, u0:u0 + 4, P * i:P * i + P],
                             PS[:, 6 + (k_done[0] - 1) % 2].rearrange("p (u q) -> p u q", u=4)).then_inc(kt_ev, 1)

            hi_part(0)
            act.wait_ge(bin_in, 32)
            for c in range(NCH):
                hi_part(2 * c + 1)
                hi_part(2 * c + 2)
                for n in of_chunk[c]:
                    i = jobs[n][1]
                    if c in QC:
                        act.wait_ge(z_mm, n + 1)
                        u = QC[c] + i
                        act.activation(t.qT[:, u], PS[:, n % 5, 0:TOK], ACT.Identity, bias=b_col[:, u:u + 1]).then_inc(z_ev_act, 1)
                    if c in GC:
                        m = NT * (c - GC[0]) + i
                        act.wait_ge(g_add, m + 1)
                        act.activation(gate[:, m % 2], gate[:, m % 2], ACT.Sigmoid).then_inc(g_sig, 1)
                        act.wait_ge(g_sig, m + 1)
                        act.dma_start(t.gates[c - GC[0], P * i:P * i + P], gate[:, m % 2]).then_inc(g_out[m % 2], 16)
                if c - 1 in KC:
                    turn_keys(c - 1)
            for i in range(2):
                act.wait_ge(g_out[i], 16 * NT * len(GC) // 2)

        @block.vector
        def _(dve):
            def lo_part(i):
                if i < 2 * NCH:
                    dve.wait_ge(hi_done, i + 1)
                    dve.tensor_tensor(w_lo[:, i % 2], t.raw[:, i % 2], w_hi[:, i % 2].bitcast(F32), ALU.subtract).then_inc(lo_done, 1)

            def mod_chunk(c):
                if c < NA:
                    dve.wait_ge(ada_mm, c + 1)
                    if c >= 2:
                        dve.wait_ge(mod_out[c % 2], 64 * (c // 2))
                    dve.tensor_tensor(mod_q[:, c % 2], PS[:, 5, 0:P], b_q[:, c % 2], ALU.add).then_inc(ada_ev, 1)

            lo_part(0)
            for c in range(NCH):
                lo_part(2 * c + 1)
                lo_part(2 * c + 2)
                if c:
                    mod_chunk(c - 1)
                if c == 1:
                    constants.vector_late(dve)
                if c in QC:
                    continue
                b = RC.index(c)
                dve.wait_ge(brow_in[b % 2], 16 * (b // 2 + 1))
                for n in of_chunk[c]:
                    i = jobs[n][1]
                    dve.wait_ge(z_mm, n + 1)
                    if c in GC:
                        m = NT * (c - GC[0]) + i
                        if m >= 2:
                            dve.wait_ge(g_out[m % 2], 16 * (m // 2))
                        dve.tensor_tensor(gate[:, m % 2], PS[:, n % 5], b_row[:, b % 2], ALU.add).then_inc(g_add, 1)
                        dve.wait_ge(g_add, m + 1)
                        dve.sem_inc(z_ev_dve, 1)
                        continue
                    if c == KEYS[2] and i == 0:
                        dve.wait_ge(k_out[0], 48)
                    dst = keys[:, KEYS.index(c) % 2, i] if c in KC else t.V[:, i, VC[c]:VC[c] + CW]
                    dve.tensor_tensor(dst, PS[:, n % 5], b_row[:, b % 2], ALU.add).then_inc(z_ev_dve, 1)


def attention_constants(t, sb, sb_early):
    sem = t.phase_semaphore
    NR = 3 * CLIP
    fall_s = sb("fall_s", [P, PAST + NF])
    flip, flip16 = sb("flip", [P, P]), sb("flip16", [P, P])
    table = sb_early("table", [HB, 2 * CLIP + 1])
    rev = sb_early("rev", [HB, NR])
    di = sb_early("di", [P, 256], I32)
    df = sb_early("df", [P, 256])
    xi = sb_early("xi", [P, PAST + NF], I32)
    xf = sb_early("xf", [P, PAST + NF])
    xn = sb_early("xn", [P, PAST + NF])
    qi = sb_early("qi", [P, 1], I32)
    qf = sb_early("qf", [P, 1])
    slope = sb_early("slope", [P, 2])
    lamv = sb_early("lamv", [P, 4, HD])
    lamp = sb_early("lamp", [P, 2, HD])
    lamd = sb_early("lamd", [P, 2])
    lame = sb_early("lame", [P, 2])
    flip_done, flip_mm, flip_ev = sem("flip_done"), sem("flip_mm"), sem("flip_ev")
    PS = t.PS
    table_in, rev_done, rev_out, band_in = sem("table_in"), sem("rev_done"), sem("rev_out"), sem("band_in")
    lam_in, g_in, iota_done, lamd_done, lame_done = sem("lam_in"), sem("g_in"), sem("iota_done"), sem("lamd_done"), sem("lame_done")
    dve_step = sem("const_dve")

    def sync_early(sp):
        sp.dma_start(table[:, :], t.rel_bias[0]).then_inc(table_in, 16)
        for i, v in enumerate((t.lq1, t.lk1, t.lq2, t.lk2)):
            sp.dma_start(lamv[:, i], v.to_broadcast([P, HD])).then_inc(lam_in, 16)
        sp.dma_start(t.sub_g[:, :], t.subln_g.to_broadcast([P, 2 * HD])).then_inc(g_in, 16)

    def sync_rev(sp):
        sp.wait_ge(rev_done, 1)
        sp.dma_start(t.rev_dram, rev[:, :]).then_inc(rev_out, 16)
        sp.wait_ge(rev_out, 16)

    def sync_late(sp, fall_p):
        h = t.rev_dram.tensor
        sp.dma_start(fall_p[:, :, :], bass.AP(h, 0, [[1, P], [NR, HB], [1, 256]])).then_inc(band_in, 16)
        sp.dma_start(fall_s[:, :], bass.AP(h, P - NF, [[NR, HB], [1, NF], [1, PAST + NF]])).then_inc(band_in, 16)

    def gpsimd(pool):
        pool.iota(di[:, :], pattern=[[-1, 256]], base=PAST, channel_multiplier=1).then_inc(iota_done, 1)
        pool.iota(xi[:, :], pattern=[[-1, PAST + NF]], base=PAST, channel_multiplier=0).then_inc(iota_done, 1)
        pool.iota(qi[:, :], pattern=[[0, 1]], base=0, channel_multiplier=1).then_inc(iota_done, 1)

    def tensor(pe, fall_p):
        pe.wait_ge(flip_done, 1)
        pe.wait_ge(band_in, 32)
        for n in range(5):
            if n >= 2:
                pe.wait_ge(flip_ev, n - 1)
            if n < 4:
                pe.matmul(PS[:, 6 + n % 2], flip[:, :], fall_p[:, 2 * n:2 * n + 2].rearrange("p h x -> p (h x)"),
                          start=True, stop=True).then_inc(flip_mm, 1)
            else:
                pe.matmul(PS[:, 6, 0:PAST + NF], flip16[:, :], fall_s[:, :], start=True, stop=True).then_inc(flip_mm, 1)
        pe.wait_ge(flip_ev, 5)

    def scalar(act):
        act.wait_ge(lamd_done, 1)
        act.activation(lame[:, :], lamd[:, :], ACT.Exp).then_inc(lame_done, 1)

    def vector_early(dve):
        link = make_link(dve, dve_step)
        dve.wait_ge(lam_in, 64)
        for i in range(2):
            link(dve.tensor_tensor(lamp[:, i], lamv[:, 2 * i], lamv[:, 2 * i + 1], ALU.mult))
        dve.tensor_reduce(lamd[:, :], lamp[:, :, :], AX.X, ALU.add).then_inc(lamd_done, 1)
        dve.wait_ge(table_in, 16)
        dve.tensor_copy(rev[:, 0:P - 1], table[:, 2 * CLIP:2 * CLIP + 1].to_broadcast([HB, P - 1]))
        dve.tensor_copy(rev[:, P - 1:NR], table[:, ::-1]).then_inc(rev_done, 1)
        dve.wait_ge(t.ident_done, 2)
        dve.tensor_copy(flip[:, :], t.ident[:, ::-1])
        dve.tensor_copy(flip16[:, :].rearrange("p (h q) -> p h q", q=NF),
                        t.ident[:, :].rearrange("p (h q) -> p h q", q=NF)[:, :, ::-1]).then_inc(flip_done, 1)
        dve.wait_ge(iota_done, 3)
        link(dve.tensor_copy(df[:, :], di[:, :]))
        link(dve.scalar_tensor_tensor(df[:, :], df[:, :], -1.0, df[:, :], ALU.mult, ALU.max))
        link(dve.tensor_scalar(df[0:CHUNK, 192:256], df[0:CHUNK, 192:256], 1e9, None, ALU.add))
        for h in range(HA):
            dve.tensor_scalar(t.alibi_p[:, h], df[:, :], -2.0 ** -(h + 1), None, ALU.mult)
        link(dve.tensor_scalar(qi[:, :], qi[:, :], NF - 1, None, ALU.bitwise_and))
        link(dve.tensor_copy(qf[:, :], qi[:, :]))
        link(dve.tensor_copy(xf[:, :], xi[:, :]))
        link(dve.tensor_scalar(xf[:, :], xf[:, :], qf[:, 0:1], None, ALU.add))
        link(dve.scalar_tensor_tensor(xn[:, :], xf[:, :], -1.0, xf[:, :], ALU.mult, ALU.max))
        for g in range(2):
            for i in range(4):
                link(dve.memset(slope[32 * i:32 * i + 32, g:g + 1], -2.0 ** -(4 * g + i + 1)))
        for g in range(2):
            dve.tensor_scalar(t.sbias[:, g], xn[:, :], slope[:, g:g + 1], None, ALU.mult)
        dve.wait_ge(lame_done, 1)
        link(dve.tensor_tensor(t.neg_lam[:, :], lame[:, 1:2], lame[:, 0:1], ALU.subtract))
        link(dve.tensor_scalar(t.neg_lam[:, :], t.neg_lam[:, :], -LAM_INIT, None, ALU.add))
        idv = t.ident[:, :].rearrange("p (i j q) -> p i j q", i=4, j=2)
        dve.scalar_tensor_tensor(t.join[:, :].rearrange("p (i q) -> p i q", i=4), idv[:, :, 1], t.neg_lam[:, 0:1],
                                 idv[:, :, 0], ALU.mult, ALU.add)
        dve.wait_ge(g_in, 16)
        dve.tensor_scalar(t.sub_g[:, :], t.sub_g[:, :], 1.0 - LAM_INIT, None, ALU.mult)

    def vector_late(dve):
        for n in range(5):
            dve.wait_ge(flip_mm, n + 1)
            if n < 4:
                ins = dve.tensor_copy(t.band_p[:, 2 * n:2 * n + 2].rearrange("p h x -> p (h x)"), PS[:, 6 + n % 2])
            else:
                ins = dve.tensor_copy(t.sbias[:, 2], PS[:, 6, 0:PAST + NF])
            ins.then_inc(flip_ev, 1)
        dve.wait_ge(flip_ev, 5)
        dve.memset(t.band_p[0:CHUNK, :, 192:256], -1e30)

    part = Shared()
    part.sync_early, part.sync_rev, part.sync_late = sync_early, sync_rev, sync_late
    part.gpsimd, part.tensor = gpsimd, tensor
    part.scalar, part.vector_early, part.vector_late = scalar, vector_early, vector_late
    return part


def load_key_cache(sp, t, b):
    sp.dma_start(t.kc[:, b % 2, 0:8], t.ckd[b]).then_inc(t.kcache_in[b % 2], 16)
    sp.dma_start(t.kc[:, b % 2, 8:12], t.ckb[b]).then_inc(t.kcache_in[b % 2], 16)


def attention_prompt(nc, t):
    PS = t.PS
    GR = [(tile, g) for tile in range(2) for g in range(6)]
    with ExitStack() as ctx:
        sb = lambda n, s, d=F32: ctx.enter_context(nc.sbuf_tensor(n, s, d))
        sem = t.phase_semaphore
        L = sb("L", [P, 2, 2, 2, 256])
        mx = sb("mx", [P, 2, 4])
        lsum = sb("lsum", [P, 2, 4])
        A = sb("A", [P, 2, 4, 256])
        AT = sb("AT", [P, 2, 8, P])
        O = sb("O", [P, 2, DA])
        OBt = sb("OBt", [P, 2, DB])
        sq = sb("sq", [P, DA])
        ss = sb("ss", [P, HA])
        sc_mm, lg_done, exp_done, a_done = sem("sc_mm"), sem("lg_done"), sem("exp_done"), sem("a_done")
        at_mm, at_ev, pv_mm, o_done, o_norm, ot_mm, ot_ev = (sem(x) for x in
            ("at_mm", "at_ev", "pv_mm", "o_done", "o_norm", "ot_mm", "ot_ev"))
        dve_step = sem("prompt_dve")
        ms_done, rms_done, rows_zero = sem("ms_done"), sem("rms_done"), sem("rows_zero")
        block = ctx.enter_context(nc.Block())

        def heads(g, j, hh):
            return (slice(64 * j, 64 * j + 64), 2 * g + hh)


        @block.sync
        def _(sp):
            for b in range(2):
                load_key_cache(sp, t, b)
            sp.wait_ge(t.zeros_done, 1)
            fills = range(E * SLOTS, NBLK * SLOTS, P)
            for n in fills:
                r = min(P, NBLK * SLOTS - n)
                sp.dma_start(t.y_dram[n:n + r].rearrange("r (a d) -> r a d", a=4),
                             t.zeros[0:r, :].unsqueeze(1).to_broadcast([r, 4, D // 4])).then_inc(rows_zero, 16)
            sp.wait_ge(rows_zero, 16 * len(fills))

        @block.gpsimd
        def _(pool):
            for tile in range(2):
                pool.wait_ge(ms_done, tile + 1)
                pool.tensor_tensor(ss[:, :], ss[:, :], t.power[:, 0:HA], ALU.pow).then_inc(rms_done, 1)

        nmat = lambda tile, g: (2 if g < 4 else 4) * (tile + 1)

        @block.tensor
        def _(pe):
            def scores(n):
                tile, g = GR[n]
                S = P * (tile + 1)
                if n >= 2:
                    pe.wait_ge(lg_done, n - 1)
                for hh in range(2):
                    for j in range(2):
                        rows, u = heads(g, j, hh)
                        mm = pe.matmul(PS[:, 6 * (n % 2) + j, 256 * hh:256 * hh + S], t.qT[rows, u, P * tile:P * tile + P],
                                       t.kT[rows, u, 0:S], start=True, stop=True)
                mm.then_inc(sc_mm, 1)

            def turn(n):
                tile, g = GR[n]
                pe.wait_ge(a_done, n + 1)
                if n >= 1:
                    pe.wait_ge(at_ev, n)
                for m in range(nmat(tile, g)):
                    hd, st = m // (tile + 1), m % (tile + 1)
                    mm = pe.transpose(PS[:, 2 + m // 4, P * (m % 4):P * (m % 4) + P], A[:, n % 2, hd, P * st:P * st + P], t.ident[:, :])
                mm.then_inc(at_mm, 1)

            def values(n):
                tile, g = GR[n]
                pe.wait_ge(at_ev, n + 1)
                if n >= 1:
                    pe.wait_ge(o_done, n)
                for hd in range(2 if g < 4 else 4):
                    for st in range(tile + 1):
                        if g < 4:
                            v = t.V[:, st, P * (2 * g + hd):P * (2 * g + hd) + P]
                            o = PS[:, 4, P * hd:P * hd + P]
                        else:
                            h = 4 * (g - 4) + hd
                            v = t.V[:, st, DA + HD * h:DA + HD * h + HD]
                            o = PS[:, 4, HD * hd:HD * hd + HD]
                        mm = pe.matmul(o, AT[:, n % 2, hd * (tile + 1) + st], v, start=st == 0, stop=st == tile)
                mm.then_inc(pv_mm, 1)

            def turn_out(tile):
                for n, b in enumerate((0, 1, 2) if tile == 0 else (2, 0, 1)):
                    if b == 2:
                        pe.wait_ge(o_done, 6 * tile + 6)
                    else:
                        pe.wait_ge(o_norm, tile + 1)
                    if tile == 0 and n:
                        pe.wait_ge(ot_ev, n)
                    if tile == 1 and n == 0:
                        pe.wait_ge(ot_ev, 3)
                    for m in range(4):
                        src = O[:, tile, P * (4 * b + m):P * (4 * b + m) + P] if b < 2 else OBt[:, tile, P * m:P * m + P]
                        mm = pe.transpose(PS[:, 5 + n * tile, P * m:P * m + P], src, t.ident[:, :])
                    mm.then_inc(ot_mm, 1)

            scores(0)
            for n in range(len(GR) + 2):
                if n + 1 < len(GR):
                    scores(n + 1)
                if 1 <= n <= len(GR):
                    turn(n - 1)
                if n >= 2:
                    values(n - 2)
                if n == 12:
                    turn_out(0)
            turn_out(1)

        @block.vector
        def _(dve):
            link = make_link(dve, dve_step)

            def logits(n):
                tile, g = GR[n]
                S, x0 = P * (tile + 1), P * (1 - tile)
                dve.wait_ge(sc_mm, n + 1)
                if n >= 2:
                    dve.wait_ge(a_done, n - 1)
                for j in range(2):
                    bias = t.alibi_p[:, 2 * g:2 * g + 2, x0:256] if g < 4 else \
                        t.band_p[:, :, x0:256].rearrange("p (u j) x -> p u j x", j=2)[:, 2 * (g - 4):2 * (g - 4) + 2, j]
                    ins = dve.scalar_tensor_tensor(L[:, n % 2, j, :, 0:S], PS[:, 6 * (n % 2) + j].rearrange("p (h x) -> p h x", h=2)[:, :, 0:S],
                                                   SM, bias, ALU.mult, ALU.add)
                    link(ins)
                link(dve.tensor_reduce(mx[:, n % 2], L[:, n % 2, :, :, 0:S], AX.X, ALU.max))
                dve.tensor_scalar(mx[:, n % 2], mx[:, n % 2], -1.0, None, ALU.mult).then_inc(lg_done, 1)

            def weights(n):
                tile, g = GR[n]
                S = P * (tile + 1)
                dve.wait_ge(exp_done, n + 1)
                link(dve.reciprocal(lsum[:, n % 2], lsum[:, n % 2]))
                if n >= 2:
                    dve.wait_ge(at_mm, n - 1)
                if g < 4:
                    link(dve.tensor_scalar(lsum[:, n % 2, 2:4], lsum[:, n % 2, 2:4], t.neg_lam[:, 0:1], None, ALU.mult))
                    for hh in range(2):
                        link(dve.tensor_scalar(A[:, n % 2, hh, 0:S], L[:, n % 2, 0, hh, 0:S], lsum[:, n % 2, hh:hh + 1], None, ALU.mult))
                        ins = dve.scalar_tensor_tensor(A[:, n % 2, hh, 0:S], L[:, n % 2, 1, hh, 0:S], lsum[:, n % 2, 2 + hh:3 + hh],
                                                       A[:, n % 2, hh, 0:S], ALU.mult, ALU.add)
                        if hh == 0:
                            link(ins)
                else:
                    for m in range(4):
                        ins = dve.tensor_scalar(A[:, n % 2, m, 0:S], L[:, n % 2, m % 2, m // 2, 0:S],
                                                lsum[:, n % 2, 2 * (m % 2) + m // 2:2 * (m % 2) + m // 2 + 1], None, ALU.mult)
                ins.then_inc(a_done, 1)

            def squares(tile):
                dve.wait_ge(o_done, 6 * tile + 4)
                link(dve.tensor_tensor(sq[:, :], O[:, tile], O[:, tile], ALU.mult))
                link(dve.tensor_reduce(ss[:, :], sq[:, :].rearrange("p (h e) -> p h e", h=HA), AX.X, ALU.add))
                dve.tensor_scalar(ss[:, :], ss[:, :], 1.0 / P, EPS, ALU.mult, ALU.add).then_inc(ms_done, 1)

            def normalise(tile):
                dve.wait_ge(rms_done, tile + 1)
                o3 = O[:, tile].rearrange("p (h e) -> p h e", h=HA)
                link(dve.tensor_tensor(o3, o3, ss[:, :].unsqueeze(2).to_broadcast([P, HA, P]), ALU.mult))
                dve.wait_ge(o_done, 6 * tile + 6)
                dve.tensor_tensor(o3, o3, t.sub_g[:, :].unsqueeze(1).to_broadcast([P, HA, P]), ALU.mult).then_inc(o_norm, 1)

            for n in range(len(GR) + 1):
                if n < len(GR):
                    logits(n)
                if n >= 1:
                    weights(n - 1)
                if n == 8:
                    squares(0)
                if n == 10:
                    normalise(0)
            squares(1)
            normalise(1)

        @block.scalar
        def _(act):
            def out_turned(tile):
                for n, b in enumerate((0, 1, 2) if tile == 0 else (2, 0, 1)):
                    act.wait_ge(ot_mm, 3 * tile + n + 1)
                    dst = t.oaT[:, 4 * b:4 * b + 4] if b < 2 else t.obT[:, :]
                    act.copy(dst[:, :, P * tile:P * tile + P], PS[:, 5 + n * tile].rearrange("p (k q) -> p k q", k=4)).then_inc(ot_ev, 1)

            for n in range(len(GR) + 2):
                if n < len(GR):
                    tile, g = GR[n]
                    S = P * (tile + 1)
                    act.wait_ge(lg_done, n + 1)
                    for j in range(2):
                        for hh in range(2):
                            r = L[:, n % 2, j, hh, 0:S]
                            ins = act.activation(r, r, ACT.Exp, bias=mx[:, n % 2, 2 * j + hh:2 * j + hh + 1],
                                                 accum_out=lsum[:, n % 2, 2 * j + hh:2 * j + hh + 1])
                    ins.then_inc(exp_done, 1)
                if 1 <= n <= len(GR):
                    tile, g = GR[n - 1]
                    act.wait_ge(at_mm, n)
                    if n >= 3:
                        act.wait_ge(pv_mm, n - 2)
                    m = nmat(tile, g)
                    act.copy(AT[:, (n - 1) % 2, 0:m].rearrange("p m q -> p (m q)"),
                             PS[:, 2:4].rearrange("p b x -> p (b x)")[:, 0:P * m]).then_inc(at_ev, 1)
                if n >= 2:
                    tile, g = GR[n - 2]
                    act.wait_ge(pv_mm, n - 1)
                    dst = O[:, tile, 256 * g:256 * g + 256] if g < 4 else OBt[:, tile, 256 * (g - 4):256 * (g - 4) + 256]
                    act.copy(dst, PS[:, 4, 0:256]).then_inc(o_done, 1)
                if n == 12:
                    out_turned(0)
            out_turned(1)


def attention_sample(nc, t):
    PS = t.PS
    SW = PAST + NF
    with ExitStack() as ctx:
        sb = lambda n, s, d=F32: ctx.enter_context(nc.sbuf_tensor(n, s, d))
        sem = t.phase_semaphore
        kc, kcache_in = t.kc, t.kcache_in
        vc = sb("vc", [P, 2, NU, P])
        kcT = sb("kcT", [P, NU, P])
        qbd = sb("qbd", [P, 2, NU, 32])
        Ls = sb("Ls", [P, 2, 3, SW])
        Pn = sb("Pn", [P, 2, 3, P])
        mxs = sb("mxs", [P, 2, 3])
        sums = sb("sums", [P, 2, 3])
        PT = sb("PT", [P, 6, P])
        Os = sb("Os", [P, 3, NSEQ, P])
        On = sb("On", [P, NSEQ, P])
        sqs = sb("sqs", [P, NSEQ, P])
        sss = sb("sss", [P, NSEQ])
        vcache_in = [sem(f"vcache_in{i}") for i in range(2)]
        q_done, kct_mm, kct_ev, ssc_mm, slg_done, sexp_done, pn_done = (sem(x) for x in
            ("q_done", "kct_mm", "kct_ev", "ssc_mm", "slg_done", "sexp_done", "pn_done"))
        pt_mm, pt_ev, spv_mm, os_done, join_mm, join_ev, on_done, sot_mm, sot_ev = (sem(x) for x in
            ("pt_mm", "pt_ev", "spv_mm", "os_done", "join_mm", "join_ev", "on_done", "sot_mm", "sot_ev"))
        dve_step = sem("sample_dve")
        sms_done, srms_done = sem("sms_done"), sem("srms_done")
        block = ctx.enter_context(nc.Block())


        @block.gpsimd
        def _(pool):
            pool.wait_ge(sms_done, 1)
            pool.tensor_tensor(sss[:, :], sss[:, :], t.power[:, 0:NSEQ], ALU.pow).then_inc(srms_done, 1)

        @block.sync
        def _(sp):
            def load_keys(b):
                if b >= 2:
                    sp.wait_ge(kct_mm, 3 * b - 3)
                load_key_cache(sp, t, b)

            for b in range(NSEQ):
                if 1 <= b and b + 1 < NSEQ:
                    load_keys(b + 1)
                if b >= 2:
                    sp.wait_ge(spv_mm, b - 1)
                sp.dma_start(vc[:, b % 2, 0:8], t.cvd[b]).then_inc(vcache_in[b % 2], 16)
                sp.dma_start(vc[:, b % 2, 8:12], t.cvb[b]).then_inc(vcache_in[b % 2], 16)

        @block.tensor
        def _(pe):
            def turn_cache(b, groups=range(3)):
                pe.wait_ge(kcache_in[b % 2], 32 * (b // 2 + 1))
                for g in groups:
                    n = 3 * b + g
                    if n >= 2:
                        pe.wait_ge(kct_ev, n - 1)
                    for i in range(4):
                        mm = pe.transpose(PS[:, n % 2, P * i:P * i + P], kc[:, b % 2, 4 * g + i], t.ident[:, :])
                    mm.then_inc(kct_mm, 1)

            def scores(b):
                pe.wait_ge(q_done, b + 1)
                pe.wait_ge(kct_ev, 3 * b + 3)
                if b >= 2:
                    pe.wait_ge(slg_done, b - 1)
                for g in range(3):
                    for i in range(4):
                        u = 4 * g + i
                        rows = slice(32 * i, 32 * i + 32)
                        pe.matmul(PS[rows, 2 + 4 * (b % 2), SW * g:SW * g + PAST], qbd[:, b % 2, u], kcT[:, u], start=True, stop=True)
                        mm = pe.matmul(PS[rows, 2 + 4 * (b % 2), SW * g + PAST:SW * g + SW], qbd[:, b % 2, u],
                                       t.kT[:, u, 256 + NF * b:256 + NF * b + NF], start=True, stop=True)
                mm.then_inc(ssc_mm, 1)

            def turn_p(b):
                pe.wait_ge(pn_done, b + 1)
                if b >= 1:
                    pe.wait_ge(pt_ev, b)
                for m in range(6):
                    src = Ls[:, b % 2, m // 2, 0:PAST] if m % 2 == 0 else Pn[:, b % 2, m // 2]
                    mm = pe.transpose(PS[:, 3 + m // 4, P * (m % 4):P * (m % 4) + P], src, t.ident[:, :])
                mm.then_inc(pt_mm, 1)

            def values(b):
                pe.wait_ge(vcache_in[b % 2], 32 * (b // 2 + 1))
                pe.wait_ge(pt_ev, b + 1)
                if b >= 1:
                    pe.wait_ge(os_done, b)
                for g in range(3):
                    for i in range(4):
                        u = 4 * g + i
                        o = PS[32 * i:32 * i + 32, 5, P * g:P * g + P]
                        pe.matmul(o, PT[:, 2 * g, 32 * i:32 * i + 32], vc[:, b % 2, u], start=True, stop=False)
                        mm = pe.matmul(o, PT[:, 2 * g + 1, 32 * i:32 * i + 32], t.V[:, 2, P * u:P * u + P], start=False, stop=True)
                mm.then_inc(spv_mm, 1)

            turn_cache(0)
            scores(0)
            turn_cache(1)
            for b in range(NSEQ):
                if b + 1 < NSEQ:
                    scores(b + 1)
                turn_p(b)
                if b + 2 < NSEQ:
                    turn_cache(b + 2, range(2))
                values(b)
                if b + 2 < NSEQ:
                    turn_cache(b + 2, range(2, 3))
            pe.wait_ge(os_done, NSEQ)
            for n in range(2):
                for i in range(4):
                    mm = pe.transpose(PS[:, n, P * i:P * i + P], Os[:, 2, 4 * n + i], t.ident[:, :])
                mm.then_inc(sot_mm, 1)
            for n in range(2):
                for g in range(2):
                    mm = pe.matmul(PS[64 * g:64 * g + 64, 2 + n], t.join[:, :], Os[:, g, 4 * n:4 * n + 4].rearrange("p b e -> p (b e)"),
                                   start=True, stop=True)
                mm.then_inc(join_mm, 1)
            pe.wait_ge(on_done, 1)
            pe.wait_ge(sot_ev, 2)
            for n in range(2):
                for i in range(4):
                    mm = pe.transpose(PS[:, n, P * i:P * i + P], On[:, 4 * n + i], t.ident[:, :])
                mm.then_inc(sot_mm, 1)

        @block.scalar
        def _(act):
            def keys(b):
                for g in range(3):
                    n = 3 * b + g
                    act.wait_ge(kct_mm, n + 1)
                    if g == 0 and b >= 1:
                        act.wait_ge(ssc_mm, b)
                    act.copy(kcT[:, 4 * g:4 * g + 4].rearrange("p u s -> p (u s)"), PS[:, n % 2]).then_inc(kct_ev, 1)

            def exponents(b):
                act.wait_ge(slg_done, b + 1)
                for g in range(3):
                    r = Ls[:, b % 2, g]
                    ins = act.activation(r, r, ACT.Exp, bias=mxs[:, b % 2, g:g + 1], accum_out=sums[:, b % 2, g:g + 1])
                ins.then_inc(sexp_done, 1)

            keys(0)
            keys(1)
            exponents(0)
            for b in range(NSEQ):
                act.wait_ge(pt_mm, b + 1)
                if b >= 1:
                    act.wait_ge(spv_mm, b)
                act.copy(PT[:, :, :].rearrange("p m s -> p (m s)"), PS[:, 3:5].rearrange("p b x -> p (b x)")[:, 0:6 * P]).then_inc(pt_ev, 1)
                if b + 1 < NSEQ:
                    exponents(b + 1)
                if b + 2 < NSEQ:
                    keys(b + 2)
            for n in range(2):
                act.wait_ge(sot_mm, n + 1)
                ob = t.obT[:, :, 256 + 64 * n:320 + 64 * n].rearrange("p i (b q) -> p b i q", q=NF)
                src = PS[:, n].rearrange("p (b i j q) -> p b i j q", b=4, i=4, j=2)
                for b in range(4):
                    for j in range(2):
                        rows = slice(64 * j, 64 * j + 64)
                        ins = act.copy(ob[rows, b], src[rows, b, :, j])
                ins.then_inc(sot_ev, 1)
            for n in range(2):
                act.wait_ge(join_mm, n + 1)
                act.copy(On[:, 4 * n:4 * n + 4].rearrange("p b e -> p (b e)"), PS[:, 2 + n]).then_inc(join_ev, 1)
            for n in range(2):
                act.wait_ge(sot_mm, 3 + n)
                act.copy(t.oaT[:, :, 256 + 64 * n:320 + 64 * n].rearrange("p u (b q) -> p u b q", q=NF),
                         PS[:, n].rearrange("p (b u q) -> p u b q", b=4, u=HA))

        @block.vector
        def _(dve):
            link = make_link(dve, dve_step)
            link(dve.memset(qbd[:, :, :, :], 0.0))
            link(dve.memset(Pn[:, :, :, :], 0.0))

            def queries(b):
                if b >= 2:
                    dve.wait_ge(ssc_mm, b - 1)
                for j in range(2):
                    rows = slice(64 * j, 64 * j + 64)
                    ins = dve.tensor_copy(qbd[rows, b % 2, :, NF * j:NF * j + NF], t.qT[rows, :, 256 + NF * b:256 + NF * b + NF])
                ins.then_inc(q_done, 1)

            def logits(b):
                r = Ls[:, b % 2]
                dve.wait_ge(ssc_mm, b + 1)
                if b >= 2:
                    dve.wait_ge(pt_mm, b - 1)
                    link(dve.memset(Pn[:, b % 2, :, NF * (b - 2):NF * (b - 2) + NF], 0.0))
                link(dve.scalar_tensor_tensor(r.rearrange("p g s -> p (g s)"), PS[:, 2 + 4 * (b % 2), 0:3 * SW], SM,
                                              t.sbias[:, :, :].rearrange("p g s -> p (g s)"), ALU.mult, ALU.add))
                link(dve.tensor_reduce(mxs[:, b % 2], r, AX.X, ALU.max))
                dve.tensor_scalar(mxs[:, b % 2], mxs[:, b % 2], -1.0, None, ALU.mult).then_inc(slg_done, 1)

            queries(0)
            queries(1)
            logits(0)
            for b in range(NSEQ):
                dve.wait_ge(sexp_done, b + 1)
                dve.tensor_copy(Pn[:, b % 2, :, NF * b:NF * b + NF], Ls[:, b % 2, :, PAST:SW]).then_inc(pn_done, 1)
                link(dve.reciprocal(sums[:, b % 2], sums[:, b % 2]))
                if b + 1 < NSEQ:
                    logits(b + 1)
                if b + 2 < NSEQ:
                    queries(b + 2)
                dve.wait_ge(spv_mm, b + 1)
                dve.tensor_tensor(Os[:, :, b], PS[:, 5, 0:3 * P].rearrange("p (g e) -> p g e", g=3),
                                  sums[:, b % 2].unsqueeze(2).to_broadcast([P, 3, P]), ALU.mult).then_inc(os_done, 1)
            dve.wait_ge(join_ev, 2)
            link(dve.tensor_tensor(sqs[:, :, :], On[:, :, :], On[:, :, :], ALU.mult))
            link(dve.tensor_reduce(sss[:, :], sqs[:, :, :], AX.X, ALU.add))
            dve.tensor_scalar(sss[:, :], sss[:, :], 1.0 / P, EPS, ALU.mult, ALU.add).then_inc(sms_done, 1)
            dve.wait_ge(srms_done, 1)
            link(dve.tensor_tensor(On[:, :, :], On[:, :, :], sss[:, :].unsqueeze(2).to_broadcast([P, NSEQ, P]), ALU.mult))
            dve.tensor_tensor(On[:, :, :], On[:, :, :], t.sub_g[:, :].unsqueeze(1).to_broadcast([P, NSEQ, P]),
                              ALU.mult).then_inc(on_done, 1)


def projection_out(nc, t):
    PS = t.PS
    with ExitStack() as ctx:
        sb = lambda n, s, d=F32: ctx.enter_context(nc.sbuf_tensor(n, s, d))
        sem = t.phase_semaphore
        M = sb("M", [P, NT, D])
        MT = sb("MT", [P, KD, TOK])
        U2 = sb("U2", [P, NT, D])
        Wa = sb("Wa", [P, 2, KD, CW])
        Wb = sb("Wb", [P, 2, DB // P, CW])
        G = sb("gates_sb", [P, NT, 2, CW])
        gated = sb("gated", [P, 2, CW])
        gate1, shift2, scale2 = sb("gate1", [P, 2, D]), sb("shift2", [P, 2, D]), sb("scale2", [P, 2, D])
        ln1 = sb("ln1", [P, 2, D])
        ln = layer_norm_state(t, sb, sem, "_4")
        wa_in = [sem(f"wa_in{i}") for i in range(2)]
        wa2_in = [sem(f"wa2_in{i}") for i in range(2)]
        wb_in = [sem(f"wb_in{i}") for i in range(2)]
        gt_in = [sem(f"gt_in{i}") for i in range(NT)]
        vec_in = sem("vec_in")
        p_mm, m_ev, mt_mm, mt_ev, y_mm, y_ev = (sem(x) for x in ("p_mm", "m_ev", "mt_mm", "mt_ev", "y_mm", "y_ev"))
        u2_done, u2_out, u2t_mm, u2t_ev = (sem(x) for x in ("u2_done", "u2_out", "u2t_mm", "u2t_ev"))
        dve_step = sem("proj_dve")
        block = ctx.enter_context(nc.Block())
        jobs = [(c, n) for c in range(2) for n in range(NT)]

        @block.sync
        def _(sp):
            def load_gates(m):
                c, n = jobs[m]
                for g in range(2):
                    sp.dma_start(G[:, m % NT, g], t.gates[2 * g + c, P * n:P * n + P]).then_inc(gt_in[m % NT], 16)

            for c in range(2):
                cols = slice(CW * c, CW * c + CW)
                sp.dma_start(Wa[:, c, 0:4], half_of(t.p_a, 2 * c)).then_inc(wa_in[c], 16)
                sp.dma_start(Wa[:, c, 4:8], half_of(t.p_a, 2 * c + 1)).then_inc(wa2_in[c], 16)
                sp.dma_start(Wb[:, c], t.p_b[0].rearrange("(k p) n -> p k n", p=P)[:, :, cols]).then_inc(wb_in[c], 16)
                if c == 0:
                    for m in range(NT):
                        load_gates(m)
            for n in range(2):
                sp.dma_start(t.X[:, n], t.x_prompt[0, P * n:P * n + P]).then_inc(vec_in, 16)
            sp.dma_start(t.X[:, 2], t.x_sample.rearrange("b s d -> (b s) d")).then_inc(vec_in, 16)
            t.load_mod(sp, gate1, 2, vec_in)
            sp.dma_start(ln1[:, 0], t.ln1_g.to_broadcast([P, D])).then_inc(vec_in, 16)
            sp.dma_start(ln1[:, 1], t.ln1_b.to_broadcast([P, D])).then_inc(vec_in, 16)
            t.load_mod(sp, shift2, 3, vec_in)
            t.load_mod(sp, scale2, 4, vec_in)
            sp.dma_start(t.wr[:, :, :], t.w_router[0].rearrange("(p k) e -> p k e", k=KD)).then_inc(t.wr_in, 16)
            for m in range(NT, 2 * NT):
                sp.wait_ge(m_ev, m - NT + 1)
                load_gates(m)
            for c in range(2):
                sp.wait_ge(p_mm, NT * (c + 1))
                sp.dma_start(Wa[:, c, 0:4], half_of(t.w_out, 2 * c)).then_inc(wa_in[c], 16)
                sp.dma_start(Wa[:, c, 4:8], half_of(t.w_out, 2 * c + 1)).then_inc(wa2_in[c], 16)
            for n in range(NT):
                sp.wait_ge(u2_done, n + 1)
                sp.dma_start(t.h_dram[P * n:P * n + P], U2[:, n]).then_inc(u2_out, 16)
            sp.wait_ge(u2_out, 16 * NT)

        @block.tensor
        def _(pe):
            def project(m):
                c, n = jobs[m]
                if m >= 2:
                    pe.wait_ge(m_ev, m - 1)
                q = slice(P * n, P * n + P)
                pe.wait_ge(wa_in[c], 16)
                for k in range(KD):
                    if k == 4:
                        pe.wait_ge(wa2_in[c], 16)
                    pe.matmul(PS[:, 2 * (m % 2)], t.oaT[:, k, q], Wa[:, c, k], start=k == 0, stop=k == KD - 1)
                pe.wait_ge(wb_in[c], 16)
                for k in range(DB // P):
                    mm = pe.matmul(PS[:, 2 * (m % 2) + 1], t.obT[:, k, q], Wb[:, c, k], start=k == 0, stop=k == DB // P - 1)
                mm.then_inc(p_mm, 1)

            def turn(n):
                pe.wait_ge(m_ev, NT + 1 + n)
                for half in range(2):
                    j = 2 * n + half
                    if j >= 2:
                        pe.wait_ge(mt_ev, j - 1)
                    for k in range(4):
                        mm = pe.transpose(PS[:, 4 + j % 2, P * k:P * k + P], M[:, n, P * (4 * half + k):P * (4 * half + k) + P], t.ident[:, :])
                    mm.then_inc(mt_mm, 1)

            def out(n):
                pe.wait_ge(mt_ev, 2 * n + 2)
                if n < 2:
                    pe.wait_ge(m_ev, NT + 2 + n)
                else:
                    pe.wait_ge(y_ev, n - 1)
                for c in range(2):
                    pe.wait_ge(wa_in[c], 32)
                    pe.wait_ge(wa2_in[c], 32)
                    for k in range(KD):
                        mm = pe.matmul(PS[:, 2 * (n % 2) + c], MT[:, k, P * n:P * n + P], Wa[:, c, k], start=k == 0, stop=k == KD - 1)
                mm.then_inc(y_mm, 1)

            def turn_u2(n):
                pe.wait_ge(u2_done, n + 1)
                for half in range(2):
                    j = 2 * n + half
                    if j >= 2:
                        pe.wait_ge(u2t_ev, j - 1)
                    for k in range(4):
                        mm = pe.transpose(PS[:, 4 + j % 2, P * k:P * k + P], U2[:, n, P * (4 * half + k):P * (4 * half + k) + P], t.ident[:, :])
                    mm.then_inc(u2t_mm, 1)

            for m in range(2 * NT):
                project(m)
                if m > NT:
                    turn(m - NT - 1)
            out(0)
            turn(2)
            for n in range(1, NT):
                out(n)
            for n in range(NT):
                turn_u2(n)

        @block.gpsimd
        def _(pool):
            rsqrts(pool, ln, *range(2 * NT))

        @block.scalar
        def _(act):
            for mm, ev, dst in ((mt_mm, mt_ev, MT), (u2t_mm, u2t_ev, t.hT)):
                for j in range(6):
                    act.wait_ge(mm, j + 1)
                    act.copy(dst[:, 4 * (j % 2):4 * (j % 2) + 4, P * (j // 2):P * (j // 2) + P],
                             PS[:, 4 + j % 2].rearrange("p (k q) -> p k q", k=4)).then_inc(ev, 1)

        @block.vector
        def _(dve):
            link = make_link(dve, dve_step)
            for m, (c, n) in enumerate(jobs):
                dve.wait_ge(p_mm, m + 1)
                dve.wait_ge(gt_in[m % NT], 32 * (m // NT + 1))
                link(dve.tensor_tensor(gated[:, :, :], PS[:, 2 * (m % 2):2 * (m % 2) + 2], G[:, m % NT], ALU.mult))
                link(dve.tensor_tensor(M[:, n, CW * c:CW * c + CW], gated[:, 0], gated[:, 1], ALU.add))
                dve.sem_inc(m_ev, 1)
            dve.wait_ge(vec_in, 16 * (NT + 8))
            for n in range(NT):
                dve.wait_ge(y_mm, n + 1)
                dve.wait_ge(mt_mm, 2 * n + 2)
                r = M[:, n]
                y = PS[:, 2 * (n % 2):2 * (n % 2) + 2].rearrange("p b x -> p (b x)")
                link(dve.tensor_tensor(r, y, gate1[:, n // 2], ALU.mult))
                dve.sem_inc(y_ev, 1)
                link(dve.scalar_tensor_tensor(r, t.X[:, n], ALPHA, r, ALU.mult, ALU.add))
                layer_norm(dve, link, ln, t.X[:, n], r)
                link(dve.tensor_tensor(t.X[:, n], t.X[:, n], ln1[:, 0], ALU.mult))
                link(dve.tensor_tensor(t.X[:, n], t.X[:, n], ln1[:, 1], ALU.add))
                layer_norm(dve, link, ln, r, t.X[:, n])
                link(dve.scalar_tensor_tensor(r, scale2[:, n // 2], 1.0, r, ALU.add, ALU.mult))
                dve.tensor_tensor(U2[:, n].rearrange("r (k p) -> r p k", k=KD), r.rearrange("r (p k) -> r p k", k=KD),
                                  shift2[:, n // 2].rearrange("r (p k) -> r p k", k=KD), ALU.add).then_inc(u2_done, 1)


def load_expert(sp, t, e, i):
    s = t.wexp_in[i]
    sp.dma_start(t.W13[:, i, 0], t.w1v[e] if isinstance(e, int) else t.w1v[bass.ds(e, 1)].rearrange("e p k n -> (e p) k n")).then_inc(s, 16)
    sp.dma_start(t.W13[:, i, 1], t.w3v[e] if isinstance(e, int) else t.w3v[bass.ds(e, 1)].rearrange("e p k n -> (e p) k n")).then_inc(s, 16)
    sp.dma_start(t.W2[:, i], t.w2v[e] if isinstance(e, int) else t.w2v[bass.ds(e, 1)].rearrange("e p k n -> (e p) k n")).then_inc(s, 16)


def routing(nc, t):
    PS = t.PS
    with ExitStack() as ctx:
        sb = lambda n, s, d=F32: ctx.enter_context(nc.sbuf_tensor(n, s, d))
        sem = t.phase_semaphore
        wr, wr_in = t.wr, t.wr_in
        ws13 = sb("ws13", [P, KD, 2, F])
        ws2 = sb("ws2_sb", [P, 2, D])
        ebias = sb("ebias", [P, E])
        sc = sb("sc", [P, NT, E])
        bi = sb("bi", [P, E])
        g8 = sb("g8", [P, NG, 8])
        gs, gm, gn = sb("gs", [P, NG]), sb("gm", [P, NG]), sb("gn", [P, NG])
        cmp, tie, gi = sb("cmp", [P, NG, NG]), sb("tie", [P, NG, NG]), sb("gi", [P, NG, NG], I32)
        t8, i8, i8f = sb("t8", [P, 8]), sb("i8", [P, 8], U32), sb("i8f", [P, 8])
        oh = sb("oh", [P, NT, TOPK, E])
        tmp = sb("tmp", [P, TOPK, E])
        mask = sb("mask", [P, NT, E], F16)
        wsum = sb("wsum", [P, 1])
        tri, ones = sb("tri", [P, P], F16), sb("ones", [P, P], F16)
        tri_f = sb("tri_f", [P, P])
        io_i, io = sb("io_i", [P, P], I32), sb("io", [P, P])
        tk_i, tk = sb("tk_i", [P, NT], I32), sb("tk", [P, NT])
        cnt, ext, inc, base = sb("cnt", [P, E]), sb("ext", [P, E]), sb("inc", [P, E]), sb("base", [P, E])
        one_e = sb("one_e", [P, E])
        code, code2 = sb("code", [P, E]), sb("code2", [P, E])
        ck, si, ci = sb("ck", [P, TOPK]), sb("si", [P, TOPK], I32), sb("ci", [P, TOPK], I32)
        sf, cf = sb("sf", [P, TOPK]), sb("cf", [P, TOPK])
        SL = sb("SL", [P, 2, TOPK, SLOTS], F16)
        CB = sb("CB", [P, 2, TOPK, NBLK], F16)
        CBf = sb("CBf", [P, TOPK, NBLK])
        sh_g, sh_h, sh_T = sb("sh_g", [P, 2, F]), sb("sh_h", [P, NT, F]), sb("sh_T", [P, 2, 2, P])
        SB = (4, 5, 7)
        ws_in, eb_in = sem("ws_in"), sem("eb_in")
        r_mm, sig_done, mask_done, rank_mm, cnt_mm, code_done, list_mm, iota_done = (sem(x) for x in
            ("r_mm", "sig_done", "mask_done", "rank_mm", "cnt_mm", "code_done", "list_mm", "riota_done"))
        s_mm, s_silu, s_hid, st_mm, st_ev, sy_mm, sy_ev, rc_done = (sem(x) for x in
            ("s_mm", "s_silu", "s_hid", "st_mm", "st_ev", "sy_mm", "sy_ev", "rc_done"))
        dve_step = sem("route_dve")
        block = ctx.enter_context(nc.Block())

        @block.sync
        def _(sp):
            sp.dma_start(ebias[:, :], t.e_bias.to_broadcast([P, E])).then_inc(eb_in, 16)
            sp.dma_start(ws13[:, :, 0], t.ws1[0].rearrange("(p k) n -> p k n", k=KD)).then_inc(ws_in, 16)
            sp.dma_start(ws13[:, :, 1], t.ws3[0].rearrange("(p k) n -> p k n", k=KD)).then_inc(ws_in, 16)
            sp.dma_start(ws2[:, :, :], t.ws2[0].rearrange("(p k) n -> p k n", k=2)).then_inc(ws_in, 16)
            for i in range(WB):
                load_expert(sp, t, i, i)
            t.load_mod(sp, t.vec, 5, t.vec_in)
            sp.dma_start(t.vec[:, 2], t.ln2_g.to_broadcast([P, D])).then_inc(t.vec_in, 16)
            sp.dma_start(t.vec[:, 3], t.ln2_b.to_broadcast([P, D])).then_inc(t.vec_in, 16)

        @block.gpsimd
        def _(pool):
            pool.iota(io_i[:, :], pattern=[[1, P]], base=0, channel_multiplier=0).then_inc(iota_done, 1)
            pool.iota(tk_i[:, :], pattern=[[P, NT]], base=0, channel_multiplier=1).then_inc(iota_done, 1)
            pool.iota(gi[:, :, :], pattern=[[1, NG], [-1, NG]], base=0, channel_multiplier=0).then_inc(iota_done, 1)

        @block.tensor
        def _(pe):
            pe.wait_ge(wr_in, 16)
            for n in range(NT):
                for k in range(KD):
                    mm = pe.matmul(PS[:, n, 0:E], t.hT[:, k, P * n:P * n + P], wr[:, k], start=k == 0, stop=k == KD - 1)
                mm.then_inc(r_mm, 1)
            pe.wait_ge(ws_in, 48)

            def shared_up(n):
                for k in range(KD):
                    mm = pe.matmul(PS[:, SB[n]], t.hT[:, k, P * n:P * n + P], ws13[:, k].rearrange("p j n -> p (j n)"),
                                   start=k == 0, stop=k == KD - 1)
                mm.then_inc(s_mm, 1)

            def rank(n):
                pe.wait_ge(mask_done, n + 1)
                for m in range(n):
                    pe.matmul(PS[:, n, 64:64 + E], ones[:, :], mask[:, m], start=m == 0, stop=False)
                pe.matmul(PS[:, n, 64:64 + E], tri[:, :], mask[:, n], start=n == 0, stop=True).then_inc(rank_mm, 1)

            shared_up(0)
            shared_up(1)
            rank(0)
            shared_up(2)
            rank(1)
            rank(2)
            for m in range(NT):
                mm = pe.matmul(PS[:, 3, 0:E], ones[:, :], mask[:, m], start=m == 0, stop=m == NT - 1)
            mm.then_inc(cnt_mm, 1)
            for n in range(NT):
                pe.wait_ge(s_hid, NT)
                if n:
                    pe.wait_ge(st_ev, n)
                for j in range(2):
                    mm = pe.transpose(PS[:, 6, P * j:P * j + P], sh_h[:, n, P * j:P * j + P], t.ident[:, :])
                mm.then_inc(st_mm, 1)
                pe.wait_ge(st_ev, n + 1)
                if n:
                    pe.wait_ge(sy_ev, n)
                for c in range(2):
                    for j in range(2):
                        mm = pe.matmul(PS[:, 4 + 3 * c], sh_T[:, n % 2, j], ws2[:, j, CW * c:CW * c + CW], start=j == 0, stop=j == 1)
                mm.then_inc(sy_mm, 1)
                pe.wait_ge(code_done, n + 1)
                for k in range(TOPK):
                    mm = pe.matmul(PS[0:SLOTS, 5, 0:NBLK], SL[:, n % 2, k], CB[:, n % 2, k], start=n + k == 0, stop=n == NT - 1 and k == TOPK - 1)
                mm.then_inc(list_mm, 1)

        @block.scalar
        def _(act):
            for n in range(NT):
                act.wait_ge(r_mm, n + 1)
                act.activation(sc[:, n], PS[:, n, 0:E], ACT.Sigmoid).then_inc(sig_done, 1)
            for n in range(NT):
                act.wait_ge(s_mm, n + 1)
                if n >= 2:
                    act.wait_ge(s_hid, n - 1)
                act.activation(sh_g[:, n % 2], PS[:, SB[n], 0:F], ACT.Silu).then_inc(s_silu, 1)
            for n in range(NT):
                act.wait_ge(st_mm, n + 1)
                if n >= 2:
                    act.wait_ge(sy_mm, n - 1)
                act.copy(sh_T[:, n % 2].rearrange("p j q -> p (j q)"), PS[:, 6, 0:2 * P]).then_inc(st_ev, 1)
                act.wait_ge(sy_mm, n + 1)
                for c in range(2):
                    ins = act.copy(t.acc[:, n, CW * c:CW * c + CW], PS[:, 4 + 3 * c])
                ins.then_inc(sy_ev, 1)

        @block.vector
        def _(dve):
            link = make_link(dve, dve_step)
            dve.wait_ge(iota_done, 3)
            link(dve.tensor_copy(io[:, :], io_i[:, :]))
            link(dve.tensor_copy(tk[:, :], tk_i[:, :]))
            link(dve.tensor_scalar(tie[:, :, :], gi[:, :, :], 0.0, None, ALU.is_gt))
            link(dve.tensor_scalar(tri[:, :], io[:, :], tk[:, 0:1], None, ALU.is_gt))
            link(dve.memset(ones[:, :], 1.0))
            link(dve.memset(one_e[:, :], 1.0))
            dve.wait_ge(eb_in, 16)

            def hidden(n):
                dve.wait_ge(s_silu, n + 1)
                dve.tensor_tensor(sh_h[:, n].rearrange("r (j p) -> r p j", j=2), sh_g[:, n % 2].rearrange("r (p j) -> r p j", j=2),
                                  PS[:, SB[n], F:2 * F].rearrange("r (p j) -> r p j", j=2), ALU.mult).then_inc(s_hid, 1)

            for n in range(NT):
                dve.wait_ge(sig_done, n + 1)
                link(dve.tensor_tensor(bi[:, :], sc[:, n], ebias[:, :], ALU.add))
                for g in range(NG):
                    ins = dve.max(g8[:, g], bi[:, 8 * g:8 * g + 8])
                link(ins)
                link(dve.tensor_tensor(gs[:, :], g8[:, :, 0], g8[:, :, 1], ALU.add))
                mine = gs[:, :].unsqueeze(2).to_broadcast([P, NG, NG])
                other = gs[:, :].unsqueeze(1).to_broadcast([P, NG, NG])
                link(dve.tensor_tensor(cmp[:, :, :], other, mine, ALU.is_equal))
                link(dve.tensor_tensor(cmp[:, :, :], cmp[:, :, :], tie[:, :, :], ALU.mult))
                link(dve.tensor_reduce(gm[:, :], cmp[:, :, :], AX.X, ALU.add))
                link(dve.tensor_tensor(cmp[:, :, :], other, mine, ALU.is_gt))
                link(dve.tensor_reduce(gn[:, :], cmp[:, :, :], AX.X, ALU.add))
                link(dve.tensor_tensor(gm[:, :], gm[:, :], gn[:, :], ALU.add))
                link(dve.tensor_scalar(gm[:, :], gm[:, :], float(TOPG), None, ALU.is_lt))
                link(dve.tensor_scalar(gn[:, :], gm[:, :], -1.0, 1e30, ALU.add, ALU.mult))
                b3 = bi[:, :].rearrange("p (g e) -> p g e", g=NG)
                link(dve.tensor_tensor(b3, b3, gm[:, :].unsqueeze(2).to_broadcast([P, NG, 8]), ALU.mult))
                link(dve.tensor_tensor(b3, b3, gn[:, :].unsqueeze(2).to_broadcast([P, NG, 8]), ALU.add))
                link(dve.max(t8[:, :], bi[:, :]))
                link(dve.max_index(i8[:, :], t8[:, :], bi[:, :]))
                link(dve.tensor_copy(i8f[:, :], i8[:, :]))
                link(dve.tensor_tensor(oh[:, n], io[:, 0:E].unsqueeze(1).to_broadcast([P, TOPK, E]),
                                       i8f[:, :].unsqueeze(2).to_broadcast([P, TOPK, E]), ALU.is_equal))
                with nc.allow_low_precision("a count of at most one"):
                    dve.tensor_reduce(mask[:, n], oh[:, n].rearrange("p k e -> p e k"), AX.X, ALU.add).then_inc(mask_done, 1)
                link(dve.tensor_tensor(tmp[:, :, :], oh[:, n], sc[:, n].unsqueeze(1).to_broadcast([P, TOPK, E]), ALU.mult))
                link(dve.tensor_reduce(t.wts[:, n], tmp[:, :, :], AX.X, ALU.add))
                link(dve.tensor_reduce(wsum[:, :], t.wts[:, n], AX.X, ALU.add))
                link(dve.reciprocal(wsum[:, :], wsum[:, :]))
                link(dve.tensor_scalar(t.wts[:, n], t.wts[:, n], wsum[:, 0:1], ROUTED_SCALE, ALU.mult, ALU.mult))
            for n in range(NT):
                hidden(n)
            dve.wait_ge(cnt_mm, 1)
            link(dve.tensor_copy(cnt[:, :], PS[:, 3, 0:E]))
            link(dve.tensor_scalar(ext[:, :], cnt[:, :], float(SLOTS), None, ALU.is_gt))
            for m in range(2, TOK // SLOTS):
                link(dve.scalar_tensor_tensor(ext[:, :], cnt[:, :], float(SLOTS * m), ext[:, :], ALU.is_gt, ALU.add))
            link(dve.tensor_tensor_scan(inc[:, :], one_e[:, :], ext[:, :], 0.0, ALU.mult, ALU.add))
            link(dve.memset(t.ov[:, 0:1], 0))
            link(dve.tensor_copy(t.ov[:, 1:E + 1], inc[0:1, :]))
            link(dve.tensor_tensor(base[:, :], inc[:, :], ext[:, :], ALU.subtract))
            link(dve.tensor_tensor(base[:, :], base[:, :], io[:, 0:E], ALU.subtract))
            link(dve.tensor_scalar(base[:, :], base[:, :], float(E - 1), None, ALU.add))
            for n in range(NT):
                dve.wait_ge(rank_mm, n + 1)
                link(dve.tensor_copy(code2[:, :], PS[:, n, 64:64 + E]))
                link(dve.scalar_tensor_tensor(code[:, :], code2[:, :], float(SLOTS), base[:, :], ALU.is_ge, ALU.mult))
                link(dve.tensor_tensor(code[:, :], code[:, :], io[:, 0:E], ALU.add))
                link(dve.scalar_tensor_tensor(code[:, :], code[:, :], float(SLOTS), code2[:, :], ALU.mult, ALU.add))
                link(dve.tensor_tensor(tmp[:, :, :], oh[:, n], code[:, :].unsqueeze(1).to_broadcast([P, TOPK, E]), ALU.mult))
                link(dve.tensor_reduce(ck[:, :], tmp[:, :, :], AX.X, ALU.add))
                link(dve.tensor_copy(t.rows[:, n], ck[:, :]))
                link(dve.tensor_scalar(si[:, :], t.rows[:, n], SLOTS - 1, None, ALU.bitwise_and))
                link(dve.tensor_scalar(ci[:, :], t.rows[:, n], 6, None, ALU.logical_shift_right))
                link(dve.tensor_copy(sf[:, :], si[:, :]))
                link(dve.tensor_copy(cf[:, :], ci[:, :]))
                if n >= 2:
                    dve.wait_ge(list_mm, n - 1)
                link(dve.tensor_tensor(SL[:, n % 2], io[:, 0:SLOTS].unsqueeze(1).to_broadcast([P, TOPK, SLOTS]),
                                       sf[:, :].unsqueeze(2).to_broadcast([P, TOPK, SLOTS]), ALU.is_equal))
                link(dve.tensor_tensor(CBf[:, :, :], io[:, 0:NBLK].unsqueeze(1).to_broadcast([P, TOPK, NBLK]),
                                       cf[:, :].unsqueeze(2).to_broadcast([P, TOPK, NBLK]), ALU.is_equal))
                dve.tensor_scalar(CB[:, n % 2], CBf[:, :, :], tk[:, n:n + 1], None, ALU.mult).then_inc(code_done, 1)
            dve.wait_ge(list_mm, NT)
            link(dve.memset(t.tokens[:, NBLK:NBLK + 1], 0))
            dve.tensor_copy(t.tokens[:, 0:NBLK], PS[0:SLOTS, 5, 0:NBLK])


def experts(nc, t):
    PS = t.PS
    with ExitStack() as ctx:
        sb = lambda n, s, d=F32: ctx.enter_context(nc.sbuf_tensor(n, s, d))
        sem = t.phase_semaphore
        XG = sb("XG", [SLOTS, WB, D])
        XT = sb("XT", [P, 2, KD, SLOTS])
        sg, hid, hidT = sb("sg", [SLOTS, 2, F]), sb("hid", [SLOTS, 2, F]), sb("hidT", [P, 2, 2, SLOTS])
        Y = sb("Y", [P, 2, CW])
        ix = sb("ix", [SLOTS, WB], I32)
        XGo, XTo = sb("XGo", [SLOTS, D]), sb("XTo", [P, KD, SLOTS])
        sgo, hido, hidTo = sb("sgo", [SLOTS, F]), sb("hido", [SLOTS, F]), sb("hidTo", [P, 2, SLOTS])
        Yo = sb("Yo", [P, CW])
        ixo = sb("ixo", [SLOTS, 1], I32)
        g_in = [sem(f"g_in{i}") for i in range(WB)]
        y_out = [sem(f"y_out{i}") for i in range(2)]
        ix_done, xt_mm, xt_ev, h_mm, silu_done, hid_done, ht_mm, ht_ev, yy_mm, yy_ev = (sem(x) for x in
            ("ix_done", "xt_mm", "xt_ev", "h_mm", "esilu_done", "hid_done", "ht_mm", "ht_ev", "yy_mm", "yy_ev"))
        o_ix, o_in, o_xt, o_xe, o_h, o_silu, o_hid, o_ht, o_he, o_y, o_ye, o_out = (sem(x) for x in
            ("o_ix", "o_in", "o_xt", "o_xe", "o_h", "o_silu", "o_hid", "o_ht", "o_he", "o_y", "o_ye", "o_out"))
        waited = sem("waited")
        block = ctx.enter_context(nc.Block())

        def at(it, i, off=0):
            return it * WB + (i + off)

        def extra(eng, e, step):
            lo = eng.value_load(t.ov[0:1, bass.ds(e, 1)], min_val=0, max_val=XB)
            hi = eng.value_load(t.ov[0:1, bass.ds(e + 1, 1)], min_val=0, max_val=XB)
            with eng.If(lo < hi):
                with eng.Fori(lo, hi) as g:
                    step(g)

        def once_above(eng, semaphore, count):
            if not isinstance(count, int) or count > 0:
                eng.wait_ge(semaphore, count)

        def stand_alone(eng):
            eng.sem_inc(waited, 1)

        def loops(eng, body):
            for i in range(WB):
                body(0, i, False)
            with eng.Fori(1, E // WB - 1) as it:
                for i in range(WB):
                    body(it, i, False)
            for i in range(WB):
                body(E // WB - 1, i, True)

        @block.sync
        def _(sp):
            def store_extra(g):
                sp.wait_ge(o_ye, g + 2)
                for h in range(2):
                    sp.dma_start(t.y_dram[bass.ds((g + E) * SLOTS, SLOTS), CW * h:CW * h + CW], Yo[64 * h:64 * h + 64, :]).then_inc(o_out, 16)

            def body(it, i, last):
                sp.wait_ge(yy_ev, at(it, i, 1))
                for h in range(2):
                    sp.dma_start(t.y_dram[bass.ds(at(it, i) * SLOTS, SLOTS), CW * h:CW * h + CW], Y[64 * h:64 * h + 64, i % 2]).then_inc(y_out[i % 2], 16)
                extra(sp, at(it, i), store_extra)
                if not last:
                    load_expert(sp, t, at(it, i, WB), i)
            sp.sem_inc(o_out, 32)
            loops(sp, body)
            for i in range(2):
                sp.wait_ge(y_out[i], 32 * E // 2)
            total = sp.value_load(t.ov[0:1, E:E + 1], min_val=0, max_val=XB)
            sp.wait_ge(o_out, total * 32 + 32)
            stand_alone(sp)

        @block.gpsimd
        def _(pool):
            def gather(e, i, n):
                pool.tensor_copy(ix[:, i:i + 1], t.tokens[:, bass.ds(e, 1)]).then_inc(ix_done, 1)
                pool.wait_ge(ix_done, n)
                stand_alone(pool)
                pool.indirect_dma_start(XG[:, i], None, t.h_dram, bass.IndirectOffsetOnAxis(ap=ix[:, i:i + 1], axis=0)).then_inc(g_in[i], 16)

            def gather_next(g):
                pool.wait_ge(o_xt, g + 1)
                pool.tensor_copy(ixo[:, 0:1], t.tokens[:, bass.ds(g + E + 1, 1)]).then_inc(o_ix, 1)
                pool.wait_ge(o_ix, g + 2)
                stand_alone(pool)
                pool.indirect_dma_start(XGo[:, :], None, t.h_dram, bass.IndirectOffsetOnAxis(ap=ixo[:, 0:1], axis=0)).then_inc(o_in, 16)

            for i in range(WB):
                gather(i, i, i + 1)
            pool.tensor_copy(ixo[:, 0:1], t.tokens[:, E:E + 1]).then_inc(o_ix, 1)
            pool.wait_ge(o_ix, 1)
            pool.indirect_dma_start(XGo[:, :], None, t.h_dram, bass.IndirectOffsetOnAxis(ap=ixo[:, 0:1], axis=0)).then_inc(o_in, 16)

            def body(it, i, last):
                extra(pool, at(it, i), gather_next)
                if not last:
                    pool.wait_ge(xt_mm, at(it, i, 1))
                    gather(at(it, i, WB), i, at(it, i, WB + 1))
            loops(pool, body)

        @block.tensor
        def _(pe):
            def turn(n, i, it):
                pe.wait_ge(g_in[i], (it + 1) * 16)
                once_above(pe, xt_ev, n)
                stand_alone(pe)
                for k in range(KD):
                    mm = pe.transpose(PS[:, 0, SLOTS * k:SLOTS * k + SLOTS], XG[:, i, P * k:P * k + P], t.ident[0:SLOTS, 0:SLOTS])
                mm.then_inc(xt_mm, 1)

            def up(n, i, it):
                pe.wait_ge(t.wexp_in[i], (it + 1) * 48)
                pe.wait_ge(xt_ev, n + 1)
                once_above(pe, hid_done, n - 1)
                for k in range(KD):
                    for h in range(2):
                        mm = pe.matmul(PS[64 * h:64 * h + 64, 2 + i % 2, 0:F], XT[:, i % 2, k], t.W13[:, i, h, k], start=k == 0, stop=k == KD - 1)
                mm.then_inc(h_mm, 1)

            def turn_extra():
                for k in range(KD):
                    mm = pe.transpose(PS[:, 1, SLOTS * k:SLOTS * k + SLOTS], XGo[:, P * k:P * k + P], t.ident[0:SLOTS, 0:SLOTS])
                mm.then_inc(o_xt, 1)

            def extra_block(i):
                def step(g):
                    pe.wait_ge(o_xe, g + 1)
                    pe.wait_ge(o_ye, g + 1)
                    for k in range(KD):
                        for h in range(2):
                            mm = pe.matmul(PS[64 * h:64 * h + 64, 7, 0:F], XTo[:, k], t.W13[:, i, h, k], start=k == 0, stop=k == KD - 1)
                    mm.then_inc(o_h, 1)
                    pe.wait_ge(o_in, (g + 2) * 16)
                    stand_alone(pe)
                    turn_extra()
                    pe.wait_ge(o_hid, g + 1)
                    stand_alone(pe)
                    for j in range(2):
                        mm = pe.transpose(PS[:, 7, SLOTS * j:SLOTS * j + SLOTS], hido[:, P * j:P * j + P], t.ident[0:SLOTS, 0:SLOTS])
                    mm.then_inc(o_ht, 1)
                    pe.wait_ge(o_he, g + 1)
                    for j in range(2):
                        for h in range(2):
                            mm = pe.matmul(PS[64 * h:64 * h + 64, 7], hidTo[:, j], t.W2[:, i, j, CW * h:CW * h + CW], start=j == 0, stop=j == 1)
                    mm.then_inc(o_y, 1)
                return step

            def body(it, i, last):
                n = at(it, i)
                nxt = (it + (i + 1) // WB, (i + 1) % WB)
                nx2 = (it + (i + 2) // WB, (i + 2) % WB)
                if not last or i + 1 < WB:
                    up(at(it, i, 1), nxt[1], nxt[0])
                pe.wait_ge(hid_done, n + 1)
                once_above(pe, ht_ev, n)
                stand_alone(pe)
                for j in range(2):
                    mm = pe.transpose(PS[:, 4, SLOTS * j:SLOTS * j + SLOTS], hid[:, i % 2, P * j:P * j + P], t.ident[0:SLOTS, 0:SLOTS])
                mm.then_inc(ht_mm, 1)
                if not last or i + 2 < WB:
                    turn(at(it, i, 2), nx2[1], nx2[0])
                pe.wait_ge(ht_ev, n + 1)
                once_above(pe, yy_ev, at(it, i, -1))
                for j in range(2):
                    for h in range(2):
                        mm = pe.matmul(PS[64 * h:64 * h + 64, 5 + i % 2], hidT[:, i % 2, j], t.W2[:, i, j, CW * h:CW * h + CW], start=j == 0, stop=j == 1)
                mm.then_inc(yy_mm, 1)
                extra(pe, n, extra_block(i))

            turn(0, 0, 0)
            turn(1, 1, 0)
            up(0, 0, 0)
            pe.wait_ge(o_in, 16)
            turn_extra()
            loops(pe, body)

        @block.scalar
        def _(act):
            def evict(n, i):
                act.wait_ge(xt_mm, n + 1)
                once_above(act, h_mm, n - 1)
                act.copy(XT[:, i % 2].rearrange("p k s -> p (k s)"), PS[:, 0]).then_inc(xt_ev, 1)

            def silu(n, i):
                act.wait_ge(h_mm, n + 1)
                once_above(act, hid_done, n - 1)
                act.activation(sg[:, i % 2], PS[0:SLOTS, 2 + i % 2, 0:F], ACT.Silu).then_inc(silu_done, 1)

            def turned_extra(count):
                act.wait_ge(o_xt, count)
                act.copy(XTo[:, :, :].rearrange("p k s -> p (k s)"), PS[:, 1]).then_inc(o_xe, 1)

            def step(g):
                act.wait_ge(o_h, g + 1)
                act.activation(sgo[:, :], PS[0:SLOTS, 7, 0:F], ACT.Silu).then_inc(o_silu, 1)
                turned_extra(g + 2)

            def body(it, i, last):
                if not last or i + 1 < WB:
                    silu(at(it, i, 1), i + 1)
                if not last or i + 2 < WB:
                    evict(at(it, i, 2), i)
                extra(act, at(it, i), step)

            evict(0, 0)
            evict(1, 1)
            silu(0, 0)
            turned_extra(1)
            loops(act, body)

        @block.vector
        def _(dve):
            def hidden(n, i):
                dve.wait_ge(silu_done, n + 1)
                once_above(dve, ht_mm, n - 1)
                dve.tensor_tensor(hid[:, i % 2].rearrange("r (j p) -> r p j", j=2), sg[:, i % 2].rearrange("r (p j) -> r p j", j=2),
                                  PS[SLOTS:P, 2 + i % 2, 0:F].rearrange("r (p j) -> r p j", j=2), ALU.mult).then_inc(hid_done, 1)

            def step(g):
                dve.wait_ge(o_silu, g + 1)
                dve.tensor_tensor(hido[:, :].rearrange("r (j p) -> r p j", j=2), sgo[:, :].rearrange("r (p j) -> r p j", j=2),
                                  PS[SLOTS:P, 7, 0:F].rearrange("r (p j) -> r p j", j=2), ALU.mult).then_inc(o_hid, 1)
                dve.wait_ge(o_ht, g + 1)
                dve.tensor_copy(hidTo[:, :, :].rearrange("p j s -> p (j s)"), PS[:, 7, 0:P]).then_inc(o_he, 1)
                dve.wait_ge(o_out, g * 32 + 32)
                dve.wait_ge(o_y, g + 1)
                dve.tensor_copy(Yo[:, :], PS[:, 7]).then_inc(o_ye, 1)

            def body(it, i, last):
                n = at(it, i)
                dve.wait_ge(ht_mm, n + 1)
                once_above(dve, yy_mm, at(it, i, -1))
                dve.tensor_copy(hidT[:, i % 2].rearrange("p j s -> p (j s)"), PS[:, 4, 0:P]).then_inc(ht_ev, 1)
                if not last or i + 1 < WB:
                    hidden(at(it, i, 1), i + 1)
                dve.wait_ge(yy_mm, n + 1)
                once_above(dve, y_out[i % 2], (it * (WB // 2) + i // 2) * 32)
                dve.tensor_copy(Y[:, i % 2], PS[:, 5 + i % 2]).then_inc(yy_ev, 1)
                extra(dve, n, step)

            dve.sem_inc(o_ye, 1)
            hidden(0, 0)
            loops(dve, body)


def combine(nc, t):
    PS = t.PS
    OWN = 3
    REST = TOPK - OWN
    with ExitStack() as ctx:
        sb = lambda n, s, d=F32: ctx.enter_context(nc.sbuf_tensor(n, s, d))
        sem = t.phase_semaphore
        G = sb("G", [P, TOPK, D])
        diag = sb("diag", [P, NT, REST, P])
        vec, vec_in = t.vec, t.vec_in
        ln = layer_norm_state(t, sb, sem, "_7")
        row_in = [sem(f"row_in{k}") for k in range(TOPK)]
        row_dve, row_pe, sum_ev = sem("row_dve"), sem("row_pe"), sem("sum_ev")
        diag_done, normed, scaled, y_done, fin_out = sem("diag_done"), sem("normed"), sem("scaled"), sem("y_done"), sem("fin_out")
        dve_step = sem("comb_dve")
        block = ctx.enter_context(nc.Block())

        @block.gpsimd
        def _(pool):
            def scale(n):
                a = t.acc[:, n]
                pool.wait_ge(normed, n + 1)
                pool.tensor_tensor(a, a, vec[:, 2], ALU.mult).then_inc(scaled, 1)
                pool.wait_ge(scaled, n + 1)
                pool.tensor_tensor(a, a, vec[:, 3], ALU.add).then_inc(y_done, 1)

            def gather(n):
                for k in (3, 0, 4, 1, 5, 2, 6, 7):
                    if n and k < OWN:
                        pool.wait_ge(row_dve, OWN * (n - 1) + k + 1)
                    elif n:
                        pool.wait_ge(row_pe, REST * (n - 1) + k - OWN + 1)
                    pool.indirect_dma_start(G[:, k], None, t.y_dram, bass.IndirectOffsetOnAxis(ap=t.rows[:, n, k:k + 1], axis=0)).then_inc(row_in[k], 16)

            gather(0)
            gather(1)
            for n in range(NT):
                rsqrts(pool, ln, n)
                if n + 2 < NT:
                    gather(n + 2)
                if n < NT - 1:
                    scale(n)

        @block.sync
        def _(sp):
            for n in range(NT):
                sp.wait_ge(y_done, n + 1)
                dst = t.yp[P * n:P * n + P] if n < 2 else t.ys
                sp.dma_start(dst, t.acc[:, n]).then_inc(fin_out, 16)
            sp.wait_ge(fin_out, 16 * NT)

        @block.tensor
        def _(pe):
            pe.wait_ge(diag_done, 1)
            for n in range(NT):
                if n >= 2:
                    pe.wait_ge(sum_ev, n - 1)
                for i in range(REST):
                    pe.wait_ge(row_in[OWN + i], 16 * (n + 1))
                    for c in range(2):
                        mm = pe.matmul(PS[:, 2 * (n % 2) + c], diag[:, n, i], G[:, OWN + i, CW * c:CW * c + CW],
                                       start=i == 0, stop=i == REST - 1)
                    mm.then_inc(row_pe, 1)

        @block.vector
        def _(dve):
            link = make_link(dve, dve_step)
            for n in range(NT):
                for i in range(REST):
                    ins = dve.tensor_scalar(diag[:, n, i], t.ident[:, :], t.wts[:, n, OWN + i:OWN + i + 1], None, ALU.mult)
            ins.then_inc(diag_done, 1)
            for n in range(NT):
                a = t.acc[:, n]
                for k in range(OWN):
                    dve.wait_ge(row_in[k], 16 * (n + 1))
                    link(dve.scalar_tensor_tensor(a, G[:, k], t.wts[:, n, k:k + 1], a, ALU.mult, ALU.add))
                    dve.sem_inc(row_dve, 1)
                dve.wait_ge(row_pe, REST * (n + 1))
                link(dve.tensor_tensor(a, a, PS[:, 2 * (n % 2):2 * (n % 2) + 2].rearrange("p b x -> p (b x)"), ALU.add))
                dve.sem_inc(sum_ev, 1)
                if n == 0:
                    dve.wait_ge(vec_in, 64)
                link(dve.tensor_tensor(a, a, vec[:, n // 2], ALU.mult))
                link(dve.scalar_tensor_tensor(a, t.X[:, n], ALPHA, a, ALU.mult, ALU.add))
                layer_norm(dve, link, ln, a, a)
                if n < NT - 1:
                    dve.sem_inc(normed, 1)
                else:
                    dve.wait_ge(y_done, NT - 1)
                    link(dve.tensor_tensor(a, a, vec[:, 2], ALU.mult))
                    dve.tensor_tensor(a, a, vec[:, 3], ALU.add).then_inc(y_done, 1)


INS = ["x_prompt", "x_sample", "cache_k_diff", "cache_v_diff", "cache_k_band", "cache_v_band", "c_prompt",
       "c_sample", "w_ada", "b_ada", "w_in", "b_in", "lambda_q1", "lambda_k1", "lambda_q2", "lambda_k2",
       "subln_g", "rel_bias", "p_a", "p_b", "w_out", "ln1_g", "ln1_b", "w_router", "e_bias", "w1", "w3", "w2",
       "ws1", "ws3", "ws2", "ln2_g", "ln2_b"]
OUTS = [("y_prompt", (1, SEQ, D)), ("y_sample", (NSEQ, NF, D)),
        ("k_diff_prompt", (1, 1, SEQ, HA, 2, HD)), ("v_diff_prompt", (1, 1, SEQ, HA, 2 * HD)),
        ("k_band_prompt", (1, 1, SEQ, HB, HD)), ("v_band_prompt", (1, 1, SEQ, HB, HD)),
        ("k_diff_sample", (1, NSEQ, NF, HA, 2, HD)), ("v_diff_sample", (1, NSEQ, NF, HA, 2 * HD)),
        ("k_band_sample", (1, NSEQ, NF, HB, HD)), ("v_band_sample", (1, NSEQ, NF, HB, HD))]


class Shared:
    pass


def streaming_layer(nc, a, o):
    t = Shared()
    t.x_prompt, t.x_sample, t.c_prompt, t.c_sample = a["x_prompt"], a["x_sample"], a["c_prompt"], a["c_sample"]
    t.w_ada, t.b_ada, t.w_in, t.b_in = a["w_ada"], a["b_ada"], a["w_in"], a["b_in"]
    t.subln_g, t.rel_bias, t.p_a, t.p_b = a["subln_g"], a["rel_bias"], a["p_a"], a["p_b"]
    t.w_out, t.ln1_g, t.ln1_b, t.w_router = a["w_out"], a["ln1_g"], a["ln1_b"], a["w_router"]
    t.e_bias, t.ws1, t.ws3, t.ws2 = a["e_bias"], a["ws1"], a["ws3"], a["ws2"]
    t.ln2_g, t.ln2_b = a["ln2_g"], a["ln2_b"]
    t.lq1, t.lk1, t.lq2, t.lk2 = (a[n] for n in ("lambda_q1", "lambda_k1", "lambda_q2", "lambda_k2"))
    t.ckd = a["cache_k_diff"].rearrange("l b s h j d -> (l b) s h (j d)")
    t.cvd = a["cache_v_diff"].rearrange("l b s h d -> (l b) s h d")
    t.ckb = a["cache_k_band"].rearrange("l b s (u j) d -> (l b) s u (j d)", j=2)
    t.cvb = a["cache_v_band"].rearrange("l b s (u j) d -> (l b) s u (j d)", j=2)
    t.w1v = a["w1"].rearrange("l e (p k) n -> (l e) p k n", k=KD)
    t.w3v = a["w3"].rearrange("l e (p k) n -> (l e) p k n", k=KD)
    t.w2v = a["w2"].rearrange("l e (p k) n -> (l e) p k n", k=2)
    t.yp = o["y_prompt"].rearrange("b s d -> (b s) d")
    t.ys = o["y_sample"].rearrange("b s d -> (b s) d")
    t.kdp = o["k_diff_prompt"].rearrange("l b s h j d -> (l b s) (h j d)")
    t.kds = o["k_diff_sample"].rearrange("l b s h j d -> (l b s) (h j d)")
    t.vdp = o["v_diff_prompt"].rearrange("l b s h d -> (l b s) (h d)")
    t.vds = o["v_diff_sample"].rearrange("l b s h d -> (l b s) (h d)")
    t.kbp = o["k_band_prompt"].rearrange("l b s h d -> (l b s) (h d)")
    t.kbs = o["k_band_sample"].rearrange("l b s h d -> (l b s) (h d)")
    t.vbp = o["v_band_prompt"].rearrange("l b s h d -> (l b s) (h d)")
    t.vbs = o["v_band_sample"].rearrange("l b s h d -> (l b s) (h d)")
    t.mod = nc.dram_tensor("mod", (1 + NSEQ, 6 * D), F32, kind="Internal").ap()
    t.rev_dram = nc.dram_tensor("rev_table", (HB, 3 * CLIP), F32, kind="Internal").ap()
    t.gates = nc.dram_tensor("gates", (len(GC), TOK, CW), F32, kind="Internal").ap()
    t.h_dram = nc.dram_tensor("h_rows", (TOK, D), F32, kind="Internal").ap()
    t.y_dram = nc.dram_tensor("expert_rows", (NBLK * SLOTS, D), F32, kind="Internal").ap()

    with ExitStack() as ctx:
        t.PS = ctx.enter_context(nc.psum_tensor("PS", [P, 8, CW], F32))

        used = []

        def scoped(scope, name, shape, dtype=F32):
            used.append(name)
            return scope.enter_context(nc.sbuf_tensor(f"{name}_{len(used)}", shape, dtype))

        t.zeros = scoped(ctx, "zeros", [P, D // 4])
        t.power = scoped(ctx, "power", [P, 2 * NSEQ])
        t.ident = scoped(ctx, "ident", [P, P])
        t.X = scoped(ctx, "X", [P, NT, D])
        t.wr = scoped(ctx, "wr", [P, KD, E])
        t.hT = scoped(ctx, "hT", [P, KD, TOK])
        t.zeros_done = ctx.enter_context(nc.semaphore("zeros_done"))
        t.ident_done = ctx.enter_context(nc.semaphore("ident_done"))
        t.wexp_in = [ctx.enter_context(nc.semaphore(f"wexp_in{i}")) for i in range(WB)]

        t.phase_sems = []

        def phase_semaphore(name):
            t.phase_sems.append(nc.alloc_semaphore(name=name))
            return t.phase_sems[-1]

        def recycle():
            nc.clear_and_free_semaphores(t.phase_sems)
            nc.all_engine_barrier()
            t.phase_sems = []
        t.phase_semaphore = phase_semaphore

        def build_identity(pool):
            pool.memset(t.power[:, :], -0.5)
            pool.memset(t.zeros[:, :], 0.0).then_inc(t.zeros_done, 1)
            pool.memset(t.ident[:, :], 0.0).then_inc(t.ident_done, 1)
            pool.wait_ge(t.ident_done, 1)
            pool.affine_select(out=t.ident[:, :], in_=t.ident[:, :], compare_op=ALU.not_equal, fill=1.0, base=0,
                               pattern=[[-1, P]], channel_multiplier=1).then_inc(t.ident_done, 1)
        t.build_identity = build_identity

        def load_mod_of(sp, dst, g, part, s):
            if g == 0:
                src = t.mod[0:1, D * part:D * part + D].to_broadcast([P, D])
            else:
                src = bass.AP(t.mod.tensor, 6 * D + D * part, [[6 * D, NSEQ], [0, NF], [1, D]])
            sp.dma_start(dst[:, g], src).then_inc(s, 16)

        def load_mod(sp, dst, part, s):
            for g in range(2):
                load_mod_of(sp, dst, g, part, s)
        t.load_mod_of = load_mod_of
        t.load_mod = load_mod

        with ExitStack() as mixer:
            t.oaT = scoped(mixer, "oaT", [P, HA, TOK])
            t.obT = scoped(mixer, "obT", [P, 4, TOK])
            with ExitStack() as attention:
                t.qT = scoped(attention, "qT", [P, NU, TOK])
                t.kT = scoped(attention, "kT", [P, NU, TOK])
                t.V = scoped(attention, "V", [P, NT, DA + DB])
                t.alibi_p = scoped(attention, "alibi_p", [P, HA, 256])
                t.band_p = scoped(attention, "band_p", [P, HB, 256])
                t.sbias = scoped(attention, "sbias", [P, 3, PAST + NF])
                t.sub_g = scoped(attention, "sub_g", [P, 2 * HD])
                t.neg_lam = scoped(attention, "neg_lam", [P, 1])
                t.join = scoped(attention, "join", [P, 64])
                with ExitStack() as scope:
                    t.raw = scoped(scope, "raw", [P, 2, 4, CW])
                    t.u_hi = scoped(scope, "u_hi", [P, KD, TOK], F32R)
                    t.u_lo = scoped(scope, "u_lo", [P, NT, KD, P], F32R)
                    t.cT = scoped(scope, "cT", [P, KD, 32])
                    t.win_in = [phase_semaphore(f"win_in{i}") for i in range(2)]
                    with ExitStack() as early:
                        constants = attention_constants(t, lambda name, shape, dtype=F32: scoped(scope, name, shape, dtype),
                                                        lambda name, shape, dtype=F32: scoped(early, name, shape, dtype))
                        conditioning(nc, t, constants)
                    projection_in(nc, t, constants)
                t.kc = scoped(attention, "kc", [P, 2, NU, P])
                t.kcache_in = [phase_semaphore(f"kcache_in{i}") for i in range(2)]
                attention_prompt(nc, t)
                attention_sample(nc, t)
            recycle()
            t.wr_in = phase_semaphore("wr_in")
            projection_out(nc, t)
        t.acc = scoped(ctx, "acc", [P, NT, D])
        t.wts = scoped(ctx, "wts", [P, NT, TOPK])
        t.rows = scoped(ctx, "rows", [P, NT, TOPK], I32)
        t.tokens = scoped(ctx, "tokens", [SLOTS, NBLK + 1], I32)
        t.ov = scoped(ctx, "ov", [1, E + 1], I32)
        t.vec = scoped(ctx, "vec", [P, 4, D])
        t.vec_in = phase_semaphore("vec7_in")
        with ExitStack() as scope:
            t.W13 = scoped(scope, "W13", [P, WB, 2, KD, F])
            t.W2 = scoped(scope, "W2", [P, WB, 2, D])
            routing(nc, t)
            experts(nc, t)
        combine(nc, t)


def kernel(**inputs):
    import concourse.bacc as bacc
    from concourse.bass_utils import run_bass_kernel_spmd

    nc = bacc.Bacc("TRN2", target_bir_lowering=False, num_devices=1)
    arrays, a, o = {}, {}, {}
    for name in INS:
        x = np.ascontiguousarray(inputs[name])
        arrays[name] = x
        a[name] = nc.dram_tensor(name, x.shape, mybir.dt.from_np(x.dtype), kind="ExternalInput").ap()
    for name, shape in OUTS:
        o[name] = nc.dram_tensor(name, shape, F32, kind="ExternalOutput").ap()
    streaming_layer(nc, a, o)
    r = run_bass_kernel_spmd(nc, [arrays], core_ids=[0])
    return tuple(r.results[0][name] for name, _ in OUTS)
```
